# Optimizing a Trainium2 kernel written in Bass

```python
import jax, jax.numpy as jnp
from jax import lax
import numpy as np

D_MODEL = 1024
BATCH = 1
SEQ = 128
DEPTH = 1
DEC_BATCH = 1
DEC_SEQ = 1024
PAST_LEN = 128

GRID_W = 64
MLA_HEADS = 4
MLA_NOPE = 128
MLA_ROPE = 64
MLA_QK = MLA_NOPE + MLA_ROPE
MLA_V = 128
Q_RANK = 512
KV_RANK = 256
ROPE_AXIS = MLA_ROPE // 2
ROPE_BASE = 10000.0
Q_BLOCK = 128
RET_HEADS = 4
RET_DK = 128
RET_DV = 128
RET_CHUNK = 128
IN_SIZES = (Q_RANK, KV_RANK, MLA_ROPE, RET_HEADS * RET_DK, RET_HEADS * RET_DK, RET_HEADS * RET_DV, RET_HEADS * RET_DV)
IN_DIM = Q_RANK + KV_RANK + MLA_ROPE + 2 * RET_HEADS * RET_DK + 2 * RET_HEADS * RET_DV
MIX_DIM = MLA_HEADS * MLA_V + RET_HEADS * RET_DV
PEER_HEADS = 8
PEER_QDIM = 256
PEER_HALF = PEER_QDIM // 2
N_KEYS = 128
N_EXPERTS = N_KEYS * N_KEYS
PEER_TOPK = 16
PEER_BLOCK = 128
EPS = 1e-6

kernel_name = "hybrid_mla_retention_peer_diffusion_step"

def rms_norm(x, w):
    xf = x.astype(jnp.float32)
    y = xf * lax.rsqrt(jnp.mean(xf * xf, axis=-1, keepdims=True) + EPS)
    return (y * w.astype(jnp.float32)).astype(x.dtype)

def ada_split(cond, w_ada, b_ada):
    m = (jax.nn.silu(cond) @ w_ada + b_ada)[:, None, :]
    return jnp.split(m, 6, axis=-1)

def modulate(x, norm_w, shift, scale):
    return rms_norm(x, norm_w) * (1.0 + scale) + shift

def axial_angles(S):
    rows = S // GRID_W
    r = jnp.repeat(jnp.arange(rows, dtype=jnp.float32), GRID_W)
    col = jnp.tile(jnp.arange(GRID_W, dtype=jnp.float32), rows)
    nf = ROPE_AXIS // 2
    freqs = jnp.power(ROPE_BASE, -jnp.arange(nf, dtype=jnp.float32) / nf)
    return r[:, None] * freqs, col[:, None] * freqs

def rope_1d(x, ang):
    x1, x2 = jnp.split(x, 2, axis=-1)
    cos = jnp.cos(ang)[None, :, None, :].astype(x.dtype)
    sin = jnp.sin(ang)[None, :, None, :].astype(x.dtype)
    return jnp.concatenate([x1 * cos - x2 * sin, x2 * cos + x1 * sin], axis=-1)

def rope_2d(x, ang_r, ang_c):
    xn = x[..., :MLA_NOPE]
    xr = x[..., MLA_NOPE:MLA_NOPE + ROPE_AXIS]
    xc = x[..., MLA_NOPE + ROPE_AXIS:]
    return jnp.concatenate([xn, rope_1d(xr, ang_r), rope_1d(xc, ang_c)], axis=-1)

def mla_kv(ckv, krope, w_ukv, k_head_norm_w):
    B, S, _ = ckv.shape
    kv = (ckv @ w_ukv).reshape(B, S, MLA_HEADS, MLA_NOPE + MLA_V)
    k_nope, v = kv[..., :MLA_NOPE], kv[..., MLA_NOPE:]
    k_r = jnp.broadcast_to(krope[:, :, None, :], (B, S, MLA_HEADS, MLA_ROPE))
    k = rms_norm(jnp.concatenate([k_nope, k_r], axis=-1), k_head_norm_w)
    return k, v

def block_attention(q, k, v):
    B, S, H, Dq = q.shape
    nb = S // Q_BLOCK
    qb = q.reshape(B, nb, Q_BLOCK, H, Dq).transpose(1, 0, 2, 3, 4)
    scale = Dq ** -0.5

    def attend(qblk):
        s = jnp.einsum('bqhd,bkhd->bhqk', qblk, k).astype(jnp.float32) * scale
        p = jax.nn.softmax(s, axis=-1).astype(v.dtype)
        return jnp.einsum('bhqk,bkhv->bqhv', p, v)

    o = lax.map(attend, qb)
    return o.transpose(1, 0, 2, 3, 4).reshape(B, S, H * v.shape[-1])

def retention_chunkwise(q, k, v, log_gamma, s0):
    B, S, H, DK = q.shape
    DV = v.shape[-1]
    n = S // RET_CHUNK

    def chunks(a):
        return a.reshape(B, n, RET_CHUNK, H, a.shape[-1]).transpose(1, 0, 2, 3, 4)

    pos = jnp.arange(RET_CHUNK, dtype=jnp.float32)
    rel = pos[:, None] - pos[None, :]
    intra = jnp.where(rel[None] >= 0, jnp.exp(jnp.maximum(rel, 0.0)[None] * log_gamma[:, None, None]), 0.0)
    q_dec = jnp.exp((pos[:, None] + 1.0) * log_gamma[None, :])[None, :, :, None]
    k_dec = jnp.exp((RET_CHUNK - 1.0 - pos)[:, None] * log_gamma[None, :])[None, :, :, None]
    c_dec = jnp.exp(RET_CHUNK * log_gamma)[None, :, None, None]

    def step(s, blk):
        qc, kc, vc = blk
        qf, kf, vf = qc.astype(jnp.float32), kc.astype(jnp.float32), vc.astype(jnp.float32)
        a = jnp.einsum('bihd,bjhd->bhij', qf, kf) * intra
        o = jnp.einsum('bhij,bjhv->bihv', a, vf) + jnp.einsum('bihd,bhdv->bihv', qf, s) * q_dec
        s_new = s * c_dec + jnp.einsum('bjhd,bjhv->bhdv', kf * k_dec, vf)
        return s_new, o

    s_fin, o = lax.scan(step, s0.astype(jnp.float32), (chunks(q), chunks(k), chunks(v)))
    return o.transpose(1, 0, 2, 3, 4).reshape(B, S, H, DV), s_fin

def retention_out(o, g, gn_w):
    B, S, H, DV = o.shape
    mu = jnp.mean(o, axis=-1, keepdims=True)
    var = jnp.mean(jnp.square(o - mu), axis=-1, keepdims=True)
    o = ((o - mu) * lax.rsqrt(var + EPS)).reshape(B, S, H * DV) * gn_w.astype(jnp.float32)
    return jax.nn.silu(g) * o.astype(g.dtype)

def peer(h, w_pq, sub_keys1, sub_keys2, u_table, v_table):
    B, S, D = h.shape
    hb = h.reshape((B * S) // PEER_BLOCK, PEER_BLOCK, D)

    def block(xb):
        q = (xb @ w_pq).reshape(PEER_BLOCK, PEER_HEADS, PEER_QDIM)
        s1 = jnp.einsum('thd,kd->thk', q[..., :PEER_HALF], sub_keys1).astype(jnp.float32)
        s2 = jnp.einsum('thd,kd->thk', q[..., PEER_HALF:], sub_keys2).astype(jnp.float32)
        v1, i1 = lax.top_k(s1, PEER_TOPK)
        v2, i2 = lax.top_k(s2, PEER_TOPK)
        cand = (v1[..., :, None] + v2[..., None, :]).reshape(PEER_BLOCK, PEER_HEADS, PEER_TOPK * PEER_TOPK)
        cidx = (i1[..., :, None] * N_KEYS + i2[..., None, :]).reshape(PEER_BLOCK, PEER_HEADS, PEER_TOPK * PEER_TOPK)
        top_s, sel = lax.top_k(cand, PEER_TOPK)
        eidx = jnp.take_along_axis(cidx, sel, axis=-1)
        g = jax.nn.softmax(top_s, axis=-1).astype(xb.dtype)
        act = jax.nn.gelu(jnp.einsum('thkd,td->thk', u_table[eidx], xb), approximate=False)
        return jnp.einsum('thk,thkd->td', g * act, v_table[eidx])

    return lax.map(block, hb).reshape(B, S, D)

def trunk_layer(x, cond, p, ctx):
    B, S, _ = x.shape
    sh1, sc1, g1, sh2, sc2, g2 = ada_split(cond, p['w_ada'], p['b_ada'])
    h = modulate(x, p['norm1_w'], sh1, sc1)
    z = h @ p['w_in']
    split_at = [int(i) for i in np.cumsum(IN_SIZES)[:-1]]
    cq, ckv, krope, qr, kr, vr, gr = jnp.split(z, split_at, axis=-1)
    ckv = rms_norm(ckv, p['kv_norm_w'])
    q = (rms_norm(cq, p['q_norm_w']) @ p['w_uq']).reshape(B, S, MLA_HEADS, MLA_QK)
    q = rms_norm(q, p['q_head_norm_w'])
    k, v = mla_kv(ckv, krope, p['w_ukv'], p['k_head_norm_w'])
    qr = qr.reshape(B, S, RET_HEADS, RET_DK)
    kr = kr.reshape(B, S, RET_HEADS, RET_DK) * (RET_DK ** -0.5)
    vr = vr.reshape(B, S, RET_HEADS, RET_DV)
    log_gamma = jax.nn.log_sigmoid(p['ret_decay_logit'].astype(jnp.float32))
    if ctx is None:
        s0_f = jnp.zeros((B, RET_HEADS, RET_DK, RET_DV), jnp.float32)
        s0_b = s0_f
    else:
        ckv_c, krope_c, state_c = ctx
        ang_r, ang_c = axial_angles(S)
        q = rope_2d(q, ang_r, ang_c)
        k = rope_2d(k, ang_r, ang_c)
        k_c, v_c = mla_kv(ckv_c, krope_c, p['w_ukv'], p['k_head_norm_w'])
        k = jnp.concatenate([k_c, k], axis=1)
        v = jnp.concatenate([v_c, v], axis=1)
        s0_f, s0_b = state_c[:, 0], state_c[:, 1]
    att = block_attention(q, k, v)
    o_f, s_f = retention_chunkwise(qr, kr, vr, log_gamma[0], s0_f)
    o_b, s_b = retention_chunkwise(qr[:, ::-1], kr[:, ::-1], vr[:, ::-1], log_gamma[1], s0_b)
    ret = retention_out(o_f + o_b[:, ::-1], gr, p['ret_gn_w'])
    x = x + g1 * (jnp.concatenate([att, ret], axis=-1) @ p['w_out'])
    h2 = modulate(x, p['norm2_w'], sh2, sc2)
    x = x + g2 * peer(h2, p['w_pq'], p['sub_keys1'], p['sub_keys2'], p['u_table'], p['v_table'])
    return x, ckv, krope, jnp.stack([s_f, s_b], axis=1).astype(x.dtype)

def setup_inputs(seed: int = 0) -> dict:
    key = jax.random.key(seed)
    ks = jax.random.split(key, 32)
    D = D_MODEL

    def nrm(k, shape, scale):
        return jax.random.normal(k, shape, jnp.float32) * scale

    def gain(k, shape):
        return 1.0 + 0.02 * jax.random.normal(k, shape, jnp.float32)

    base_logit = jnp.log(jnp.power(2.0, 5.0 + jnp.arange(RET_HEADS, dtype=jnp.float32)) - 1.0)
    return {
        "x_prompt": nrm(ks[0], (BATCH, SEQ, D), 1.0),
        "x_sample": nrm(ks[1], (DEC_BATCH, DEC_SEQ, D), 1.0),
        "c": nrm(ks[2], (DEC_BATCH, D), 1.0),
        "cache_ckv": nrm(ks[3], (DEC_BATCH, DEPTH, PAST_LEN, KV_RANK), 1.0),
        "cache_krope": nrm(ks[4], (DEC_BATCH, DEPTH, PAST_LEN, MLA_ROPE), 1.0),
        "state_ret": nrm(ks[5], (DEC_BATCH, DEPTH, 2, RET_HEADS, RET_DK, RET_DV), 0.5),
        "c_ctx": nrm(ks[6], (D,), 1.0),
        "w_ada": nrm(ks[7], (DEPTH, D, 6 * D), 0.5 * D ** -0.5),
        "b_ada": nrm(ks[8], (DEPTH, 6 * D), 0.02),
        "norm1_w": gain(ks[9], (DEPTH, D)),
        "w_in": nrm(ks[10], (DEPTH, D, IN_DIM), D ** -0.5),
        "q_norm_w": gain(ks[11], (DEPTH, Q_RANK)),
        "w_uq": nrm(ks[12], (DEPTH, Q_RANK, MLA_HEADS * MLA_QK), Q_RANK ** -0.5),
        "kv_norm_w": gain(ks[13], (DEPTH, KV_RANK)),
        "w_ukv": nrm(ks[14], (DEPTH, KV_RANK, MLA_HEADS * (MLA_NOPE + MLA_V)), KV_RANK ** -0.5),
        "q_head_norm_w": gain(ks[15], (DEPTH, MLA_QK)),
        "k_head_norm_w": gain(ks[16], (DEPTH, MLA_QK)),
        "ret_decay_logit": base_logit[None, None, :] + 0.1 * jax.random.normal(ks[17], (DEPTH, 2, RET_HEADS), jnp.float32),
        "ret_gn_w": gain(ks[18], (DEPTH, RET_HEADS * RET_DV)),
        "w_out": nrm(ks[19], (DEPTH, MIX_DIM, D), MIX_DIM ** -0.5),
        "norm2_w": gain(ks[20], (DEPTH, D)),
        "w_pq": nrm(ks[21], (DEPTH, D, PEER_HEADS * PEER_QDIM), D ** -0.5),
        "sub_keys1": nrm(ks[22], (DEPTH, N_KEYS, PEER_HALF), PEER_HALF ** -0.5),
        "sub_keys2": nrm(ks[23], (DEPTH, N_KEYS, PEER_HALF), PEER_HALF ** -0.5),
        "u_table": nrm(ks[24], (DEPTH, N_EXPERTS, D), D ** -0.5),
        "v_table": nrm(ks[25], (DEPTH, N_EXPERTS, D), 0.5),
    }

def reference(x_prompt, x_sample, c, cache_ckv, cache_krope, state_ret, c_ctx, w_ada, b_ada, norm1_w, w_in,
              q_norm_w, w_uq, kv_norm_w, w_ukv, q_head_norm_w, k_head_norm_w, ret_decay_logit, ret_gn_w,
              w_out, norm2_w, w_pq, sub_keys1, sub_keys2, u_table, v_table):
    y_prompt, y_sample = x_prompt, x_sample
    ckv_list, krope_list, ret_list = [], [], []
    for l in range(DEPTH):
        p = {
            'w_ada': w_ada[l], 'b_ada': b_ada[l], 'norm1_w': norm1_w[l], 'w_in': w_in[l],
            'q_norm_w': q_norm_w[l], 'w_uq': w_uq[l], 'kv_norm_w': kv_norm_w[l], 'w_ukv': w_ukv[l],
            'q_head_norm_w': q_head_norm_w[l], 'k_head_norm_w': k_head_norm_w[l],
            'ret_decay_logit': ret_decay_logit[l], 'ret_gn_w': ret_gn_w[l], 'w_out': w_out[l],
            'norm2_w': norm2_w[l], 'w_pq': w_pq[l], 'sub_keys1': sub_keys1[l], 'sub_keys2': sub_keys2[l],
            'u_table': u_table[l], 'v_table': v_table[l],
        }
        y_prompt, ckv_l, krope_l, ret_l = trunk_layer(y_prompt, c_ctx[None, :], p, None)
        ckv_list.append(ckv_l)
        krope_list.append(krope_l)
        ret_list.append(ret_l)
        y_sample, _, _, _ = trunk_layer(y_sample, c, p, (cache_ckv[:, l], cache_krope[:, l], state_ret[:, l]))
    new_cache_ckv = jnp.stack(ckv_list, axis=1)
    new_cache_krope = jnp.stack(krope_list, axis=1)
    new_state_ret = jnp.stack(ret_list, axis=1)
    return (y_prompt, y_sample, new_cache_ckv, new_cache_krope, new_state_ret)


_drawn_inputs = setup_inputs


def setup_inputs(seed=0):
    import zlib

    import numpy as np

    out = dict(_drawn_inputs(seed))
    spreads = {}
    factors = {'cache_ckv': 8.0,
     'cache_krope': 8.0,
     'state_ret': 2.822,
     'q_norm_w': 8.0,
     'q_head_norm_w': 8.0,
     'k_head_norm_w': 8.0,
     'ret_gn_w': 8.0,
     'norm2_w': 4.566}
    for name, (base, spread) in spreads.items():
        noise = np.random.default_rng([zlib.crc32(name.encode()), seed]).standard_normal(out[name].shape)
        drawn = base * np.exp(spread * noise) if base else spread * noise
        out[name] = __import__('jax').numpy.asarray(drawn.astype(out[name].dtype))
    for name, factor in factors.items():
        out[name] = (out[name] * factor).astype(out[name].dtype)
    return out
```

```python
import numpy as np
import concourse.bass as bass
from concourse import mybir
from contextlib import ExitStack

F32 = mybir.dt.float32
F32R = mybir.dt.float32r
U16 = mybir.dt.uint16
U32 = mybir.dt.uint32
BF16 = mybir.dt.bfloat16
ALU = mybir.AluOpType
ACT = mybir.ActivationFunctionType
AX = mybir.AxisListType

P = 128
D = 1024
KD = D // P
TILES = 9
CTX = TILES
T = TILES * P
HEADS = 4
NOPE, ROPE, QK = 128, 64, 192
Q_RANK, KV_RANK = 512, 256
Z_ATT = Q_RANK + KV_RANK + ROPE
Z_RET = 4 * HEADS * P
IN_DIM = Z_ATT + Z_RET
Z_CUTS = [(0, 512), (512, 832)] + [(832 + 512 * c, 832 + 512 * (c + 1)) for c in range(4)]
GRID_W = 64
EPS = 1e-6
PEER_HEADS = 8
TOPK = 16
PAIRS = PEER_HEADS * TOPK
N_KEYS = 128
GROUP = 3
NEG = -3.0e38

C_IDENT, C_IOTA = range(2)
C_RELF, C_RELB, C_MASKF, C_MASKB = range(4)


def grid_constants():
    j, i = np.meshgrid(np.arange(P), np.arange(P), indexing="ij")
    k_scale = np.float32(P ** -0.5)
    grid = np.zeros((P, 2, P), np.float32)
    grid[:, C_IDENT] = np.eye(P)
    grid[:, C_IOTA] = i
    out = np.zeros((P, 4, P), np.float32)
    out[:, C_RELF] = np.maximum(i - j, 0)
    out[:, C_RELB] = np.maximum(j - i, 0)
    out[:, C_MASKF] = (i >= j) * k_scale
    out[:, C_MASKB] = (j >= i) * k_scale
    return grid, out


def column_constants():
    p = np.arange(P, dtype=np.float32)
    return np.stack([p + 1, P - p, P - 1 - p, p, np.full(P, EPS, np.float32), np.full(P, P, np.float32)], 1).astype(np.float32)


def rope_constants():
    nf = ROPE // 4
    freqs = np.power(np.float32(10000.0), -np.arange(nf, dtype=np.float32) / np.float32(nf)).astype(np.float32)
    t = np.arange(8 * P)
    out = np.zeros((TILES + 1, P, 2, ROPE), np.float32)
    out[:, :, 0] = 1.0
    for axis, pos in enumerate((t // GRID_W, t % GRID_W)):
        ang = pos.astype(np.float32)[:, None] * freqs
        cos, sin = np.cos(ang).astype(np.float32), np.sin(ang).astype(np.float32)
        at = axis * 2 * nf
        out[1:TILES, :, 0, at:at + 2 * nf] = np.concatenate([cos, cos], 1).reshape(8, P, 2 * nf)
        out[1:TILES, :, 1, at:at + 2 * nf] = np.concatenate([-sin, sin], 1).reshape(8, P, 2 * nf)
    return np.ascontiguousarray(out.transpose(1, 0, 2, 3))


class Links:

    def __init__(self, eng, sem):
        self.eng, self.sem, self.base, self.n = eng, sem, 0, 0

    def at(self, base):
        self.base, self.n = base, 0

    def __call__(self, ins):
        self.n += 1
        ins.then_inc(self.sem, 1)
        self.eng.wait_ge(self.sem, self.base + self.n)


def tiles_in_two_stages(eng, pre, post):
    pre(0, 0)
    pre(1, 1)
    post(0, 0)
    with eng.Fori(0, 3) as k:
        pre(k * 2 + 2, 0)
        post(k * 2 + 1, 1)
        pre(k * 2 + 3, 1)
        post(k * 2 + 2, 0)
    pre(8, 0)
    post(7, 1)
    post(8, 0)


def use_of(t, slot):
    if isinstance(t, int):
        return t // 2
    return (t - slot) // 2


class Mem:

    def __init__(self, nc, stack):
        self.nc, self.stack = nc, stack

    def sb(self, name, shape, dt=F32):
        return self.stack.enter_context(self.nc.sbuf_tensor(name, shape, dt))

    def ps(self, name, shape, dt=F32):
        return self.stack.enter_context(self.nc.psum_tensor(name, shape, dt))


def stage_modulation(nc, sem, m, keep, a):
    cT = m.sb("cT", [P, KD, 2])
    sig = m.sb("sig", [P, KD, 2])
    scT = m.sb("scT", [P, KD, 2])
    wada = [m.sb(f"wada{i}", [P, KD, 512]) for i in range(2)]
    brow = [m.sb(f"brow{i}", [2, 512]) for i in range(2)]
    mrow = keep.z1[0:2].rearrange("p t c -> p (t c)")[:, 0:6 * D]
    nw = m.sb("nw", [P, 2, KD])
    sel = m.sb("sel", [2, 2, P])
    logit = m.sb("logit", [P, 8])
    dk = m.sb("dk", [P, 5, 8])
    prow = m.ps("prow", [P, 2, 512])
    pcol = m.ps("pcol", [P, 64])
    pgate = m.ps("pgate", [P, 4, 512])

    const_in, ada_in = sem("const_in"), [sem("ada_in0"), sem("ada_in1")]
    bias_in = [sem("bias_in0"), sem("bias_in1")]
    small_in = sem("small_in")
    sig_done, cond_ready, row_full, row_free, rows_done = (
        sem(x) for x in ("sig_done", "cond_ready", "row_full", "row_free", "rows_done"))
    cols_full, gate_full, gate_free = sem("cols_full"), sem("gate_full"), sem("gate_free")
    dve_a, act_a, lg_ready, ln_in, ln_out, rel_done, cols_d = (
        sem(x) for x in ("dve_a", "act_a", "lg_ready", "ln_in", "ln_out", "rel_done", "cols_d"))
    CHUNKS = 12
    wv = a["w_ada"].rearrange("(k p) n -> p k n", p=P)
    w_in_v = a["w_in"].rearrange("(k p) n -> p k n", p=P)

    with nc.Block() as block:

        @block.sync
        def _(sp):
            sp.dma_start(cT[:], a["cT"]).then_inc(small_in, 16)
            sp.dma_start(sel[:], a["sel"]).then_inc(small_in, 16)
            sp.dma_start(nw[:], a["norm_cols"]).then_inc(small_in, 16)
            sp.dma_start(logit[:], a["decay_logit"].partition_broadcast(P)).then_inc(small_in, 16)
            sp.dma_start(keep.grid[:], a["grid"]).then_inc(const_in, 16)
            sp.dma_start(keep.cols[:], a["cols"]).then_inc(const_in, 16)
            with sp.Fori(0, CHUNKS // 2) as k:
                for s in range(2):
                    sp.wait_ge(row_full, k * 2 + s + 1)
                    sp.dma_start(wada[s][:], wv[:, :, bass.ds(k * 1024 + s * 512, 512)]).then_inc(ada_in[s], 16)
                    sp.wait_ge(row_free, k * 2 + s + 1)
                    sp.dma_start(brow[s][:], a["b_ada"][bass.ds(k * 1024 + s * 512, 512)].partition_broadcast(2)).then_inc(bias_in[s], 16)
            for c, (lo, hi) in enumerate(Z_CUTS):
                sp.dma_start(keep.w_in[:, :, lo:hi], w_in_v[:, :, lo:hi]).then_inc(keep.w_in_in[c], 16)

        @block.tensor
        def _(pe):
            pe.sem_inc(row_full, 2)
            pe.wait_ge(cond_ready, 1)
            with pe.Fori(0, CHUNKS // 2) as k:
                for s in range(2):
                    pe.wait_ge(ada_in[s], (k + 1) * 16)
                    pe.wait_ge(row_free, k * 2 + s + 1)
                    for c in range(KD):
                        last = nc.tensor.matmul(prow[0:2, s, :], scT[:, c, :], wada[s][:, c, :], start=c == 0, stop=c == KD - 1)
                    last.then_inc(row_full, 1)
            pe.wait_ge(rows_done, CHUNKS)
            pe.wait_ge(const_in, 32)
            pe.wait_ge(small_in, 64)
            for n, part in enumerate((1, 0, 4, 3)):
                for c in range(KD):
                    at = part * D + c * P
                    last = nc.tensor.matmul(pcol[:, (n * KD + c) * 2:(n * KD + c) * 2 + 2], mrow[:, at:at + P],
                                            keep.grid[0:2, C_IDENT, 0:2], start=True, stop=True)
            last.then_inc(cols_full, 1)
            n = 0
            for g, part in enumerate((2, 5)):
                for cond in range(2):
                    for half in range(2):
                        if n >= 4:
                            pe.wait_ge(gate_free, n - 3)
                        at = part * D + half * 512
                        nc.tensor.matmul(pgate[:, n % 4, :], sel[:, cond, :], mrow[:, at:at + 512],
                                         start=True, stop=True).then_inc(gate_full, 1)
                        n += 1

        @block.vector
        def _(dve):
            link = Links(dve, dve_a)
            dve.sem_inc(row_free, 2)
            dve.wait_ge(sig_done, 1)
            nc.vector.tensor_mul(scT[:], cT[:], sig[:]).then_inc(cond_ready, 1)
            dve.wait_ge(ln_in, 1)
            e, u, d, mask, lp = (dk[:, n, :] for n in range(5))
            lg = keep.log_decay[:]
            link(nc.vector.tensor_scalar(u, e, 1.0, None, ALU.add))
            link(nc.vector.tensor_scalar(d, u, -1.0, None, ALU.add))
            link(nc.vector.tensor_scalar(mask, u, 1.0, None, ALU.is_equal))
            nc.vector.tensor_add(d, d, mask).then_inc(ln_out, 1)
            dve.wait_ge(act_a, 2)
            dve.wait_ge(ln_out, 1)
            link(nc.vector.tensor_add(lp, lp, mask))
            link(nc.vector.reciprocal(d, d))
            link(nc.vector.tensor_mul(lp, lp, d))
            link(nc.vector.tensor_mul(lp, lp, e))
            nc.vector.scalar_tensor_tensor(out=lg, in0=logit[:], scalar=0.0, in1=lp, op0=ALU.min, op1=ALU.subtract).then_inc(lg_ready, 1)
            dve.wait_ge(rel_done, 1)
            link(nc.vector.tensor_scalar(keep.dec[:, 2:4, :], keep.dec[:, 2:4, :], float(P ** -0.5), None, ALU.mult))
            with dve.Fori(0, CHUNKS // 2) as k:
                for s in range(2):
                    dve.wait_ge(row_full, k * 2 + s + 3)
                    dve.wait_ge(bias_in[s], (k + 1) * 16)
                    at = bass.ds(k * 1024 + s * 512, 512)
                    nc.vector.tensor_add(mrow[:, at], prow[0:2, s, :], brow[s][:]).then_inc(rows_done, 1)
                    dve.wait_ge(rows_done, k * 2 + s + 1)
                    dve.sem_inc(row_free, 1)
            dve.wait_ge(cols_full, 1)
            pc = pcol[:].rearrange("p (n k c) -> p n k c", n=4, k=KD)
            for i in range(2):
                for cond in range(2):
                    nc.vector.scalar_tensor_tensor(out=keep.mod[:, 2 * i, cond, :], in0=pc[:, 2 * i, :, cond], scalar=1.0,
                                                   in1=nw[:, i, :], op0=ALU.add, op1=ALU.mult)
                    nc.vector.tensor_copy(keep.mod[:, 2 * i + 1, cond, :], pc[:, 2 * i + 1, :, cond])
            for n in range(8):
                dve.wait_ge(gate_full, n + 1)
                g, cond, half = n // 4, n // 2 % 2, n % 2
                nc.vector.tensor_copy(keep.gate[:, g, cond, half * 512:half * 512 + 512], pgate[:, n % 4, :]).then_inc(gate_free, 1)

        @block.scalar
        def _(act):
            act.wait_ge(small_in, 64)
            nc.scalar.activation(sig[:], cT[:], ACT.Sigmoid).then_inc(sig_done, 1)
            nc.scalar.activation(dk[:, 0, :], logit[:], ACT.Abs).then_inc(act_a, 1)
            act.wait_ge(act_a, 1)
            nc.scalar.activation(dk[:, 0, :], dk[:, 0, :], ACT.Exp, scale=-1.0).then_inc(ln_in, 1)
            act.wait_ge(ln_out, 1)
            nc.scalar.activation(dk[:, 4, :], dk[:, 1, :], ACT.Ln).then_inc(act_a, 1)
            act.wait_ge(lg_ready, 1)
            act.wait_ge(const_in, 32)
            for n, (dirn, col) in enumerate(((0, 0), (1, 1), (0, 2), (1, 3))):
                nc.scalar.activation(keep.dec[:, n, :], keep.log_decay[:, dirn * 4:dirn * 4 + 4], ACT.Exp, scale=keep.cols[:, col:col + 1])
            nc.scalar.activation(keep.cdec[:], keep.log_decay[:], ACT.Exp, scale=keep.cols[:, 5:6]).then_inc(rel_done, 1)


def stage_project(nc, sem, m, keep, a):
    xt = [m.sb(f"xt{i}", [P, D]) for i in range(2)]
    xn = m.sb("xn", [P, D])
    junk = m.sb("sq_junk", [P, D])
    st = [m.sb(f"st{i}", [P, 3]) for i in range(2)]
    hT = [m.sb(f"hT{i}", [P, KD, P]) for i in range(2)]
    zr = [m.sb(f"zr{i}", [P, Z_RET]) for i in range(2)]
    pT = m.ps("pT", [P, KD, P])
    pz = [m.ps(f"pz{i}", [P, 512]) for i in range(6)]
    x_in = [sem("x_in0"), sem("x_in1")]
    z_out = [sem("z_out0"), sem("z_out1")]
    xt_free, ss_done, rms_done, rstd_done, xn_full, xn_free, T_full, hT_full, hT_free = (
        sem(x) for x in ("xt_free", "ss_done", "rms_done", "rstd_done", "xn_full", "xn_free", "T_full", "hT_full", "hT_free"))
    z_full, zfree_act, zfree_dve = sem("z_full"), sem("zfree_act"), sem("zfree_dve")
    ctx_in = sem("ctx_in")
    xv = a["x"].rearrange("(t p) d -> t p d", p=P)
    zd = keep.z_dram

    with nc.Block() as block:

        @block.sync
        def _(sp):
            sp.dma_start(keep.z1[:, CTX, Q_RANK:Q_RANK + KV_RANK], a["cache_ckv"]).then_inc(ctx_in, 16)
            sp.dma_start(keep.z1[:, CTX, Q_RANK + KV_RANK:Z_ATT], a["cache_krope"]).then_inc(ctx_in, 16)

            def load(t, s):
                sp.wait_ge(xt_free, t + 1)
                sp.dma_start(xt[s][:], xv[t]).then_inc(x_in[s], 16)

            def store(t, s):
                sp.wait_ge(zfree_act, t * 3 + 6)
                sp.wait_ge(zfree_dve, t * 3 + 6)
                sp.dma_start(zd[t], zr[s][:]).then_inc(z_out[s], 16)

            tiles_in_two_stages(sp, load, store)
            sp.wait_ge(ctx_in, 32)
            sp.wait_ge(z_out[0], 16 * 6)
            sp.wait_ge(z_out[1], 16 * 5)

        @block.scalar
        def _(act):
            act.sem_inc(zfree_act, 3)
            act.sem_inc(xt_free, 2)

            def pre(t, s):
                act.wait_ge(x_in[s], use_of(t, s) * 16 + 16)
                nc.scalar.activation(junk[:], xt[s][:], ACT.Square, accum_out=st[s][:, 0:1]).then_inc(ss_done, 1)
                act.wait_ge(ss_done, t + 1)
                nc.scalar.activation(st[s][:, 1:2], st[s][:, 0:1], ACT.Sqrt, scale=1.0 / D, bias=keep.cols[:, 4:5]).then_inc(rms_done, 1)
                act.wait_ge(T_full, t + 1)
                act.wait_ge(hT_free, t + 1)
                c = 0 if isinstance(t, int) and t == 0 else 1
                for k in range(KD):
                    last = nc.scalar.activation(hT[s][:, k, :], pT[:, k, :], ACT.Identity, scale=keep.mod[:, 0, c, k:k + 1],
                                                bias=keep.mod[:, 1, c, k:k + 1])
                last.then_inc(hT_full, 1)

            def post(t, s):
                for c in (0, 2, 4):
                    act.wait_ge(z_full, t * 6 + c + 1)
                    if c == 0:
                        out = keep.z1[:, t, 0:Q_RANK]
                    else:
                        if c == 2:
                            act.wait_ge(z_out[s], use_of(t, s) * 16 + 16)
                        out = zr[s][:, (c - 2) * 512:(c - 1) * 512]
                    nc.scalar.activation(out, pz[c][:], ACT.Copy).then_inc(zfree_act, 1)

            tiles_in_two_stages(act, pre, post)

        @block.vector
        def _(dve):
            dve.sem_inc(zfree_dve, 3)
            dve.sem_inc(z_out[0], 16)
            dve.sem_inc(z_out[1], 16)

            def pre(t, s):
                dve.wait_ge(rms_done, t + 1)
                nc.vector.reciprocal(st[s][:, 2:3], st[s][:, 1:2]).then_inc(rstd_done, 1)
                dve.wait_ge(rstd_done, t + 1)
                dve.wait_ge(xn_free, t + 1)
                nc.vector.tensor_scalar(xn[:], xt[s][:], st[s][:, 2:3], None, ALU.mult).then_inc(xn_full, 1)
                dve.wait_ge(xn_full, t + 1)
                dve.sem_inc(xt_free, 1)

            def post(t, s):
                for c in (1, 3, 5):
                    dve.wait_ge(z_full, t * 6 + c + 1)
                    if c == 1:
                        out, src = keep.z1[:, t, Q_RANK:Z_ATT], pz[1][:, 0:Z_ATT - Q_RANK]
                    else:
                        if c == 3:
                            dve.wait_ge(z_out[s], use_of(t, s) * 16 + 16)
                        out, src = zr[s][:, (c - 2) * 512:(c - 1) * 512], pz[c][:]
                    nc.vector.tensor_copy(out, src).then_inc(zfree_dve, 1)

            tiles_in_two_stages(dve, pre, post)

        @block.tensor
        def _(pe):
            pe.sem_inc(xn_free, 1)
            pe.sem_inc(hT_free, 2)

            def pre(t, s):
                pe.wait_ge(xn_full, t + 1)
                if not (isinstance(t, int) and t == 0):
                    pe.wait_ge(hT_full, t)
                for k in range(KD):
                    last = nc.tensor.transpose(pT[:, k, :], xn[:, k * P:(k + 1) * P], keep.ident)
                last.then_inc(T_full, 1)
                pe.wait_ge(T_full, t + 1)
                pe.sem_inc(xn_free, 1)

            def post(t, s):
                pe.wait_ge(hT_full, t + 1)
                for c, (lo, hi) in enumerate(Z_CUTS):
                    pe.wait_ge(keep.w_in_in[c], 16)
                    pe.wait_ge(zfree_dve if c % 2 else zfree_act, t * 3 + c // 2 + 1)
                    for k in range(KD):
                        last = nc.tensor.matmul(pz[c][:, 0:hi - lo], hT[s][:, k, :], keep.w_in[:, k, lo:hi], start=k == 0, stop=k == KD - 1)
                    last.then_inc(z_full, 1)
                pe.wait_ge(z_full, t * 6 + 6)
                pe.sem_inc(hT_free, 1)

            tiles_in_two_stages(pe, pre, post)


def stage_qkv(nc, sem, m, keep, a):
    w_uq = m.sb("w_uq", [P, 4, HEADS * QK])
    w_ukv = m.sb("w_ukv", [P, 2, HEADS * 2 * P])
    qncol = m.sb("qncol", [P, 4])
    kvn = m.sb("kvn", [P, KV_RANK])
    wqh = m.sb("wqh", [P, QK])
    wkh = m.sb("wkh", [P, QK])
    rope = m.sb("rope", [P, TILES + 1, 2, ROPE])
    junk = m.sb("junk", [P, Z_ATT + HEADS * (NOPE + QK)])
    st = [m.sb(f"qst{i}", [P, 8]) for i in range(2)]
    ckvn = m.sb("ckvn", [P, KV_RANK])
    cq = m.sb("cq", [P, Q_RANK])
    cqT = [m.sb(f"cqT{i}", [P, 4, P]) for i in range(2)]
    ckvT = [m.sb(f"ckvT{i}", [P, 2, P]) for i in range(2)]
    qs = m.sb("qs", [P, HEADS, QK])
    qn = m.sb("qn", [P, HEADS, QK])
    qm = m.sb("qm", [P, 2, HEADS, ROPE])
    qr = m.sb("qr", [P, HEADS, ROPE])
    kn = m.sb("kn", [P, HEADS, NOPE])
    km = m.sb("km", [P, 4, ROPE])
    kr = m.sb("kr", [P, HEADS, ROPE])
    hst = m.sb("hst", [P, 3, 8])
    pcq = m.ps("pcq", [P, 4, P])
    pckv = m.ps("pckv", [P, 512])
    pq = m.ps("pq", [P, 2, 512])
    pkv = m.ps("pkv", [P, 2, 512])
    pf = [m.ps(f"pf{i}", [P, 4, P]) for i in range(2)]

    w_in, z_sq, z_rms, z_rec, ckvn_full = (sem(x) for x in ("qkv_w_in", "z_sq", "z_rms", "z_rec", "ckvn_full"))
    zT_full, cqT_full, ckvT_full, qkv_full, proj_free_a, proj_free_d = (
        sem(x) for x in ("zT_full", "cqT_full", "ckvT_full", "qkv_full", "proj_free_a", "proj_free_d"))
    qs_full, head_sq, head_sum, head_rms, qk_ready = (sem(x) for x in ("qs_full", "head_sq", "head_sum", "head_rms", "qk_ready"))
    f0_full, f1_full, f0_read, f1_read, f2_full, f2_read = (sem(x) for x in ("f0_full", "f1_full", "f0_read", "f1_read", "f2_full", "f2_read"))
    dve_c, cache_out, cq_full = sem("qkv_dve"), sem("cache_out"), sem("cq_full")
    PRE_LINKS, POST_LINKS = 0, 12

    def is_ctx(t):
        return isinstance(t, int) and t == CTX

    with nc.Block() as block:

        def all_tiles(eng, pre, post):
            tiles_in_two_stages(eng, pre, post)
            pre(CTX, 1)
            post(CTX, 1)

        @block.gpsimd
        def _(pool):
            def copy(t):
                if not (isinstance(t, int) and t == 0):
                    pool.wait_ge(zT_full, t)
                nc.gpsimd.tensor_copy(cq[:], keep.z1[:, t, 0:Q_RANK]).then_inc(cq_full, 1)

            copy(0)
            with pool.Fori(1, TILES) as t:
                copy(t)

        @block.sync
        def _(sp):
            sp.dma_start(w_uq[:], a["w_uq"].rearrange("(k p) n -> p k n", p=P)).then_inc(w_in, 16)
            sp.dma_start(w_ukv[:], a["w_ukv"].rearrange("(k p) n -> p k n", p=P)).then_inc(w_in, 16)
            sp.dma_start(qncol[:], a["q_norm_cols"]).then_inc(w_in, 16)
            sp.dma_start(kvn[:], a["kv_norm"].partition_broadcast(P)).then_inc(w_in, 16)
            sp.dma_start(wqh[:], a["q_head_norm"].partition_broadcast(P)).then_inc(w_in, 16)
            sp.dma_start(wkh[:], a["k_head_norm"].partition_broadcast(P)).then_inc(w_in, 16)
            sp.dma_start(rope[:], a["rope"]).then_inc(w_in, 16)
            sp.dma_start(a["out"][3][0, 0], keep.z1[:, 0, Q_RANK + KV_RANK:Z_ATT]).then_inc(cache_out, 16)
            sp.wait_ge(ckvn_full, 1)
            sp.dma_start(a["out"][2][0, 0], ckvn[:]).then_inc(cache_out, 16)
            sp.wait_ge(cache_out, 32)

        @block.scalar
        def _(act):
            act.sem_inc(proj_free_a, 1)
            act.wait_ge(w_in, 112)

            def pre(t, s):
                z = keep.z1[:, t]
                if not is_ctx(t):
                    nc.scalar.activation(junk[:, 0:Q_RANK], z[:, 0:Q_RANK], ACT.Square, scale=Q_RANK ** -0.5, accum_out=st[s][:, 0:1])
                    nc.scalar.activation(junk[:, Q_RANK:Q_RANK + KV_RANK], z[:, Q_RANK:Q_RANK + KV_RANK], ACT.Square, scale=KV_RANK ** -0.5, accum_out=st[s][:, 1:2])
                nc.scalar.activation(junk[:, Q_RANK + KV_RANK:Z_ATT], z[:, Q_RANK + KV_RANK:Z_ATT], ACT.Square, scale=QK ** -0.5, accum_out=st[s][:, 2:3]).then_inc(z_sq, 1)
                act.wait_ge(z_sq, t + 1)
                if not is_ctx(t):
                    nc.scalar.activation(st[s][:, 3:5], st[s][:, 0:2], ACT.Sqrt, bias=keep.cols[:, 4:5]).then_inc(z_rms, 1)
                act.wait_ge(zT_full, t + 1)
                if not is_ctx(t):
                    for k in range(4):
                        last = nc.scalar.activation(cqT[s][:, k, :], pcq[:, k, :], ACT.Identity, scale=qncol[:, k:k + 1])
                    last.then_inc(cqT_full, 1)

            def post(t, s):
                act.wait_ge(qkv_full, t + 1)
                nc.scalar.activation(keep.v_sb[:, t].rearrange("p (b h v) -> p b h v", b=2, h=2),
                                     pkv[:].rearrange("p b (h c) -> p b h c", h=2)[:, :, :, P:2 * P], ACT.Copy)
                for h in range(HEADS):
                    last = nc.scalar.activation(junk[:, Z_ATT + h * NOPE:Z_ATT + (h + 1) * NOPE], pkv[:, h // 2, (h % 2) * 256:(h % 2) * 256 + NOPE], ACT.Square,
                                                scale=QK ** -0.5, accum_out=hst[:, 0, 4 + h:5 + h])
                if not is_ctx(t):
                    act.wait_ge(qs_full, t + 1)
                    for h in range(HEADS):
                        last = nc.scalar.activation(junk[:, Z_ATT + HEADS * NOPE + h * QK:Z_ATT + HEADS * NOPE + (h + 1) * QK], qs[:, h, :], ACT.Square, scale=QK ** -0.5, accum_out=hst[:, 0, h:h + 1])
                last.then_inc(head_sq, 1)
                act.wait_ge(head_sum, t + 1)
                lo = 4 if is_ctx(t) else 0
                nc.scalar.activation(hst[:, 1, lo:8], hst[:, 0, lo:8], ACT.Sqrt, bias=keep.cols[:, 4:5]).then_inc(head_rms, 1)
                if not is_ctx(t):
                    act.wait_ge(f0_full, t + 1)
                    nc.scalar.activation(keep.qTn[:, :, bass.ds(t * P, P)], pf[0][:], ACT.Copy).then_inc(f0_read, 1)
                act.wait_ge(f2_full, t + 1)
                if not is_ctx(t):
                    nc.scalar.activation(keep.qTr[:, :, bass.ds(t * P, P)], pf[0][:, 0:2, :], ACT.Copy)
                nc.scalar.activation(keep.kTr[:, :, bass.ds(t * P, P)], pf[0][:, 2:4, :], ACT.Copy).then_inc(f2_read, 1)

            all_tiles(act, pre, post)

        @block.vector
        def _(dve):
            link = Links(dve, dve_c)
            dve.sem_inc(proj_free_d, 1)
            dve.wait_ge(w_in, 112)

            def pre(t, s):
                z = keep.z1[:, t]
                if not is_ctx(t):
                    dve.wait_ge(z_rms, t + 1)
                    nc.vector.reciprocal(st[s][:, 5:7], st[s][:, 3:5]).then_inc(z_rec, 1)
                    dve.wait_ge(z_rec, t + 1)
                    if not (isinstance(t, int) and t == 0):
                        dve.wait_ge(zT_full, t)
                    if isinstance(t, int) and t == 1:
                        dve.wait_ge(cache_out, 32)
                    nc.vector.scalar_tensor_tensor(out=ckvn[:], in0=z[:, Q_RANK:Q_RANK + KV_RANK], scalar=st[s][:, 6:7],
                                                   in1=kvn[:], op0=ALU.mult, op1=ALU.mult).then_inc(ckvn_full, 1)
                dve.wait_ge(zT_full, t + 1)
                nc.vector.tensor_copy(ckvT[s][:], pckv[:, 0:KV_RANK].rearrange("p (k t) -> p k t", k=2)).then_inc(ckvT_full, 1)

            def rotate(x, cos, sin, m1, m2):
                nc.vector.tensor_mul(m1, x, cos)
                x4 = [v.rearrange("p h (a b f) -> p h a b f", a=2, b=2) for v in (x, sin, m2)]
                for b in range(2):
                    last = nc.vector.tensor_mul(x4[2][:, :, :, b], x4[0][:, :, :, 1 - b], x4[1][:, :, :, b])
                return last

            def post(t, s):
                link.at(t * POST_LINKS)
                dve.wait_ge(qkv_full, t + 1)
                cos = rope[:, t, 0:1].to_broadcast([P, HEADS, ROPE])
                sin = rope[:, t, 1:2].to_broadcast([P, HEADS, ROPE])
                if not is_ctx(t):
                    if not (isinstance(t, int) and t == 0):
                        dve.wait_ge(head_sq, t)
                    nc.vector.tensor_scalar(qs[:].rearrange("p (b h) c -> p b (h c)", b=2), pq[:, :, 0:2 * QK], st[s][:, 5:6], None,
                                            ALU.mult).then_inc(qs_full, 1)
                link(nc.vector.tensor_mul(km[:, 0], keep.z1[:, t, Q_RANK + KV_RANK:Z_ATT], wkh[:, NOPE:QK]))
                link(rotate(km[:, 0:1], rope[:, t, 0:1], rope[:, t, 1:2], km[:, 1:2], km[:, 2:3]))
                link(nc.vector.tensor_add(km[:, 3], km[:, 1], km[:, 2]))
                dve.wait_ge(head_sq, t + 1)
                nc.vector.tensor_scalar(hst[:, 0, 4:8], hst[:, 0, 4:8], st[s][:, 2:3], None, ALU.add).then_inc(head_sum, 1)
                dve.wait_ge(head_rms, t + 1)
                lo = 4 if is_ctx(t) else 0
                link(nc.vector.reciprocal(hst[:, 2, lo:8], hst[:, 1, lo:8]))
                if not (isinstance(t, int) and t == 0):
                    dve.wait_ge(f2_full, t)
                for h in range(HEADS):
                    last = nc.vector.scalar_tensor_tensor(out=kn[:, h, :], in0=pkv[:, h // 2, (h % 2) * 256:(h % 2) * 256 + NOPE],
                                                          scalar=hst[:, 2, 4 + h:5 + h], in1=wkh[:, 0:NOPE], op0=ALU.mult, op1=ALU.mult)
                last.then_inc(proj_free_d, 1)
                for h in range(HEADS):
                    last = nc.vector.tensor_scalar(kr[:, h, :], km[:, 3, :], hst[:, 2, 4 + h:5 + h], None, ALU.mult)
                if is_ctx(t):
                    last.then_inc(qk_ready, 1)
                else:
                    for h in range(HEADS):
                        last = nc.vector.scalar_tensor_tensor(out=qn[:, h, :], in0=qs[:, h, :], scalar=hst[:, 2, h:h + 1],
                                                              in1=wqh[:], op0=ALU.mult, op1=ALU.mult)
                    link(last)
                    link(rotate(qn[:, :, NOPE:QK], cos, sin, qm[:, 0], qm[:, 1]))
                    nc.vector.tensor_add(qr[:], qm[:, 0], qm[:, 1]).then_inc(qk_ready, 1)
                dve.wait_ge(f1_full, t + 1)
                nc.vector.tensor_copy(keep.kTn[:, :, bass.ds(t * P, P)], pf[1][:]).then_inc(f1_read, 1)
                for _ in range(POST_LINKS - link.n):
                    dve.sem_inc(dve_c, 1)

            all_tiles(dve, pre, post)

        @block.tensor
        def _(pe):
            pe.wait_ge(w_in, 112)

            def pre(t, s):
                if not is_ctx(t):
                    pe.wait_ge(ckvn_full, t + 1)
                if not (isinstance(t, int) and t == 0):
                    pe.wait_ge(cqT_full, t)
                    pe.wait_ge(ckvT_full, t)
                if is_ctx(t):
                    z = keep.z1[:, CTX]
                else:
                    pe.wait_ge(cq_full, t + 1)
                    for k in range(4):
                        nc.tensor.transpose(pcq[:, k, :], cq[:, k * P:(k + 1) * P], keep.ident)
                for k in range(2):
                    src = z[:, Q_RANK + k * P:Q_RANK + (k + 1) * P] if is_ctx(t) else ckvn[:, k * P:(k + 1) * P]
                    last = nc.tensor.transpose(pckv[:, k * P:(k + 1) * P], src, keep.ident)
                last.then_inc(zT_full, 1)

            def post(t, s):
                pe.wait_ge(ckvT_full, t + 1)
                if not (isinstance(t, int) and t == 0):
                    pe.wait_ge(head_sq, t)
                    pe.wait_ge(proj_free_d, t + 1)
                if not is_ctx(t):
                    pe.wait_ge(cqT_full, t + 1)
                    for b in range(2):
                        for k in range(4):
                            nc.tensor.matmul(pq[:, b, 0:2 * QK], cqT[s][:, k, :], w_uq[:, k, b * 2 * QK:(b + 1) * 2 * QK], start=k == 0, stop=k == 3)
                for b in range(2):
                    for k in range(2):
                        last = nc.tensor.matmul(pkv[:, b, :], ckvT[s][:, k, :], w_ukv[:, k, b * 512:(b + 1) * 512], start=k == 0, stop=k == 1)
                last.then_inc(qkv_full, 1)
                pe.wait_ge(qk_ready, t + 1)
                if not (isinstance(t, int) and t == 0):
                    pe.wait_ge(f2_read, t)
                    pe.wait_ge(f1_read, t)
                if not is_ctx(t):
                    for h in range(HEADS):
                        last = nc.tensor.transpose(pf[0][:, h, :], qn[:, h, 0:NOPE], keep.ident)
                    last.then_inc(f0_full, 1)
                for h in range(HEADS):
                    last = nc.tensor.transpose(pf[1][:, h, :], kn[:, h, :], keep.ident)
                last.then_inc(f1_full, 1)
                if not is_ctx(t):
                    pe.wait_ge(f0_read, t + 1)
                    for b in range(2):
                        nc.tensor.transpose(pf[0][:, b, :], qr[:, 2 * b:2 * b + 2, :].rearrange("p h c -> p (h c)"), keep.ident)
                for b in range(2):
                    last = nc.tensor.transpose(pf[0][:, 2 + b, :], kr[:, 2 * b:2 * b + 2, :].rearrange("p h c -> p (h c)"), keep.ident)
                last.then_inc(f2_full, 1)

            all_tiles(pe, pre, post)


def stage_attention(nc, sem, m, keep, a):
    KT = TILES
    qcn = m.sb("qcn", [P, HEADS, P])
    qcr = m.sb("qcr", [P, 2, P])
    probs = [m.sb(f"probs{i}", [P, KT * P]) for i in range(2)]
    pT_sb = m.sb("pT_sb", [P, KT, P])
    sst = [m.sb(f"sst{i}", [P, 4]) for i in range(2)]
    ps_s = m.ps("ps_s", [P, 3 * 512])
    ps_t = m.ps("ps_t", [P, 12, P])
    ps_o = m.ps("ps_o", [P, P])
    SCALE = QK ** -0.5
    q_full, s_full, s_read, max_done, bias_done, p_full, t_full, pt_a, pt_d, o_full, rec_done, o_read = (
        sem(x) for x in ("q_full", "s_full", "s_read", "max_done", "bias_done", "p_full", "pt_full", "pt_act", "pt_dve",
                         "o_full", "rec_done", "o_read"))

    def spans(t):
        if isinstance(t, int) and t == 0:
            return [(0, P)], 1, 0
        return [(0, 512), (512, 1024), (1024, KT * P)], KT, 1

    with nc.Block() as block:

        @block.gpsimd
        def _(pool):
            def copy(t):
                for h in range(HEADS):
                    if not (isinstance(t, int) and t == 0):
                        pool.wait_ge(s_full, (t - 1) * HEADS + h + 1)
                    if h % 2 == 0:
                        if not (isinstance(t, int) and t == 0):
                            pool.wait_ge(s_full, (t - 1) * HEADS + h + 2)
                        nc.gpsimd.tensor_copy(qcr[:, h // 2, :], keep.qTr[:, h // 2, bass.ds(t * P, P)])
                    nc.gpsimd.tensor_copy(qcn[:, h, :], keep.qTn[:, h, bass.ds(t * P, P)]).then_inc(q_full, 1)

            copy(0)
            copy(1)
            with pool.Fori(2, TILES) as t:
                copy(t)

        @block.tensor
        def _(pe):
            def scores(t, h):
                n = t * HEADS + h
                cuts, _, k0 = spans(t)
                pe.wait_ge(q_full, n + 1)
                if not (isinstance(n, int) and n == 0):
                    pe.wait_ge(s_read, n)
                r = slice((h % 2) * ROPE, (h % 2 + 1) * ROPE)
                for lo, hi in cuts:
                    nc.tensor.matmul(ps_s[:, lo:hi], qcn[:, h, :], keep.kTn[:, h, k0 * P + lo:k0 * P + hi], start=True, stop=False)
                    last = nc.tensor.matmul(ps_s[:, lo:hi], qcr[r, h // 2, :], keep.kTr[r, h // 2, k0 * P + lo:k0 * P + hi], start=False, stop=True)
                last.then_inc(s_full, 1)

            def values(t, h):
                n = t * HEADS + h
                _, kts, k0 = spans(t)
                pe.wait_ge(p_full, n + 1)
                if not (isinstance(n, int) and n == 0):
                    pe.wait_ge(pt_a, n)
                    pe.wait_ge(pt_d, n)
                for k in range(kts):
                    last = nc.tensor.transpose(ps_t[:, k, :], probs[h % 2][:, k * P:(k + 1) * P], keep.ident)
                last.then_inc(t_full, 1)
                pe.wait_ge(pt_a, n + 1)
                pe.wait_ge(pt_d, n + 1)
                if not (isinstance(n, int) and n == 0):
                    pe.wait_ge(o_read, n)
                for k in range(kts):
                    last = nc.tensor.matmul(ps_o[:], pT_sb[:, k, :], keep.v_sb[:, k0 + k, h * P:(h + 1) * P], start=k == 0, stop=k == kts - 1)
                last.then_inc(o_full, 1)

            def tile(t, more=True):
                for h in range(HEADS):
                    if h < HEADS - 1:
                        scores(t, h + 1)
                    elif more:
                        scores(t + 1, 0)
                    values(t, h)

            scores(0, 0)
            tile(0)
            with pe.Fori(1, TILES - 1) as t:
                tile(t)
            tile(TILES - 1, more=False)

        @block.scalar
        def _(act):
            def exps(t, h):
                n = t * HEADS + h
                cuts, kts, _ = spans(t)
                act.wait_ge(bias_done, n + 1)
                nc.scalar.activation(probs[h % 2][:, 0:kts * P], ps_s[:, 0:kts * P], ACT.Exp, scale=SCALE, bias=sst[h % 2][:, 1:2],
                                     accum_out=sst[h % 2][:, 2:3]).then_inc(p_full, 1)
                act.wait_ge(p_full, n + 1)
                act.sem_inc(s_read, 1)

            def evict(t, h):
                n = t * HEADS + h
                _, kts, _ = spans(t)
                act.wait_ge(t_full, n + 1)
                if kts > 4:
                    nc.scalar.activation(pT_sb[:, 4:kts, :], ps_t[:, 4:kts, :], ACT.Copy).then_inc(pt_a, 1)
                else:
                    act.sem_inc(pt_a, 1)

            def tile(t, more=True):
                for h in range(HEADS):
                    if h < HEADS - 1:
                        exps(t, h + 1)
                    elif more:
                        exps(t + 1, 0)
                    evict(t, h)

            exps(0, 0)
            tile(0)
            with act.Fori(1, TILES - 1) as t:
                tile(t)
            tile(TILES - 1, more=False)

        @block.vector
        def _(dve):
            def maxima(t, h):
                n = t * HEADS + h
                _, kts, _ = spans(t)
                dve.wait_ge(s_full, n + 1)
                nc.vector.reduce_max(sst[h % 2][:, 0:1], ps_s[:, 0:kts * P], AX.X).then_inc(max_done, 1)
                dve.wait_ge(max_done, n + 1)
                nc.vector.tensor_scalar(sst[h % 2][:, 1:2], sst[h % 2][:, 0:1], -SCALE, None, ALU.mult).then_inc(bias_done, 1)

            def evict(t, h):
                n = t * HEADS + h
                _, kts, _ = spans(t)
                dve.wait_ge(t_full, n + 1)
                if not (isinstance(n, int) and n == 0):
                    dve.wait_ge(o_full, n)
                nc.vector.tensor_copy(pT_sb[:, 0:min(4, kts), :], ps_t[:, 0:min(4, kts), :]).then_inc(pt_d, 1)
                nc.vector.reciprocal(sst[h % 2][:, 3:4], sst[h % 2][:, 2:3]).then_inc(rec_done, 1)
                dve.wait_ge(rec_done, n + 1)
                dve.wait_ge(o_full, n + 1)
                nc.vector.tensor_scalar(keep.mix[:, t, h * P:(h + 1) * P], ps_o[:], sst[h % 2][:, 3:4], None, ALU.mult).then_inc(o_read, 1)

            def tile(t, more=True):
                for h in range(HEADS):
                    if h < HEADS - 1:
                        maxima(t, h + 1)
                    elif more:
                        maxima(t + 1, 0)
                    evict(t, h)

            maxima(0, 0)
            tile(0)
            with dve.Fori(1, TILES - 1) as t:
                tile(t)
            tile(TILES - 1, more=False)


def wait_count(eng, sem, count):
    if not isinstance(count, int) or count > 0:
        eng.wait_ge(sem, count)


def stage_retention(nc, sem, m, keep, a):
    HV = HEADS * P
    kv = [m.sb(f"kv{i}", [P, 2, HV]) for i in range(2)]
    kb = [m.sb(f"kb{i}", [P, HEADS, P]) for i in range(2)]
    s_b = m.sb("s_b", [P, TILES, HV])
    s_f = m.sb("s_f", [P, HV])
    s_fin = m.sb("s_fin", [P, 2, HV])
    zt = [m.sb(f"zt{i}", [P, 4, HEADS, P]) for i in range(2)]
    qf = m.sb("qf", [P, HEADS, P])
    qb = m.sb("qb", [P, HEADS, P])
    kf = [m.sb(f"kf{i}", [P, HEADS, P]) for i in range(2)]
    qT, kT = m.sb("qT", [P, HEADS, P]), m.sb("kT", [P, HEADS, P])
    qfT = [m.sb(f"qfT{i}", [P, HEADS, P]) for i in range(2)]
    qbT = [m.sb(f"qbT{i}", [P, HEADS, P]) for i in range(2)]
    aT = [m.sb(f"aT{i}", [P, HEADS, P]) for i in range(2)]
    sg = [m.sb(f"sg{i}", [P, HV]) for i in range(2)]
    gn = m.sb("gn", [P, HV])
    chunk = m.sb("chunk", [P, 4, P])
    decays = m.sb("decays", [P, 8, P])
    decay_T = m.sb("decay_T", [P, HEADS, P])
    stats = m.sb("stats", [P, HEADS, 6])
    mv = m.sb("mv", [P, HEADS, 2])
    rs = m.sb("rs", [P, 2, HEADS])
    on = m.sb("on", [P, HEADS, P])
    bank_q, bank_k, bank_qf, bank_qb, bank_a, bank_o, bank_s = (
        m.ps(f"bank_{x}", [P, HEADS, P]) for x in ("q", "k", "qf", "qb", "a", "o", "s"))

    s_in, g_in, kv_in, z_in = sem("s_in"), sem("g_in"), [sem("kv_in0"), sem("kv_in1")], [sem("z_in0"), sem("z_in1")]
    kb_full, sb_upd, sb_next = sem("kb_full"), sem("sb_upd"), sem("sb_next")
    qf_full, qb_full, kf_full, qT_full, kT_full, qfT_full, qbT_full = (
        sem(x) for x in ("qf_full", "qb_full", "kf_full", "ret_qT", "ret_kT", "ret_qfT", "ret_qbT"))
    t1_full, t2_full, a_full, aT_full, o_full, st_full, sf_next, sig_full, sg_full = (
        sem(x) for x in ("ret_t1", "ret_t2", "ret_a", "ret_aT", "ret_o", "ret_st", "sf_next", "gate_sig", "gate_silu"))
    decays_full, waited = sem("decays_full"), sem("aggr_waited")
    var_full, std_full, mix_done, dve_d, fin_full, st_out = (
        sem(x) for x in ("ret_var", "ret_std", "ret_mix", "ret_dve", "fin_full", "st_out"))
    zd = keep.z_dram
    LINKS = 3

    with nc.Block() as block:

        @block.sync
        def _(sp):
            sp.dma_start(s_b[:, TILES - 1, :], a["state"][:, 1].rearrange("p h v -> p (h v)")).then_inc(s_in, 16)
            sp.dma_start(s_f[:], a["state"][:, 0].rearrange("p h v -> p (h v)")).then_inc(s_in, 16)
            sp.dma_start(gn[:], a["gn"].partition_broadcast(P)).then_inc(g_in, 16)
            sp.dma_start(chunk[:], a["chunk"]).then_inc(s_in, 16)
            for n in range(TILES - 2):
                if n >= 2:
                    sp.wait_ge(sb_upd, n - 1)
                sp.dma_start(kv[n % 2][:].rearrange("p a c -> p (a c)"), zd[TILES - 1 - n][:, HV:3 * HV]).then_inc(kv_in[n % 2], 16)

            def load(t, s):
                wait_count(sp, mix_done, t - 1)
                sp.dma_start(zt[s][:].rearrange("p a h c -> p (a h c)"), zd[t]).then_inc(z_in[s], 16)

            tiles_in_two_stages(sp, load, lambda t, s: None)
            sp.wait_ge(fin_full, 2)
            for d in range(2):
                sp.dma_start(a["out"][4][0, 0, d].rearrange("h k v -> k h v"), s_fin[:, d].rearrange("p (h v) -> p h v", h=HEADS)).then_inc(st_out, 16)
            sp.wait_ge(st_out, 32)

        @block.gpsimd
        def _(pool):
            def decayed(out, x, n):
                return nc.gpsimd.tensor_mul(out, x, keep.dec[:, n, :].unsqueeze(2).to_broadcast([P, HEADS, P]))

            for n in range(TILES - 2):
                pool.wait_ge(kv_in[n % 2], 16 * (n // 2 + 1))
                wait_count(pool, sb_upd, n - 1)
                decayed(kb[n % 2][:], kv[n % 2][:, 0].rearrange("p (h c) -> p h c", h=HEADS), 3).then_inc(kb_full, 1)

            def pre(t, s):
                pool.wait_ge(z_in[s], use_of(t, s) * 16 + 16)
                wait_count(pool, t2_full, t)
                decayed(qf[:], zt[s][:, 0], 0).then_inc(qf_full, 1)
                decayed(qb[:], zt[s][:, 0], 1).then_inc(qb_full, 1)
                if isinstance(t, int) and t == 0:
                    pool.wait_ge(sb_upd, TILES - 2)
                    decayed(kb[0][:], zt[s][:, 1], 3).then_inc(kb_full, 1)
                pool.wait_ge(sig_full, t + 1)
                nc.gpsimd.tensor_mul(sg[s][:], sg[s][:], zt[s][:, 3].rearrange("p h c -> p (h c)")).then_inc(sg_full, 1)
                pool.wait_ge(sg_full, t * 2 + 1)
                if isinstance(t, int) and t == 0:
                    pool.wait_ge(g_in, 16)
                nc.gpsimd.tensor_mul(sg[s][:], sg[s][:], gn[:]).then_inc(sg_full, 1)

            tiles_in_two_stages(pool, pre, lambda t, s: None)

        @block.tensor
        def _(pe):
            for n in range(TILES - 2):
                pe.wait_ge(kb_full, n + 1)
                wait_count(pe, sb_next, n)
                for h in range(HEADS):
                    last = nc.tensor.matmul(bank_s[:, h, :], kb[n % 2][:, h, :], kv[n % 2][:, 1, h * P:(h + 1) * P], start=True, stop=True)
                last.then_inc(sb_upd, 1)

            def pre(t, s):
                pe.wait_ge(z_in[s], use_of(t, s) * 16 + 16)
                wait_count(pe, qT_full, t)
                wait_count(pe, kT_full, t)
                for h in range(HEADS):
                    nc.tensor.transpose(bank_q[:, h, :], zt[s][:, 0, h, :], keep.ident)
                for h in range(HEADS):
                    last = nc.tensor.transpose(bank_k[:, h, :], zt[s][:, 1, h, :], keep.ident)
                last.then_inc(t1_full, 1)
                pe.wait_ge(qf_full, t + 1)
                pe.wait_ge(qb_full, t + 1)
                wait_count(pe, qfT_full, t)
                wait_count(pe, qbT_full, t)
                for h in range(HEADS):
                    nc.tensor.transpose(bank_qf[:, h, :], qf[:, h, :], keep.ident)
                for h in range(HEADS):
                    last = nc.tensor.transpose(bank_qb[:, h, :], qb[:, h, :], keep.ident)
                last.then_inc(t2_full, 1)
                pe.wait_ge(qT_full, t + 1)
                pe.wait_ge(kT_full, t + 1)
                wait_count(pe, aT_full, t)
                for h in range(HEADS):
                    last = nc.tensor.matmul(bank_a[:, h, :], kT[:, h, :], qT[:, h, :], start=True, stop=True)
                last.then_inc(a_full, 1)

            def post(t, s):
                prompt = isinstance(t, int) and t == 0
                pe.wait_ge(aT_full, t + 1)
                wait_count(pe, mix_done, t)
                if not prompt:
                    pe.wait_ge(qfT_full, t + 1)
                    pe.wait_ge(qbT_full, t + 1)
                    pe.wait_ge(sb_next, TILES - 2)
                    wait_count(pe, sf_next, t - 1)
                    pe.wait_ge(s_in, 48)
                for h in range(HEADS):
                    v = slice(h * P, (h + 1) * P)
                    last = nc.tensor.matmul(bank_o[:, h, :], aT[s][:, h, :], zt[s][:, 2, h, :], start=True, stop=prompt)
                    if not prompt:
                        nc.tensor.matmul(bank_o[:, h, :], qfT[s][:, h, :], s_f[:, v], start=False, stop=False)
                        last = nc.tensor.matmul(bank_o[:, h, :], qbT[s][:, h, :], s_b[:, t, v], start=False, stop=True)
                last.then_inc(o_full, 1)
                pe.wait_ge(kf_full, t + 1)
                if prompt:
                    pe.wait_ge(sb_next, TILES - 2)
                else:
                    wait_count(pe, sf_next, t - 1)
                for h in range(HEADS):
                    last = nc.tensor.matmul(bank_s[:, h, :], kf[s][:, h, :], zt[s][:, 2, h, :], start=True, stop=True)
                last.then_inc(st_full, 1)
                if prompt:
                    pe.wait_ge(fin_full, 1)
                    pe.wait_ge(kb_full, TILES - 1)
                    for h in range(HEADS):
                        last = nc.tensor.matmul(bank_s[:, h, :], kb[0][:, h, :], zt[s][:, 2, h, :], start=True, stop=True)
                    last.then_inc(sb_upd, 1)
                    pe.wait_ge(fin_full, 2)

            tiles_in_two_stages(pe, pre, post)

        @block.scalar
        def _(act):
            act.wait_ge(s_in, 48)
            for n in range(8):
                last = nc.scalar.activation(decays[:, n, :], chunk[:, C_RELF + n // 4, :], ACT.Exp, scale=keep.log_decay[:, n:n + 1])
            last.then_inc(decays_full, 1)

            def pre(t, s):
                act.wait_ge(z_in[s], use_of(t, s) * 16 + 16)
                wait_count(act, mix_done, t - 1)
                nc.scalar.activation(sg[s][:], zt[s][:, 3].rearrange("p h c -> p (h c)"), ACT.Sigmoid).then_inc(sig_full, 1)
                act.wait_ge(t1_full, t + 1)
                wait_count(act, a_full, t)
                nc.scalar.activation(qT[:], bank_q[:], ACT.Copy).then_inc(qT_full, 1)
                act.wait_ge(t2_full, t + 1)
                wait_count(act, o_full, t - 1)
                nc.scalar.activation(qfT[s][:], bank_qf[:], ACT.Copy).then_inc(qfT_full, 1)

            def post(t, s):
                act.wait_ge(var_full, t + 1)
                nc.scalar.activation(rs[:, 0, :], mv[:, :, 1], ACT.Sqrt, bias=keep.cols[:, 4:5]).then_inc(std_full, 1)

            tiles_in_two_stages(act, pre, post)

        @block.vector
        def _(dve):
            link = Links(dve, dve_d)
            dve.wait_ge(s_in, 48)
            dve.wait_ge(decays_full, 1)
            heads = decays[:].rearrange("p (d h) c -> p d h c", d=2)
            for d in range(2):
                last = nc.vector.tensor_mul(heads[:, d], heads[:, d], chunk[:, C_MASKF + d:C_MASKF + d + 1].to_broadcast([P, HEADS, P]))
            link(last)
            link(nc.vector.tensor_add(decay_T[:], heads[:, 0], heads[:, 1]))
            for n in range(TILES - 2):
                t = TILES - 1 - n
                dve.wait_ge(sb_upd, n + 1)
                wait_count(dve, sb_next, n)
                for h in range(HEADS):
                    v = slice(h * P, (h + 1) * P)
                    last = nc.vector.scalar_tensor_tensor(out=s_b[:, t - 1, v], in0=s_b[:, t, v], scalar=keep.cdec[:, 4 + h:5 + h],
                                                          in1=bank_s[:, h, :], op0=ALU.mult, op1=ALU.add)
                last.then_inc(sb_next, 1)

            def pre(t, s):
                dve.wait_ge(z_in[s], use_of(t, s) * 16 + 16)
                wait_count(dve, st_full, t - 1)
                nc.vector.tensor_mul(kf[s][:], zt[s][:, 1], keep.dec[:, 2, :].unsqueeze(2).to_broadcast([P, HEADS, P])).then_inc(kf_full, 1)
                dve.wait_ge(t1_full, t + 1)
                wait_count(dve, a_full, t)
                nc.vector.tensor_copy(kT[:], bank_k[:]).then_inc(kT_full, 1)
                dve.wait_ge(t2_full, t + 1)
                wait_count(dve, o_full, t - 1)
                nc.vector.tensor_copy(qbT[s][:], bank_qb[:]).then_inc(qbT_full, 1)
                dve.wait_ge(a_full, t + 1)
                nc.vector.tensor_mul(aT[s][:], bank_a[:], decay_T[:]).then_inc(aT_full, 1)

            def post(t, s):
                link.at(t * LINKS + 2)
                dve.wait_ge(o_full, t + 1)
                for h in range(HEADS):
                    last = nc.vector.bn_stats(stats[:, h, :], bank_o[:, h, :])
                link(last)
                dve.sem_inc(waited, 1)
                for h in range(HEADS):
                    last = nc.vector.bn_aggr(mv[:, h, :], stats[:, h, :])
                last.then_inc(var_full, 1)
                dve.wait_ge(st_full, t + 1)
                if isinstance(t, int) and t == 0:
                    nc.vector.tensor_copy(s_fin[:, 0, :].rearrange("p (h v) -> p h v", h=HEADS), bank_s[:]).then_inc(fin_full, 1)
                    dve.wait_ge(sb_upd, TILES - 1)
                    nc.vector.tensor_copy(s_fin[:, 1, :].rearrange("p (h v) -> p h v", h=HEADS), bank_s[:]).then_inc(fin_full, 1)
                else:
                    for h in range(HEADS):
                        v = slice(h * P, (h + 1) * P)
                        last = nc.vector.scalar_tensor_tensor(out=s_f[:, v], in0=s_f[:, v], scalar=keep.cdec[:, h:h + 1],
                                                              in1=bank_s[:, h, :], op0=ALU.mult, op1=ALU.add)
                    last.then_inc(sf_next, 1)
                    dve.wait_ge(sf_next, t)
                dve.wait_ge(std_full, t + 1)
                link(nc.vector.reciprocal(rs[:, 1, :], rs[:, 0, :]))
                for h in range(HEADS):
                    last = nc.vector.tensor_scalar(on[:, h, :], bank_o[:, h, :], mv[:, h, 0:1], rs[:, 1, h:h + 1], ALU.subtract, ALU.mult)
                link(last)
                dve.wait_ge(sg_full, t * 2 + 2)
                nc.vector.tensor_mul(keep.mix[:, t, HV:2 * HV], on[:].rearrange("p h c -> p (h c)"), sg[s][:]).then_inc(mix_done, 1)
                dve.wait_ge(mix_done, t + 1)
                assert link.n == LINKS

            tiles_in_two_stages(dve, pre, post)


def stage_scores(nc, sem, m, keep, a):
    G = 2 * PEER_HEADS
    w_out = m.sb("w_out", [P, KD, D])
    wc = m.sb("wc", [P, KD, G, P])
    mx = m.sb("mx", [P, D])
    mT = m.sb("mT", [P, KD, P])
    x1 = m.sb("x1", [P, D])
    xn = m.sb("xn2", [P, D])
    hs = m.sb("hs", [P, KD, P])
    st = m.sb("st2", [P, 3])
    sc = m.sb("sc", [P, G, P])
    sc2 = m.sb("sc2", [P, G, P])
    top = m.sb("top", [P, G, TOPK])
    idx = m.sb("idx", [P, G, TOPK], U32)
    idxf = m.sb("idxf", [P, G, TOPK], BF16)
    best = m.sb("best", [P, PEER_HEADS, TOPK])
    sel = m.sb("sel_i", [P, PEER_HEADS, TOPK], U32)
    selab = m.sb("sel_ab", [P, 2, PEER_HEADS, TOPK], U32)
    selabf = m.sb("sel_abf", [P, 2, PEER_HEADS, TOPK], BF16)
    iota16 = m.sb("iota16", [P, TOPK], BF16)
    pairs = m.sb("pairs", [P, 3, PEER_HEADS, TOPK])
    sums = m.sb("sums", [P, 2, PEER_HEADS])
    pT = m.ps("pT2", [P, KD, P])
    po = m.ps("po", [P, 2, 512])
    psc = m.ps("psc", [P, G, P])
    wp = [sc[:].rearrange("p g k -> p (g k)")[:, 0:D], sc[:].rearrange("p g k -> p (g k)")[:, D:2 * D]]
    skT = sc2[:, 0:2, :]
    cand, cand2 = sc, sc2
    hot, hot2 = (sc2[:].rearrange("p g k -> p (g k)").bitcast(BF16)[:, n * 2 * D:(n + 1) * 2 * D].rearrange(
        "p (h k c) -> p h k c", h=PEER_HEADS, k=TOPK) for n in range(2))

    w_in, sk_in, wp_in = sem("sco_w_in"), sem("sk_in"), [sem("wp_in0"), sem("wp_in1")]
    wc_full, wc_read_a, wc_read_d = sem("wc_full"), sem("wc_read_a"), sem("wc_read_d")
    mx_full, mt_full, mT_full, po_full, x_in, x1_full, x1_out, ss, rms, rec, xn_full = (
        sem(x) for x in ("mx_full", "mt_full", "mT_full", "po_full", "xt2_in", "x1_full", "x1_out", "ss2", "rms2", "rec2", "xn2_full"))
    ht_full, hs_full, h2_out, psc_full, sc_a, sc_d, dve_t, e_in, e_out, pairs_full, pt_full, pairs_read, po_x = (
        sem(x) for x in ("ht_full", "hs_full", "h2_out", "psc_full", "sc_act", "sc_dve", "topk_dve", "e_in", "e_out",
                         "pairs_full", "pairsT_full", "pairs_read", "po_x"))
    waited = sem("sort_waited")
    LINKS = 23
    xv = a["x"].rearrange("(t p) d -> t p d", p=P)
    wpv = a["w_pqT"].rearrange("(g p) d -> g p d", p=P)

    with nc.Block() as block:

        @block.sync
        def _(sp):
            sp.dma_start(skT, a["keysT"]).then_inc(sk_in, 16)
            for g in range(G):
                wait_count(sp, wc_full, 2 * g - 2)
                sp.dma_start(wp[g % 2], wpv[g]).then_inc(wp_in[g % 2], 16)
            sp.dma_start(w_out[:], a["w_out"].rearrange("(k p) n -> p k n", p=P)).then_inc(w_in, 16)

            def tile(t):
                wait_count(sp, x1_out, t * 16)
                wait_count(sp, xn_full, t)
                sp.sem_inc(waited, 1)
                sp.dma_start(x1[:], xv[t]).then_inc(x_in, 16)
                sp.wait_ge(x1_full, t + 1)
                sp.dma_start(keep.x1_dram[t], x1[:]).then_inc(x1_out, 16)
                sp.wait_ge(hs_full, t + 1)
                sp.dma_start(keep.h2_dram[:, :, bass.ds(t * P, P)], hs[:]).then_inc(h2_out, 16)

            tile(0)
            with sp.Fori(1, TILES) as t:
                tile(t)
            sp.wait_ge(x1_out, 16 * TILES)
            sp.wait_ge(h2_out, 16 * TILES)

        @block.gpsimd
        def _(pool):
            nc.gpsimd.tensor_copy(iota16[:], keep.grid[:, C_IOTA, 0:TOPK]).then_inc(e_in, 1)

            def tile(t):
                wait_count(pool, mt_full, t)
                nc.gpsimd.tensor_copy(mx[:], keep.mix[:, t, :]).then_inc(mx_full, 1)

            tile(0)
            with pool.Fori(1, TILES) as t:
                tile(t)

        @block.tensor
        def _(pe):
            pe.wait_ge(sk_in, 16)
            n = 0
            for g in range(G):
                pe.wait_ge(wp_in[g % 2], 16 * (g // 2 + 1))
                for half in range(2):
                    bank = psc[:, 4 * (n % 4):4 * (n % 4) + 4, :]
                    wait_count(pe, wc_read_a if n % 2 == 0 else wc_read_d, n // 2 - 1)
                    for k in range(4):
                        at = (half * 4 + k) * P
                        last = nc.tensor.matmul(bank[:, k, :], wp[g % 2][:, at:at + P], skT[:, g % 2, :], start=True, stop=True)
                    last.then_inc(wc_full, 1)
                    n += 1
            pe.wait_ge(w_in, 16)
            pe.wait_ge(wc_read_a, G)
            pe.wait_ge(wc_read_d, G)

            def project(t):
                pe.wait_ge(mx_full, t + 1)
                wait_count(pe, hs_full, t)
                for k in range(KD):
                    last = nc.tensor.transpose(pT[:, k, :], mx[:, k * P:(k + 1) * P], keep.ident)
                last.then_inc(mt_full, 1)
                pe.wait_ge(mT_full, t + 1)
                wait_count(pe, po_x, t)
                for half in range(2):
                    for k in range(KD):
                        last = nc.tensor.matmul(po[:, half, :], mT[:, k, :], w_out[:, k, half * 512:(half + 1) * 512], start=k == 0, stop=k == KD - 1)
                last.then_inc(po_full, 1)

            def scores(t):
                pe.wait_ge(xn_full, t + 1)
                wait_count(pe, pairs_read, t - 1)
                for k in range(KD):
                    last = nc.tensor.transpose(pT[:, k, :], xn[:, k * P:(k + 1) * P], keep.ident)
                last.then_inc(ht_full, 1)
                pe.wait_ge(hs_full, t + 1)
                wait_count(pe, sc_a, t)
                wait_count(pe, sc_d, t)
                for b in range(4):
                    for k in range(KD):
                        last = nc.tensor.matmul(psc[:, 4 * b:4 * b + 4, :], hs[:, k, :], wc[:, k, 4 * b:4 * b + 4, :], start=k == 0, stop=k == KD - 1)
                last.then_inc(psc_full, 1)

            def pairs_to_columns(t):
                pe.wait_ge(pairs_full, t + 1)
                wait_count(pe, pairs_read, t)
                for n in range(3):
                    last = nc.tensor.transpose(pT[:, n, :], pairs[:, n].rearrange("p h k -> p (h k)"), keep.ident)
                last.then_inc(pt_full, 1)

            project(0)
            scores(0)
            project(1)
            scores(1)
            project(2)
            pairs_to_columns(0)
            with pe.Fori(2, TILES - 1) as t:
                scores(t)
                project(t + 1)
                pairs_to_columns(t - 1)
            scores(TILES - 1)
            pairs_to_columns(TILES - 2)
            pairs_to_columns(TILES - 1)

        @block.scalar
        def _(act):
            for n in range(0, 2 * G, 2):
                act.wait_ge(wc_full, n + 1)
                nc.scalar.activation(wc[:, (n % 2) * 4:(n % 2) * 4 + 4, n // 2, :], psc[:, 4 * (n % 4):4 * (n % 4) + 4, :], ACT.Copy).then_inc(wc_read_a, 1)

            def mix_columns(t):
                act.wait_ge(mt_full, t + 1)
                wait_count(act, po_full, t)
                nc.scalar.activation(mT[:], pT[:], ACT.Copy).then_inc(mT_full, 1)

            def norm(t):
                act.wait_ge(x1_full, t + 1)
                wait_count(act, ht_full, t)
                nc.scalar.activation(xn[:], x1[:], ACT.Square, accum_out=st[:, 0:1]).then_inc(ss, 1)
                act.wait_ge(ss, t + 1)
                nc.scalar.activation(st[:, 1:2], st[:, 0:1], ACT.Sqrt, scale=1.0 / D, bias=keep.cols[:, 4:5]).then_inc(rms, 1)
                act.wait_ge(ht_full, t + 1)
                wait_count(act, h2_out, t * 16)
                wait_count(act, psc_full, t)
                c = 0 if isinstance(t, int) and t == 0 else 1
                for k in range(KD):
                    last = nc.scalar.activation(hs[:, k, :], pT[:, k, :], ACT.Identity, scale=keep.mod[:, 2, c, k:k + 1], bias=keep.mod[:, 3, c, k:k + 1])
                last.then_inc(hs_full, 1)

            def keep_scores(t):
                act.wait_ge(psc_full, t + 1)
                wait_count(act, e_in, t + 1)
                nc.scalar.activation(sc[:, 0:8, :], psc[:, 0:8, :], ACT.Copy).then_inc(sc_a, 1)

            def exps(t):
                act.wait_ge(e_in, t + 2)
                nc.scalar.activation(pairs[:, 2], best[:], ACT.Exp).then_inc(e_out, 1)

            mix_columns(0)
            norm(0)
            mix_columns(1)
            with act.Fori(1, TILES - 1) as t:
                norm(t)
                keep_scores(t - 1)
                mix_columns(t + 1)
                exps(t - 1)
            norm(TILES - 1)
            for t in (TILES - 2, TILES - 1):
                keep_scores(t)
                exps(t)

        @block.vector
        def _(dve):
            link = Links(dve, dve_t)
            for n in range(1, 2 * G, 2):
                dve.wait_ge(wc_full, n + 1)
                nc.vector.tensor_copy(wc[:, (n % 2) * 4:(n % 2) * 4 + 4, n // 2, :], psc[:, 4 * (n % 4):4 * (n % 4) + 4, :]).then_inc(wc_read_d, 1)

            def residual(t):
                c = 0 if isinstance(t, int) and t == 0 else 1
                dve.wait_ge(po_full, t + 1)
                wait_count(dve, ht_full, t)
                link(nc.vector.tensor_mul(xn[:], po[:].rearrange("p b c -> p (b c)"), keep.gate[:, 0, c, :]))
                dve.sem_inc(po_x, 1)
                dve.wait_ge(x_in, (t + 1) * 16)
                nc.vector.tensor_add(x1[:], x1[:], xn[:]).then_inc(x1_full, 1)
                dve.wait_ge(rms, t + 1)
                nc.vector.reciprocal(st[:, 2:3], st[:, 1:2]).then_inc(rec, 1)
                dve.wait_ge(rec, t + 1)
                nc.vector.tensor_scalar(xn[:], x1[:], st[:, 2:3], None, ALU.mult).then_inc(xn_full, 1)

            def top_k(t):
                dve.wait_ge(psc_full, t + 1)
                nc.vector.tensor_copy(sc[:, 8:16, :], psc[:, 8:16, :]).then_inc(sc_d, 1)
                dve.wait_ge(sc_d, t + 1)
                dve.wait_ge(sc_a, t + 1)
                dve.sem_inc(waited, 1)
                sixteen_best(sc, sc2, top, idx, G)
                link(nc.vector.tensor_copy(idxf[:], idx[:]))
                c4 = cand[:].rearrange("p g k -> p (g k)").rearrange("p (h a b) -> p h a b", h=PEER_HEADS, a=TOPK)
                t4 = top[:].rearrange("p (h s) k -> p h s k", s=2)
                link(nc.vector.tensor_tensor(c4, t4[:, :, 0, :].unsqueeze(3).to_broadcast([P, PEER_HEADS, TOPK, TOPK]),
                                             t4[:, :, 1, :].unsqueeze(2).to_broadcast([P, PEER_HEADS, TOPK, TOPK]), ALU.add))
                cf = [x[:].rearrange("p g k -> p (g k)").rearrange("p (h c) -> p h c", h=PEER_HEADS) for x in (cand, cand2)]
                dve.sem_inc(waited, 1)
                sixteen_best(cf[0], cf[1], best, sel, PEER_HEADS)
                wait_count(dve, pt_full, t)
                link(nc.vector.tensor_scalar(selab[:, 0], sel[:], 4, None, ALU.logical_shift_right))
                link(nc.vector.tensor_scalar(selab[:, 1], sel[:], TOPK - 1, None, ALU.bitwise_and))
                link(nc.vector.tensor_copy(sums[:, 0, :], best[:, :, 0]))
                nc.vector.tensor_tensor(best[:], best[:], sums[:, 0, :].unsqueeze(2).to_broadcast([P, PEER_HEADS, TOPK]), ALU.subtract).then_inc(e_in, 1)
                link(nc.vector.tensor_copy(selabf[:], selab[:]))
                i4 = idxf[:].rearrange("p (h s) k -> p h s k", s=2)
                shape = [P, PEER_HEADS, TOPK, TOPK]
                for s in range(2):
                    link(nc.vector.tensor_tensor(hot, selabf[:, s].unsqueeze(3).to_broadcast(shape),
                                                 iota16[:].unsqueeze(1).unsqueeze(1).to_broadcast(shape), ALU.is_equal))
                    link(nc.vector.tensor_tensor(hot2, hot, i4[:, :, s, :].unsqueeze(2).to_broadcast(shape), ALU.mult))
                    link(nc.vector.reduce_sum(pairs[:, s], hot2, AX.X))
                dve.wait_ge(e_out, t + 1)
                link(nc.vector.reduce_sum(sums[:, 0, :], pairs[:, 2], AX.X))
                link(nc.vector.reciprocal(sums[:, 1, :], sums[:, 0, :]))
                nc.vector.tensor_tensor(pairs[:, 2], pairs[:, 2], sums[:, 1, :].unsqueeze(2).to_broadcast([P, PEER_HEADS, TOPK]), ALU.mult).then_inc(pairs_full, 1)
                dve.wait_ge(pt_full, t + 1)
                nc.vector.tensor_copy(keep.pairsT[:, :, bass.ds(t * P, P)], pT[:, 0:3, :]).then_inc(pairs_read, 1)

            def sixteen_best(x, rest, values, where, groups):
                for g in range(groups):
                    last = nc.vector.max(values[:, g, 0:8], x[:, g, :])
                link(last)
                dve.sem_inc(waited, 1)
                for g in range(groups):
                    nc.vector.max_index(where[:, g, 0:8], values[:, g, 0:8], x[:, g, :])
                for g in range(groups):
                    last = nc.vector.match_replace(rest[:, g, :], values[:, g, 0:8], x[:, g, :], NEG)
                link(last)
                dve.sem_inc(waited, 1)
                for g in range(groups):
                    last = nc.vector.max(values[:, g, 8:16], rest[:, g, :])
                link(last)
                dve.sem_inc(waited, 1)
                for g in range(groups):
                    last = nc.vector.max_index(where[:, g, 8:16], values[:, g, 8:16], rest[:, g, :])
                link(last)

            residual(0)
            with dve.Fori(1, TILES) as t:
                link.at((t - 1) * LINKS + 1)
                residual(t)
                top_k(t - 1)
            assert link.n == LINKS, link.n
            link.at(TILES * LINKS - LINKS + 1)
            top_k(TILES - 1)


class WeightSteps:
    B = 4
    BLOCK = 32
    STEPS = GROUP * P // B
    PER_BLOCK = BLOCK // B

    def __init__(self, nc, sem, m, keep, banks, name):
        B = self.B
        self.nc, self.keep, self.banks = nc, keep, banks
        self.hot_i = [m.sb(f"{name}_hot_i{i}", [P, B, P], BF16) for i in range(2)]
        self.hot_j = [[m.sb(f"{name}_hot_j{i}{k}", [P, B, P], BF16) for k in range(3)] for i in range(2)]
        self.iota = m.sb(f"{name}_iota_bf", [P, P], BF16)
        self.part_bf = m.sb(f"{name}_part_bf", [P, GROUP * P], BF16)
        self.rest = m.sb(f"{name}_w_rest", [P, GROUP * P])
        self.parts = m.sb(f"{name}_w_parts", [P, 3, GROUP * P])
        self.wt = m.sb(f"{name}_wt", [P, 2, N_KEYS, self.BLOCK])
        self.pw = [m.ps(f"{name}_pw{i}", [P, B, N_KEYS]) for i in range(banks)]
        self.iota_full, self.part_done, self.hot_full, self.pw_full, self.pw_read, self.wt_free, self.stored = (
            sem(f"{name}_{x}") for x in ("iota_full", "part_done", "hot_full", "pw_full", "pw_read", "wt_free", "w_stored"))

    def split(self, dve, g, made):
        nc, base = self.nc, made * 6
        w = self.keep.pairsT[:, 2, g * GROUP * P:(g + 1) * GROUP * P]

        def link(ins, n):
            ins.then_inc(self.part_done, 1)
            dve.wait_ge(self.part_done, base + n)

        for k in range(3):
            src = w if k == 0 else self.rest[:]
            link(nc.vector.tensor_copy(self.part_bf[:], src), 2 * k + 1)
            ins = nc.vector.tensor_copy(self.parts[:, k, :], self.part_bf[:])
            if k < 2:
                ins = nc.vector.tensor_sub(self.rest[:], src, self.part_bf[:])
            link(ins, 2 * k + 2)

    def vector(self, dve, g, n, c, s):
        nc = self.nc
        dve.wait_ge(self.pw_full, n + 1)
        for b in range(self.B):
            i, j = (self.keep.pairsT[:, r, bass.ds(c * self.B + (g * GROUP * P + b), 1)] for r in range(2))
            nc.vector.tensor_scalar(self.hot_i[s][:, b, :], self.iota[:], i, None, ALU.is_equal)
            for k in range(3):
                last = nc.vector.tensor_scalar(self.hot_j[s][k][:, b, :], self.iota[:], j, self.parts[:, k, bass.ds(c * self.B + b, 1)],
                                               ALU.is_equal, ALU.mult)
        last.then_inc(self.hot_full, 1)

    def tensor(self, pe, n, s):
        pe.wait_ge(self.hot_full, n + 1)
        wait_count(pe, self.pw_read, n + 1 - self.banks)
        for b in range(self.B):
            for k in range(3):
                last = self.nc.tensor.matmul(self.pw[s % self.banks][:, b, :], self.hot_i[s][:, b, :], self.hot_j[s][k][:, b, :],
                                             start=k == 0, stop=k == 2)
        last.then_inc(self.pw_full, 1)

    def scalar(self, act, n, s):
        act.wait_ge(self.wt_free, n // self.PER_BLOCK + 1)
        act.wait_ge(self.pw_full, n + 3)
        out = self.wt[:, (n // self.PER_BLOCK) % 2, :, bass.ds((n % self.PER_BLOCK) * self.B, self.B)]
        self.nc.scalar.activation(out.rearrange("p j b -> p b j"), self.pw[s % self.banks][:], ACT.Copy).then_inc(self.pw_read, 1)

    def store(self, eng, block, at):
        wait_count(eng, self.stored, block * 16)
        eng.sem_inc(self.wt_free, 1)
        eng.wait_ge(self.pw_read, block * self.PER_BLOCK + self.PER_BLOCK)
        eng.dma_start(self.keep.w_dram[at], self.wt[:, block % 2]).then_inc(self.stored, 16)


def stage_weights(nc, sem, m, keep, a):
    w = WeightSteps(nc, sem, m, keep, 2, "first")
    BLOCKS = w.STEPS // w.PER_BLOCK

    def steps(eng, body):
        body(0, 0)
        body(1, 1)
        with eng.Fori(1, w.STEPS // 2) as k:
            for s in range(2):
                body(k * 2 + s, s)

    with nc.Block() as block:

        @block.vector
        def _(dve):
            nc.vector.tensor_copy(w.iota[:], keep.grid[:, C_IOTA, :]).then_inc(w.iota_full, 1)
            dve.wait_ge(w.iota_full, 1)
            w.split(dve, 0, 0)
            steps(dve, lambda n, s: w.vector(dve, 0, n, n, s))

        @block.tensor
        def _(pe):
            pe.sem_inc(w.pw_full, 2)
            steps(pe, lambda n, s: w.tensor(pe, n, s))

        @block.scalar
        def _(act):
            act.sem_inc(w.wt_free, 1)
            steps(act, lambda n, s: w.scalar(act, n, s))

        @block.sync
        def _(sp):
            w.store(sp, 0, 0)
            with sp.Fori(1, BLOCKS) as b:
                w.store(sp, b, b)
            sp.wait_ge(w.stored, 16 * BLOCKS)


def stage_experts(nc, sem, m, keep, a):
    GT = GROUP * P
    GROUPS = T // GT
    J = N_KEYS
    h_hi, h_lo = m.sb("h_hi", [P, KD, GT], F32R), m.sb("h_lo", [P, KD, GT], F32R)
    two = lambda name, shape, dt=F32: [m.sb(f"{name}{i}", shape, dt) for i in range(2)]
    u_raw, u_hi, u_lo = two("u_raw", [P, KD, P]), two("u_hi", [P, KD, P], F32R), two("u_lo", [P, KD, P], F32R)
    v_raw, v_hi, v_lo = two("v_raw", [P, D]), two("v_hi", [P, D], F32R), two("v_lo", [P, D], F32R)
    act_g, g_all, g_hi, g_lo = two("act_g", [P, GT]), two("g_all", [P, GT]), two("g_hi", [P, GT], F32R), two("g_lo", [P, GT], F32R)
    x1 = [m.sb(f"x1g{i}", [P, D]) for i in range(GROUP)]
    y = m.sb("y", [P, D])
    w = WeightSteps(nc, sem, m, keep, 1, "next")
    JC = 8
    TB = GT // w.BLOCK
    w_ring = m.sb("w_ring", [P, 2, TB, JC, w.BLOCK])
    p_a = m.ps("p_a", [P, 512])
    p_y = [m.ps(f"p_y{i}", [P, 2, 512]) for i in range(GROUP)]

    pair = lambda name: [sem(name + "0"), sem(name + "1")]
    h_in, u_in, v_in, w_in = sem("h_in"), pair("u_in"), pair("v_in"), sem("w_load")
    x1_in, y_out = [sem(f"x1_in{i}") for i in range(GROUP)], [sem(f"y_out{i}") for i in range(GROUP)]
    h_hi_full, h_lo_full, uhi_full, ulo_full, vhi_full, vlo_full, a_full, gelu_full, g_full, ghi_full, glo_full, y_step, y_mul, y_full = (
        sem(x) for x in ("h_hi_full", "h_lo_full", "uhi_full", "ulo_full", "vhi_full", "vlo_full", "a_full", "gelu_full",
                         "g_full", "ghi_full", "glo_full", "y_step", "y_mul", "y_full"))

    def blocks(eng, g, pre, post, between=lambda: None, weights=lambda n, c, s: None, late=None):
        both = lambda n, j, s: (pre(n, j, s), late(n, j, s) if late else None)
        o = g * J
        both(o, 0, 0)
        both(o + 1, 1, 1)
        post(o, 0, 0)
        between()

        def turn(k, c0=None):
            for s in range(2):
                j = k * 2 + s
                pre(j + (o + 2), j + 2, s)
                if c0 is not None and not late:
                    weights(j + c0, j, s)
                post(j + (o + 1), j + 1, 1 - s)
                if c0 is not None and late:
                    weights(j + c0, j, s)
                if late:
                    late(j + (o + 2), j + 2, s)

        done = 0
        if g < GROUPS - 1:
            done = w.STEPS
            with eng.Fori(0, done // 2) as k:
                turn(k, g * w.STEPS)
        with eng.Fori(done // 2, J // 2 - 1) as k:
            turn(k)
        post(o + J - 1, J - 1, 1)

    def used(n, s):
        return n // 2 if isinstance(n, int) else (n - s) // 2

    with nc.Block() as block:

        @block.sync
        def _(sp):
            def load(n, j, s):
                wait_count(sp, ulo_full, n - 1)
                sp.dma_start(u_raw[s][:], a["uT"][j]).then_inc(u_in[s], 16)
                wait_count(sp, vlo_full, n - 1)
                sp.dma_start(v_raw[s][:], a["v"][j]).then_inc(v_in[s], 16)

            def store_y(g):
                for i in range(GROUP):
                    t = g * GROUP + i
                    sp.wait_ge(y_full, t + 1)
                    dst = a["out"][0][0] if t == 0 else a["out"][1][0, (t - 1) * P:t * P, :]
                    sp.dma_start(dst, x1[i][:]).then_inc(y_out[i], 16)

            for g in range(GROUPS):
                def between():
                    if g:
                        store_y(g - 1)
                    for i in range(GROUP):
                        wait_count(sp, y_out[i], 16 * g)
                        sp.dma_start(x1[i][:], keep.x1_dram[g * GROUP + i]).then_inc(x1_in[i], 16)

                blocks(sp, g, load, lambda n, j, s: None, between)
            store_y(GROUPS - 1)
            for i in range(GROUP):
                sp.wait_ge(y_out[i], 16 * GROUPS)

        @block.scalar
        def _(act):
            act.sem_inc(w.wt_free, 1)

            def split(n, j, s):
                act.wait_ge(u_in[s], used(n, s) * 16 + 16)
                wait_count(act, a_full, n - 1)
                nc.scalar.activation(u_hi[s][:], u_raw[s][:], ACT.Copy).then_inc(uhi_full, 1)

            def split_v(n, j, s):
                act.wait_ge(v_in[s], used(n, s) * 16 + 16)
                wait_count(act, y_step, n - 1)
                nc.scalar.activation(v_hi[s][:], v_raw[s][:], ACT.Copy).then_inc(vhi_full, 1)

            def gelu(n, j, s):
                act.wait_ge(a_full, n + 1)
                wait_count(act, g_full, n - 1)
                nc.scalar.activation(act_g[s][:], p_a[:, 0:GT], ACT.Gelu).then_inc(gelu_full, 1)

            for g in range(GROUPS):
                blocks(act, g, split, gelu, weights=lambda n, c, s: w.scalar(act, n, s), late=split_v)

        @block.gpsimd
        def _(pool):
            CHUNKS = J // JC

            def load_w(g, c):
                n = c + g * CHUNKS
                wait_count(pool, w_in, n * 16)
                wait_count(pool, g_full, (n - 1) * JC)
                pool.dma_start(w_ring[:, n % 2], keep.w_dram[g * TB:(g + 1) * TB, :, bass.ds(c * JC, JC), :].rearrange("b i j t -> i b j t")).then_inc(w_in, 16)

            def split(n, j, s):
                pool.wait_ge(vhi_full, n + 1)
                wait_count(pool, y_step, n - 1)
                nc.gpsimd.tensor_sub(v_lo[s][:], v_raw[s][:], v_hi[s][:].bitcast(F32)).then_inc(vlo_full, 1)

            for g in range(GROUPS):
                if g:
                    pool.wait_ge(a_full, g * J)
                    pool.wait_ge(w.stored, 16 * g * TB)
                pool.dma_start(h_lo[:].bitcast(F32), keep.h2_dram[:, :, g * GT:(g + 1) * GT]).then_inc(h_in, 16)
                load_w(g, 0)
                load_w(g, 1)
                o = g * J
                split(o, 0, 0)
                split(o + 1, 1, 1)

                def eight(k, stores):
                    for s in range(JC):
                        split(k * JC + (o + 2 + s), None, s % 2)
                    if stores:
                        w.store(pool, k + g * TB, k + (g + 1) * TB)
                    load_w(g, k + 2)

                full = TB if g < GROUPS - 1 else 0
                if full:
                    eight(0, True)
                    with pool.Fori(1, TB) as k:
                        eight(k, True)
                with pool.Fori(full, CHUNKS - 2) as k:
                    eight(k, False)
                for j in range(J - 2 * JC + 2, J):
                    split(o + j, None, j % 2)

        @block.vector
        def _(dve):
            nc.vector.tensor_copy(w.iota[:], keep.grid[:, C_IOTA, :]).then_inc(w.iota_full, 1)
            dve.wait_ge(w.iota_full, 1)

            def split(n, j, s):
                dve.wait_ge(uhi_full, n + 1)
                nc.vector.tensor_sub(u_lo[s][:], u_raw[s][:], u_hi[s][:].bitcast(F32)).then_inc(ulo_full, 1)

            def weigh(n, j, s):
                dve.wait_ge(gelu_full, n + 1)
                dve.wait_ge(w_in, (n // JC) * 16 + 16)
                three = lambda x: x[:].rearrange("p (b t) -> p b t", t=w.BLOCK)
                nc.vector.tensor_mul(three(g_all[s]), three(act_g[s]), w_ring[:, (n // JC) % 2, :, n % JC, :]).then_inc(g_full, 1)
                dve.wait_ge(g_full, n + 1)
                wait_count(dve, y_step, n - 1)
                nc.vector.tensor_copy(g_hi[s][:], g_all[s][:]).then_inc(ghi_full, 1)
                dve.wait_ge(ghi_full, n + 1)
                nc.vector.tensor_sub(g_lo[s][:], g_all[s][:], g_hi[s][:].bitcast(F32)).then_inc(glo_full, 1)

            for g in range(GROUPS):
                dve.wait_ge(h_in, 16 * (g + 1))
                nc.vector.tensor_copy(h_hi[:], h_lo[:].bitcast(F32)).then_inc(h_hi_full, 1)
                dve.wait_ge(h_hi_full, g + 1)
                nc.vector.tensor_sub(h_lo[:], h_lo[:].bitcast(F32), h_hi[:].bitcast(F32)).then_inc(h_lo_full, 1)
                if g < GROUPS - 1:
                    dve.wait_ge(w.pw_full, g * w.STEPS + 2)
                    w.split(dve, g + 1, g)
                blocks(dve, g, split, weigh, weights=lambda n, c, s: w.vector(dve, g + 1, n, c, s))
                dve.wait_ge(y_step, (g + 1) * J)
                for i in range(GROUP):
                    t = g * GROUP + i
                    c = 0 if t == 0 else 1
                    wait_count(dve, y_full, t)
                    nc.vector.tensor_mul(y[:], p_y[i][:].rearrange("p b c -> p (b c)"), keep.gate[:, 1, c, :]).then_inc(y_mul, 1)
                    dve.wait_ge(y_mul, t + 1)
                    dve.wait_ge(x1_in[i], 16 * (g + 1))
                    nc.vector.tensor_add(x1[i][:], x1[i][:], y[:]).then_inc(y_full, 1)

        @block.tensor
        def _(pe):
            pe.sem_inc(w.pw_full, 2)
            for g in range(GROUPS):
                def down(n, j, s):
                    pe.wait_ge(uhi_full, n + 1)
                    wait_count(pe, gelu_full, n)
                    for k in range(KD):
                        nc.tensor.matmul(p_a[:, 0:GT], u_hi[s][:, k, :], h_hi[:, k, :], start=k == 0, stop=False)
                        nc.tensor.matmul(p_a[:, 0:GT], u_hi[s][:, k, :], h_lo[:, k, :], start=False, stop=False)
                    pe.wait_ge(ulo_full, n + 1)
                    for k in range(KD):
                        last = nc.tensor.matmul(p_a[:, 0:GT], u_lo[s][:, k, :], h_hi[:, k, :], start=False, stop=k == KD - 1)
                    last.then_inc(a_full, 1)

                def up(n, j, s):
                    pe.wait_ge(ghi_full, n + 1)
                    pe.wait_ge(vlo_full, n + 1)
                    first, end = (isinstance(j, int) and j == x for x in (0, J - 1))
                    if first:
                        wait_count(pe, y_mul, g * GROUP)
                    for hi in (True, False):
                        if not hi:
                            pe.wait_ge(glo_full, n + 1)
                        for i in range(GROUP):
                            part = (g_hi if hi else g_lo)[s][:, i * P:(i + 1) * P]
                            for vv in (v_hi[s], v_lo[s]) if hi else (v_hi[s],):
                                for half in range(2):
                                    last = nc.tensor.matmul(p_y[i][:, half, :], part, vv[:, half * 512:(half + 1) * 512],
                                                            start=first and hi and vv is v_hi[s], stop=end and not hi)
                    last.then_inc(y_step, 1)

                pe.wait_ge(h_lo_full, g + 1)
                blocks(pe, g, down, up, weights=lambda n, c, s: w.tensor(pe, n, s))



class Keep:
    pass


def build(nc, a, debug=None):
    with ExitStack() as stack:
        top = Mem(nc, stack)
        keep = Keep()

        def run(stage):
            taken = []

            def sem(name):
                taken.append(nc.alloc_semaphore(name=name))
                return taken[-1]

            with ExitStack() as inner:
                stage(nc, sem, Mem(nc, inner), keep, a)
            nc.clear_and_free_semaphores(taken)
            nc.all_engine_barrier()

        keep.grid = top.sb("grid", [P, 2, P])
        keep.ident = keep.grid[:, C_IDENT, :]
        keep.cols = top.sb("cols", [P, 6])
        keep.mod = top.sb("mod", [P, 4, 2, KD])
        keep.gate = top.sb("gate", [P, 2, 2, D])
        keep.dec = top.sb("dec", [P, 4, HEADS])
        keep.cdec = top.sb("cdec", [P, 8])
        keep.log_decay = top.sb("log_decay", [P, 8])
        keep.pairsT = top.sb("pairsT", [P, 3, T])
        keep.z_dram = nc.dram_tensor("z_spill", [TILES, P, Z_RET], F32).ap()
        keep.x1_dram = nc.dram_tensor("x1_spill", [TILES, P, D], F32).ap()
        keep.h2_dram = nc.dram_tensor("h2_spill", [P, KD, T], F32).ap()
        keep.w_dram = nc.dram_tensor("weights_spill", [T // WeightSteps.BLOCK, P, N_KEYS, WeightSteps.BLOCK], F32).ap()
        keep.w_in_in = [stack.enter_context(nc.semaphore(f"w_in_in{c}")) for c in range(6)]

        with ExitStack() as s1:
            m1 = Mem(nc, s1)
            keep.mix = m1.sb("mix", [P, TILES, D])
            keep.z1 = keep.mix[:].rearrange("p t c -> p (t c)")[:, 0:(TILES + 1) * Z_ATT].rearrange("p (t c) -> p t c", c=Z_ATT)
            with ExitStack() as s2:
                keep.w_in = Mem(nc, s2).sb("w_in", [P, KD, IN_DIM])
                run(stage_modulation)
                run(stage_project)
            if debug and debug(nc, stack, keep, "z1"):
                return
            with ExitStack() as s2:
                m2 = Mem(nc, s2)
                keep.qTn = m2.sb("qTn", [P, HEADS, T])
                keep.qTr = m2.sb("qTr", [P, 2, T])
                keep.kTn = m2.sb("kTn", [P, HEADS, T + P])
                keep.kTr = m2.sb("kTr", [P, 2, T + P])
                keep.v_sb = m2.sb("v_sb", [P, TILES + 1, HEADS * P])
                run(stage_qkv)
                if debug and debug(nc, stack, keep, "qkv"):
                    return
                run(stage_attention)
            run(stage_retention)
            if debug and debug(nc, stack, keep, "mix"):
                return
            run(stage_scores)
            if debug and debug(nc, stack, keep, "topk"):
                return
        run(stage_weights)
        if debug and debug(nc, stack, keep, "w"):
            return
        run(stage_experts)


_OUTS = [(1, 128, 1024), (1, 1024, 1024), (1, 1, 128, 256), (1, 1, 128, 64), (1, 1, 2, 4, 128, 128)]


def lay_out(x):
    g = {k: np.asarray(v) for k, v in x.items()}
    blocks = lambda v: np.ascontiguousarray(v.reshape(-1, P).T)
    sel = np.zeros((2, 2, P), np.float32)
    sel[0, 0] = sel[1, 1] = 1.0
    return {
        "x": np.concatenate([g["x_prompt"][0], g["x_sample"][0]]),
        "cT": np.ascontiguousarray(np.stack([g["c_ctx"], g["c"][0]]).reshape(2, KD, P).transpose(2, 1, 0)),
        "cache_ckv": g["cache_ckv"][0, 0], "cache_krope": g["cache_krope"][0, 0],
        "state": np.ascontiguousarray(g["state_ret"][0, 0].transpose(2, 0, 1, 3)),
        "w_ada": g["w_ada"][0], "b_ada": g["b_ada"][0],
        "norm_cols": np.ascontiguousarray(np.stack([blocks(g["norm1_w"][0]), blocks(g["norm2_w"][0])], 1)),
        "w_in": g["w_in"][0], "q_norm_cols": blocks(g["q_norm_w"][0]), "kv_norm": g["kv_norm_w"][0],
        "w_uq": g["w_uq"][0], "w_ukv": g["w_ukv"][0],
        "q_head_norm": g["q_head_norm_w"][0], "k_head_norm": g["k_head_norm_w"][0],
        "decay_logit": g["ret_decay_logit"][0].reshape(-1), "gn": g["ret_gn_w"][0], "w_out": g["w_out"][0],
        "w_pqT": np.ascontiguousarray(g["w_pq"][0].T),
        "keysT": np.ascontiguousarray(np.stack([g["sub_keys1"][0].T, g["sub_keys2"][0].T], 1)),
        "uT": np.ascontiguousarray(g["u_table"][0].reshape(N_KEYS, N_KEYS, KD, P).transpose(1, 3, 2, 0)),
        "v": np.ascontiguousarray(g["v_table"][0].reshape(N_KEYS, N_KEYS, D).transpose(1, 0, 2)),
        "sel": sel, "grid": grid_constants()[0], "chunk": grid_constants()[1], "cols": column_constants(), "rope": rope_constants(),
    }


def kernel(**inputs):
    import concourse.bacc as _bacc
    from concourse.bass_utils import run_bass_kernel_spmd as _run

    nc = _bacc.Bacc("TRN2", target_bir_lowering=False, num_devices=1)
    arrays = lay_out(inputs)
    a = {k: nc.dram_tensor(f"in_{k}", v.shape, F32, kind="ExternalInput").ap() for k, v in arrays.items()}
    a["out"] = [nc.dram_tensor(f"out_{i}", s, F32, kind="ExternalOutput").ap() for i, s in enumerate(_OUTS)]
    build(nc, a)
    r = _run(nc, [{f"in_{k}": v for k, v in arrays.items()}], core_ids=[0])
    return tuple(r.results[0][f"out_{i}"] for i in range(len(_OUTS)))
```

```python
import numpy as np
import concourse.bass as bass
from concourse import mybir
from contextlib import ExitStack

F32 = mybir.dt.float32
F32R = mybir.dt.float32r
U16 = mybir.dt.uint16
U32 = mybir.dt.uint32
BF16 = mybir.dt.bfloat16
ALU = mybir.AluOpType
ACT = mybir.ActivationFunctionType
AX = mybir.AxisListType

P = 128
D = 1024
KD = D // P
TILES = 9
CTX = TILES
T = TILES * P
HEADS = 4
NOPE, ROPE, QK = 128, 64, 192
Q_RANK, KV_RANK = 512, 256
Z_ATT = Q_RANK + KV_RANK + ROPE
Z_RET = 4 * HEADS * P
IN_DIM = Z_ATT + Z_RET
CHUNK = 320
CUT = 3 * CHUNK - Z_ATT
GRID_W = 64
EPS = 1e-6
PEER_HEADS = 8
TOPK = 16
PAIRS = PEER_HEADS * TOPK
N_KEYS = 128
GROUP = 3
NEG = -3.0e38

C_IDENT, C_IOTA = range(2)
C_RELF, C_RELB, C_MASKF, C_MASKB = range(4)


def grid_constants():
    j, i = np.meshgrid(np.arange(P), np.arange(P), indexing="ij")
    k_scale = np.float32(P ** -0.5)
    grid = np.zeros((P, 2, P), np.float32)
    grid[:, C_IDENT] = np.eye(P)
    grid[:, C_IOTA] = i
    out = np.zeros((P, 4, P), np.float32)
    out[:, C_RELF] = np.maximum(i - j, 0)
    out[:, C_RELB] = np.maximum(j - i, 0)
    out[:, C_MASKF] = (i >= j) * k_scale
    out[:, C_MASKB] = (j >= i) * k_scale
    return grid, out


def column_constants():
    p = np.arange(P, dtype=np.float32)
    cols = np.stack([p + 1, P - p, P - 1 - p, p, np.full(P, EPS, np.float32), np.full(P, P, np.float32)], 1)
    wide = 4 * TOPK
    starts = np.concatenate([np.arange(0, wide, TOPK), np.arange(wide, wide + (TOPK - 4) * 4, 4)])
    return np.concatenate([cols, np.tile(starts, (P, 1))], 1).astype(np.float32)


def rope_constants():
    nf = ROPE // 4
    freqs = np.power(np.float32(10000.0), -np.arange(nf, dtype=np.float32) / np.float32(nf)).astype(np.float32)
    t = np.arange(8 * P)
    out = np.zeros((TILES + 1, P, 2, ROPE), np.float32)
    out[:, :, 0] = 1.0
    for axis, pos in enumerate((t // GRID_W, t % GRID_W)):
        ang = pos.astype(np.float32)[:, None] * freqs
        cos, sin = np.cos(ang).astype(np.float32), np.sin(ang).astype(np.float32)
        at = axis * 2 * nf
        out[1:TILES, :, 0, at:at + 2 * nf] = np.concatenate([cos, cos], 1).reshape(8, P, 2 * nf)
        out[1:TILES, :, 1, at:at + 2 * nf] = np.concatenate([-sin, sin], 1).reshape(8, P, 2 * nf)
    return np.ascontiguousarray(out.transpose(1, 0, 2, 3))


class Links:

    def __init__(self, eng, sem):
        self.eng, self.sem, self.base, self.n = eng, sem, 0, 0

    def at(self, base):
        self.base, self.n = base, 0

    def __call__(self, ins):
        self.n += 1
        ins.then_inc(self.sem, 1)
        self.eng.wait_ge(self.sem, self.base + self.n)


def tiles_in_two_stages(eng, pre, post):
    pre(0, 0)
    pre(1, 1)
    post(0, 0)
    with eng.Fori(0, 3) as k:
        pre(k * 2 + 2, 0)
        post(k * 2 + 1, 1)
        pre(k * 2 + 3, 1)
        post(k * 2 + 2, 0)
    pre(8, 0)
    post(7, 1)
    post(8, 0)


def use_of(t, slot):
    if isinstance(t, int):
        return t // 2
    return (t - slot) // 2


class Mem:

    def __init__(self, nc, stack):
        self.nc, self.stack = nc, stack

    def sb(self, name, shape, dt=F32):
        return self.stack.enter_context(self.nc.sbuf_tensor(name, shape, dt))

    def ps(self, name, shape, dt=F32):
        return self.stack.enter_context(self.nc.psum_tensor(name, shape, dt))


def stage_modulation(nc, sem, m, keep, a):
    cT = m.sb("cT", [P, KD, 2])
    sig = m.sb("sig", [P, KD, 2])
    scT = m.sb("scT", [P, KD, 2])
    wada = [m.sb(f"wada{i}", [P, KD, 512]) for i in range(2)]
    brow = [m.sb(f"brow{i}", [2, 512]) for i in range(2)]
    mrow = keep.z1[0:2].rearrange("p t c -> p (t c)")[:, 0:6 * D]
    nw = m.sb("nw", [P, 2, KD])
    sel = m.sb("sel", [2, 2, P])
    logit = m.sb("logit", [P, 8])
    dk = m.sb("dk", [P, 5, 8])
    prow = m.ps("prow", [P, 2, 512])
    pcol = m.ps("pcol", [P, 64])
    pgate = m.ps("pgate", [P, 4, 512])

    const_in, ada_in = sem("const_in"), [sem("ada_in0"), sem("ada_in1")]
    bias_in = [sem("bias_in0"), sem("bias_in1")]
    small_in = sem("small_in")
    sig_done, cond_ready, row_full, row_free, rows_done = (
        sem(x) for x in ("sig_done", "cond_ready", "row_full", "row_free", "rows_done"))
    cols_full, gate_full, gate_free = sem("cols_full"), sem("gate_full"), sem("gate_free")
    dve_a, act_a, lg_ready, ln_in, ln_out, rel_done = (
        sem(x) for x in ("dve_a", "act_a", "lg_ready", "ln_in", "ln_out", "rel_done"))
    CHUNKS = 12
    wv = a["w_ada"].rearrange("(k p) n -> p k n", p=P)
    w_in_v = a["w_in"].rearrange("(k p) n -> p k n", p=P)

    with nc.Block() as block:

        @block.sync
        def _(sp):
            sp.dma_start(cT[:], a["cT"]).then_inc(small_in, 16)
            sp.dma_start(sel[:], a["sel"]).then_inc(small_in, 16)
            sp.dma_start(nw[:], a["norm_cols"]).then_inc(small_in, 16)
            sp.dma_start(logit[:], a["decay_logit"].partition_broadcast(P)).then_inc(small_in, 16)
            sp.dma_start(keep.grid[:], a["grid"]).then_inc(const_in, 16)
            sp.dma_start(keep.cols[:], a["cols"]).then_inc(const_in, 16)
            with sp.Fori(0, CHUNKS // 2) as k:
                for s in range(2):
                    sp.wait_ge(row_full, k * 2 + s + 1)
                    sp.dma_start(wada[s][:], wv[:, :, bass.ds(k * 1024 + s * 512, 512)]).then_inc(ada_in[s], 16)
                    sp.wait_ge(row_free, k * 2 + s + 1)
                    sp.dma_start(brow[s][:], a["b_ada"][bass.ds(k * 1024 + s * 512, 512)].partition_broadcast(2)).then_inc(bias_in[s], 16)
            for q in range(2):
                sp.dma_start(keep.w_raw[q][:], w_in_v[:, 2 * q:2 * q + 2, 0:CHUNK]).then_inc(keep.w_in_in[q], 16)

        @block.tensor
        def _(pe):
            pe.sem_inc(row_full, 2)
            pe.wait_ge(cond_ready, 1)
            with pe.Fori(0, CHUNKS // 2) as k:
                for s in range(2):
                    pe.wait_ge(ada_in[s], (k + 1) * 16)
                    pe.wait_ge(row_free, k * 2 + s + 1)
                    for c in range(KD):
                        last = nc.tensor.matmul(prow[0:2, s, :], scT[:, c, :], wada[s][:, c, :], start=c == 0, stop=c == KD - 1)
                    last.then_inc(row_full, 1)
            pe.wait_ge(rows_done, CHUNKS)
            pe.wait_ge(const_in, 32)
            pe.wait_ge(small_in, 64)
            for n, part in enumerate((1, 0, 4, 3)):
                for c in range(KD):
                    at = part * D + c * P
                    last = nc.tensor.matmul(pcol[:, (n * KD + c) * 2:(n * KD + c) * 2 + 2], mrow[:, at:at + P],
                                            keep.grid[0:2, C_IDENT, 0:2], start=True, stop=True)
            last.then_inc(cols_full, 1)
            n = 0
            for g, part in enumerate((2, 5)):
                for cond in range(2):
                    for half in range(2):
                        if n >= 4:
                            pe.wait_ge(gate_free, n - 3)
                        at = part * D + half * 512
                        nc.tensor.matmul(pgate[:, n % 4, :], sel[:, cond, :], mrow[:, at:at + 512],
                                         start=True, stop=True).then_inc(gate_full, 1)
                        n += 1

        @block.vector
        def _(dve):
            link = Links(dve, dve_a)
            dve.sem_inc(row_free, 2)
            dve.wait_ge(sig_done, 1)
            nc.vector.tensor_mul(scT[:], cT[:], sig[:]).then_inc(cond_ready, 1)
            dve.wait_ge(ln_in, 1)
            e, u, d, mask, lp = (dk[:, n, :] for n in range(5))
            lg = keep.log_decay[:]
            link(nc.vector.tensor_scalar(u, e, 1.0, None, ALU.add))
            link(nc.vector.tensor_scalar(d, u, -1.0, None, ALU.add))
            link(nc.vector.tensor_scalar(mask, u, 1.0, None, ALU.is_equal))
            nc.vector.tensor_add(d, d, mask).then_inc(ln_out, 1)
            dve.wait_ge(act_a, 2)
            dve.wait_ge(ln_out, 1)
            link(nc.vector.tensor_add(lp, lp, mask))
            link(nc.vector.reciprocal(d, d))
            link(nc.vector.tensor_mul(lp, lp, d))
            link(nc.vector.tensor_mul(lp, lp, e))
            nc.vector.scalar_tensor_tensor(out=lg, in0=logit[:], scalar=0.0, in1=lp, op0=ALU.min, op1=ALU.subtract).then_inc(lg_ready, 1)
            dve.wait_ge(rel_done, 1)
            link(nc.vector.tensor_scalar(keep.dec[:, 2:4, :], keep.dec[:, 2:4, :], float(P ** -0.5), None, ALU.mult))
            with dve.Fori(0, CHUNKS // 2) as k:
                for s in range(2):
                    dve.wait_ge(row_full, k * 2 + s + 3)
                    dve.wait_ge(bias_in[s], (k + 1) * 16)
                    at = bass.ds(k * 1024 + s * 512, 512)
                    nc.vector.tensor_add(mrow[:, at], prow[0:2, s, :], brow[s][:]).then_inc(rows_done, 1)
                    dve.wait_ge(rows_done, k * 2 + s + 1)
                    dve.sem_inc(row_free, 1)
            dve.wait_ge(cols_full, 1)
            pc = pcol[:].rearrange("p (n k c) -> p n k c", n=4, k=KD)
            for i in range(2):
                for cond in range(2):
                    nc.vector.scalar_tensor_tensor(out=keep.mod[:, 2 * i, cond, :], in0=pc[:, 2 * i, :, cond], scalar=1.0,
                                                   in1=nw[:, i, :], op0=ALU.add, op1=ALU.mult)
                    nc.vector.tensor_copy(keep.mod[:, 2 * i + 1, cond, :], pc[:, 2 * i + 1, :, cond])
            for n in range(8):
                dve.wait_ge(gate_full, n + 1)
                g, cond, half = n // 4, n // 2 % 2, n % 2
                nc.vector.tensor_copy(keep.gate[:, g, cond, half * 512:half * 512 + 512], pgate[:, n % 4, :]).then_inc(gate_free, 1)

        @block.scalar
        def _(act):
            act.wait_ge(small_in, 64)
            nc.scalar.activation(sig[:], cT[:], ACT.Sigmoid).then_inc(sig_done, 1)
            nc.scalar.activation(dk[:, 0, :], logit[:], ACT.Abs).then_inc(act_a, 1)
            act.wait_ge(act_a, 1)
            nc.scalar.activation(dk[:, 0, :], dk[:, 0, :], ACT.Exp, scale=-1.0).then_inc(ln_in, 1)
            act.wait_ge(ln_out, 1)
            nc.scalar.activation(dk[:, 4, :], dk[:, 1, :], ACT.Ln).then_inc(act_a, 1)
            act.wait_ge(lg_ready, 1)
            act.wait_ge(const_in, 32)
            for n, (dirn, col) in enumerate(((0, 0), (1, 1), (0, 2), (1, 3))):
                nc.scalar.activation(keep.dec[:, n, :], keep.log_decay[:, dirn * 4:dirn * 4 + 4], ACT.Exp, scale=keep.cols[:, col:col + 1])
            nc.scalar.activation(keep.cdec[:], keep.log_decay[:], ACT.Exp, scale=keep.cols[:, 5:6]).then_inc(rel_done, 1)


def stage_project(nc, sem, m, keep, a):
    CHUNKS, PARTS = IN_DIM // CHUNK, 4
    KP = KD // PARTS
    xt = [m.sb(f"xt{i}", [P, D]) for i in range(2)]
    xn = m.sb("xn", [P, D])
    hT = m.sb("hT", [P, KD, P])
    st = [m.sb(f"st{i}", [P, 3]) for i in range(2)]
    h_hi = [m.sb(f"h_hi{t}", [P, KD, P], F32R) for t in range(TILES)]
    h_lo = [m.sb(f"h_lo{t}", [P, KD, P], F32R) for t in range(TILES)]
    zs = [m.sb(f"z_rows{i}", [P, CHUNK]) for i in range(3)]
    pT = [m.ps(f"pT{i}", [P, KD, P]) for i in range(2)]
    pz = [m.ps(f"pz{i}", [P, 512]) for i in range(3)]
    x_in, z_out = [sem(f"x_in{i}") for i in range(2)], [sem(f"z_out{i}") for i in range(3)]
    ss_done, rms_done, rstd_done, xn_full, T_full, mod_full, hi_full, h_full = (
        sem(x) for x in ("ss_done", "rms_done", "rstd_done", "xn_full", "T_full", "mod_full", "proj_hi_full", "h_full"))
    whi_full, w_full, z_full, z_read, ctx_in, waited = (
        sem(x) for x in ("whi_full", "w_full", "z_full", "z_read", "ctx_in", "split_waited"))
    xv = a["x"].rearrange("(t p) d -> t p d", p=P)
    w_in_v = a["w_in"].rearrange("(k p) n -> p k n", p=P)
    w_hi, w_lo = keep.w_hi, keep.w_lo

    def chunks(eng, body):
        body(0, 0)
        with eng.Fori(0, (CHUNKS - 1) // 2) as k:
            body(k * 2 + 1, 1)
            body(k * 2 + 2, 0)

    with nc.Block() as block:

        @block.sync
        def _(sp):
            for t in range(2):
                sp.dma_start(xt[t][:], xv[t]).then_inc(x_in[t], 16)
            sp.dma_start(keep.z1[:, CTX, Q_RANK:Q_RANK + KV_RANK], a["cache_ckv"]).then_inc(ctx_in, 16)
            sp.dma_start(keep.z1[:, CTX, Q_RANK + KV_RANK:Z_ATT], a["cache_krope"]).then_inc(ctx_in, 16)
            def load(c, q):
                sp.wait_ge(w_full, c * PARTS + q - 1)
                sp.dma_start(keep.w_raw[q % 2][:], w_in_v[:, q * KP:(q + 1) * KP, bass.ds(c * CHUNK, CHUNK)]).then_inc(keep.w_in_in[q % 2], 16)

            for q in range(2, PARTS):
                load(0, q)
            with sp.Fori(1, CHUNKS) as c:
                for q in range(PARTS):
                    load(c, q)
            sp.wait_ge(ctx_in, 32)
            for i in range(3):
                sp.wait_ge(z_out[i], 16 * 3 * (CHUNKS - 2))

        @block.gpsimd
        def _(pool):
            def split(c, s):
                if not (isinstance(c, int) and c == 0):
                    pool.wait_ge(z_full, c * TILES)
                for q in range(PARTS):
                    part, raw = slice(q * KP, (q + 1) * KP), keep.w_raw[q % 2]
                    pool.wait_ge(keep.w_in_in[q % 2], c * (PARTS // 2 * 16) + (q // 2 * 16 + 16))
                    pool.sem_inc(waited, 1)
                    nc.gpsimd.tensor_copy(w_hi[s][:, part, :], raw[:]).then_inc(whi_full, 1)
                    pool.wait_ge(whi_full, c * PARTS + q + 1)
                    nc.gpsimd.tensor_sub(w_lo[s][:, part, :], raw[:], w_hi[s][:, part, :].bitcast(F32)).then_inc(w_full, 1)

            chunks(pool, split)

        @block.scalar
        def _(act):
            act.sem_inc(z_read, 3)

            def squares(t):
                s = t % 2
                act.wait_ge(x_in[s], t // 2 * 16 + 16)
                nc.scalar.activation(h_hi[t][:].rearrange("p k c -> p (k c)"), xt[s][:], ACT.Square, accum_out=st[s][:, 0:1]).then_inc(ss_done, 1)
                act.wait_ge(ss_done, t + 1)
                nc.scalar.activation(st[s][:, 1:2], st[s][:, 0:1], ACT.Sqrt, scale=1.0 / D, bias=keep.cols[:, 4:5]).then_inc(rms_done, 1)

            def modulated(t):
                act.wait_ge(T_full, t + 1)
                if t + 2 < TILES:
                    act.dma_start(xt[t % 2][:], xv[t + 2]).then_inc(x_in[t % 2], 16)
                wait_count(act, h_full, t)
                c = 0 if t == 0 else 1
                for k in range(KD):
                    last = nc.scalar.activation(hT[:, k, :], pT[t % 2][:, k, :], ACT.Identity, scale=keep.mod[:, 0, c, k:k + 1],
                                                bias=keep.mod[:, 1, c, k:k + 1])
                last.then_inc(mod_full, 1)

            def evict(c, t):
                act.wait_ge(z_full, (c + 1) * TILES + t + 1)
                bank = pz[t % 3]
                if isinstance(c, int) and c < 2:
                    nc.scalar.activation(keep.z1[:, t, c * CHUNK:(c + 1) * CHUNK], bank[:, 0:CHUNK], ACT.Copy).then_inc(z_read, 1)
                    return
                if isinstance(c, int):
                    nc.scalar.activation(keep.z1[:, t, 2 * CHUNK:Z_ATT], bank[:, 0:CHUNK - CUT], ACT.Copy)
                    wait_count(act, z_out[t % 3], t // 3 * 16)
                    nc.scalar.activation(zs[t % 3][:, 0:CUT], bank[:, CHUNK - CUT:CHUNK], ACT.Copy).then_inc(z_read, 1)
                    act.wait_ge(z_read, c * TILES + t + 4)
                    act.dma_start(keep.z_dram[t][:, 0:CUT], zs[t % 3][:, 0:CUT]).then_inc(z_out[t % 3], 16)
                    return
                act.wait_ge(z_out[t % 3], c * 48 + (t // 3 * 16 - 96))
                nc.scalar.activation(zs[t % 3][:], bank[:, 0:CHUNK], ACT.Copy).then_inc(z_read, 1)
                act.wait_ge(z_read, c * TILES + t + 4)
                act.dma_start(keep.z_dram[t][:, bass.ds(c * CHUNK - Z_ATT, CHUNK)], zs[t % 3][:]).then_inc(z_out[t % 3], 16)

            squares(0)
            for t in range(TILES):
                if t + 1 < TILES:
                    squares(t + 1)
                modulated(t)
                if t:
                    evict(0, t - 1)
            evict(0, TILES - 1)
            for c in (1, 2):
                for t in range(TILES):
                    evict(c, t)
            with act.Fori(3, CHUNKS) as c:
                for t in range(TILES):
                    evict(c, t)

        @block.vector
        def _(dve):
            def normalised(t):
                s = t % 2
                dve.wait_ge(rms_done, t + 1)
                nc.vector.reciprocal(st[s][:, 2:3], st[s][:, 1:2]).then_inc(rstd_done, 1)
                dve.wait_ge(rstd_done, t + 1)
                wait_count(dve, T_full, t)
                nc.vector.tensor_scalar(xn[:], xt[s][:], st[s][:, 2:3], None, ALU.mult).then_inc(xn_full, 1)

            normalised(0)
            for t in range(TILES):
                if t + 1 < TILES:
                    normalised(t + 1)
                dve.wait_ge(mod_full, t + 1)
                nc.vector.tensor_copy(h_hi[t][:], hT[:]).then_inc(hi_full, 1)
                dve.wait_ge(hi_full, t + 1)
                nc.vector.tensor_sub(h_lo[t][:], hT[:], h_hi[t][:].bitcast(F32)).then_inc(h_full, 1)

        @block.tensor
        def _(pe):
            pe.sem_inc(z_full, TILES)

            def transposed(t):
                pe.wait_ge(xn_full, t + 1)
                wait_count(pe, mod_full, t - 1)
                for k in range(KD):
                    last = nc.tensor.transpose(pT[t % 2][:, k, :], xn[:, k * P:(k + 1) * P], keep.ident)
                last.then_inc(T_full, 1)

            def multiply(c, s, t):
                pe.wait_ge(z_read, c * TILES + t + 1)
                for k in range(KD):
                    for n, (h, w) in enumerate(((h_hi, w_hi), (h_hi, w_lo), (h_lo, w_hi))):
                        last = nc.tensor.matmul(pz[t % 3][:, 0:CHUNK], h[t][:, k, :], w[s][:, k, :], start=k == n == 0, stop=k == KD - 1 and n == 2)
                last.then_inc(z_full, 1)

            def chunk(c, s):
                first = isinstance(c, int)
                if first:
                    transposed(0)
                pe.wait_ge(w_full, c * PARTS + PARTS)
                for t in range(TILES):
                    if first:
                        if t + 1 < TILES:
                            transposed(t + 1)
                        pe.wait_ge(h_full, t + 1)
                    multiply(c, s, t)

            chunks(pe, chunk)


def stage_qkv(nc, sem, m, keep, a):
    w_uq = m.sb("w_uq", [P, 4, HEADS * QK])
    w_ukv = m.sb("w_ukv", [P, 2, HEADS * 2 * P])
    qncol = m.sb("qncol", [P, 4])
    kvn = m.sb("kvn", [P, KV_RANK])
    wqh = m.sb("wqh", [P, QK])
    wkh = m.sb("wkh", [P, QK])
    rope = m.sb("rope", [P, TILES + 1, 2, ROPE])
    junk = m.sb("junk", [P, Z_ATT + HEADS * (NOPE + QK)])
    st = [m.sb(f"qst{i}", [P, 8]) for i in range(2)]
    ckvn = m.sb("ckvn", [P, KV_RANK])
    cq = m.sb("cq", [P, Q_RANK])
    cqT = [m.sb(f"cqT{i}", [P, 4, P]) for i in range(2)]
    ckvT = [m.sb(f"ckvT{i}", [P, 2, P]) for i in range(2)]
    qs = m.sb("qs", [P, HEADS, QK])
    qn = m.sb("qn", [P, HEADS, QK])
    qm = m.sb("qm", [P, 2, HEADS, ROPE])
    qr = m.sb("qr", [P, HEADS, ROPE])
    ks = m.sb("ks", [P, HEADS, NOPE])
    kn = m.sb("kn", [P, HEADS, NOPE])
    km = m.sb("km", [P, 4, ROPE])
    kr = m.sb("kr", [P, HEADS, ROPE])
    hst = m.sb("hst", [P, 3, 8])
    pcq = m.ps("pcq", [P, 4, P])
    pckv = m.ps("pckv", [P, 512])
    pq = m.ps("pq", [P, 2, 512])
    pkv = m.ps("pkv", [P, 2, 512])
    pf = [m.ps(f"pf{i}", [P, 4, P]) for i in range(2)]

    w_in, z_sq, z_rms, z_rec, ckvn_full = (sem(x) for x in ("qkv_w_in", "z_sq", "z_rms", "z_rec", "ckvn_full"))
    zT_full, cqT_full, ckvT_full, qkv_full, v_kept, qk_kept = (
        sem(x) for x in ("zT_full", "cqT_full", "ckvT_full", "qkv_full", "v_kept", "qk_kept"))
    head_sq, head_sum, head_rms, head_rec, qk_ready = (sem(x) for x in ("head_sq", "head_sum", "head_rms", "head_rec", "qk_ready"))
    f0_full, f1_full, f0_read, f1_read, f2_full, f2_read = (sem(x) for x in ("f0_full", "f1_full", "f0_read", "f1_read", "f2_full", "f2_read"))
    dve_c, cache_out, cq_full = sem("qkv_dve"), sem("cache_out"), sem("cq_full")
    POST_LINKS = 5

    def is_ctx(t):
        return isinstance(t, int) and t == CTX

    with nc.Block() as block:

        def all_tiles(eng, pre, heads, project, post):
            def turn(t, s):
                pre(t + 1, 1 - s)
                heads(t, s)
                project(t + 1, 1 - s)
                post(t, s)

            pre(0, 0)
            project(0, 0)
            turn(0, 0)
            with eng.Fori(0, 3) as k:
                turn(k * 2 + 1, 1)
                turn(k * 2 + 2, 0)
            turn(7, 1)
            heads(8, 0)
            post(8, 0)
            pre(CTX, 1)
            project(CTX, 1)
            heads(CTX, 1)
            post(CTX, 1)

        nothing = lambda t, s: None

        @block.gpsimd
        def _(pool):
            def copy(t):
                if not (isinstance(t, int) and t == 0):
                    pool.wait_ge(zT_full, t)
                nc.gpsimd.tensor_copy(cq[:], keep.z1[:, t, 0:Q_RANK]).then_inc(cq_full, 1)

            copy(0)
            with pool.Fori(1, TILES) as t:
                copy(t)

        @block.sync
        def _(sp):
            sp.dma_start(w_uq[:], a["w_uq"].rearrange("(k p) n -> p k n", p=P)).then_inc(w_in, 16)
            sp.dma_start(w_ukv[:], a["w_ukv"].rearrange("(k p) n -> p k n", p=P)).then_inc(w_in, 16)
            sp.dma_start(qncol[:], a["q_norm_cols"]).then_inc(w_in, 16)
            sp.dma_start(kvn[:], a["kv_norm"].partition_broadcast(P)).then_inc(w_in, 16)
            sp.dma_start(wqh[:], a["q_head_norm"].partition_broadcast(P)).then_inc(w_in, 16)
            sp.dma_start(wkh[:], a["k_head_norm"].partition_broadcast(P)).then_inc(w_in, 16)
            sp.dma_start(rope[:], a["rope"]).then_inc(w_in, 16)
            sp.dma_start(a["out"][3][0, 0], keep.z1[:, 0, Q_RANK + KV_RANK:Z_ATT]).then_inc(cache_out, 16)
            sp.wait_ge(ckvn_full, 1)
            sp.dma_start(a["out"][2][0, 0], ckvn[:]).then_inc(cache_out, 16)
            sp.wait_ge(cache_out, 32)

        @block.scalar
        def _(act):
            act.wait_ge(w_in, 112)

            def pre(t, s):
                z = keep.z1[:, t]
                if not is_ctx(t):
                    nc.scalar.activation(junk[:, 0:Q_RANK], z[:, 0:Q_RANK], ACT.Square, scale=Q_RANK ** -0.5, accum_out=st[s][:, 0:1])
                    nc.scalar.activation(junk[:, Q_RANK:Q_RANK + KV_RANK], z[:, Q_RANK:Q_RANK + KV_RANK], ACT.Square, scale=KV_RANK ** -0.5, accum_out=st[s][:, 1:2])
                nc.scalar.activation(junk[:, Q_RANK + KV_RANK:Z_ATT], z[:, Q_RANK + KV_RANK:Z_ATT], ACT.Square, scale=QK ** -0.5, accum_out=st[s][:, 2:3]).then_inc(z_sq, 1)
                act.wait_ge(z_sq, t + 1)
                if not is_ctx(t):
                    nc.scalar.activation(st[s][:, 3:5], st[s][:, 0:2], ACT.Sqrt, bias=keep.cols[:, 4:5]).then_inc(z_rms, 1)
                act.wait_ge(zT_full, t + 1)
                if not is_ctx(t):
                    for k in range(4):
                        last = nc.scalar.activation(cqT[s][:, k, :], pcq[:, k, :], ACT.Identity, scale=qncol[:, k:k + 1])
                    last.then_inc(cqT_full, 1)

            def project(t, s):
                act.wait_ge(qkv_full, t + 1)
                nc.scalar.activation(keep.v_sb[:, t].rearrange("p (b h v) -> p b h v", b=2, h=2),
                                     pkv[:].rearrange("p b (h c) -> p b h c", h=2)[:, :, :, P:2 * P], ACT.Copy).then_inc(v_kept, 1)

            def heads(t, s):
                act.wait_ge(qk_kept, t + 1)
                wait_count(act, head_rec, t)
                for h in range(HEADS):
                    last = nc.scalar.activation(junk[:, Z_ATT + h * NOPE:Z_ATT + (h + 1) * NOPE], ks[:, h, :], ACT.Square,
                                                scale=QK ** -0.5, accum_out=hst[:, 0, 4 + h:5 + h])
                if not is_ctx(t):
                    for h in range(HEADS):
                        last = nc.scalar.activation(junk[:, Z_ATT + HEADS * NOPE + h * QK:Z_ATT + HEADS * NOPE + (h + 1) * QK], qs[:, h, :], ACT.Square, scale=QK ** -0.5, accum_out=hst[:, 0, h:h + 1])
                last.then_inc(head_sq, 1)
                act.wait_ge(head_sum, t + 1)
                lo = 4 if is_ctx(t) else 0
                nc.scalar.activation(hst[:, 1, lo:8], hst[:, 0, lo:8], ACT.Sqrt, bias=keep.cols[:, 4:5]).then_inc(head_rms, 1)

            def post(t, s):
                if not is_ctx(t):
                    act.wait_ge(f0_full, t + 1)
                    nc.scalar.activation(keep.qTn[:, :, bass.ds(t * P, P)], pf[0][:], ACT.Copy).then_inc(f0_read, 1)
                act.wait_ge(f2_full, t + 1)
                if not is_ctx(t):
                    nc.scalar.activation(keep.qTr[:, :, bass.ds(t * P, P)], pf[0][:, 0:2, :], ACT.Copy)
                nc.scalar.activation(keep.kTr[:, :, bass.ds(t * P, P)], pf[0][:, 2:4, :], ACT.Copy).then_inc(f2_read, 1)

            all_tiles(act, pre, heads, project, post)

        @block.vector
        def _(dve):
            link = Links(dve, dve_c)
            dve.wait_ge(w_in, 112)

            def pre(t, s):
                z = keep.z1[:, t]
                if not is_ctx(t):
                    dve.wait_ge(z_rms, t + 1)
                    nc.vector.reciprocal(st[s][:, 5:7], st[s][:, 3:5]).then_inc(z_rec, 1)
                    dve.wait_ge(z_rec, t + 1)
                    if not (isinstance(t, int) and t == 0):
                        dve.wait_ge(zT_full, t)
                    if isinstance(t, int) and t == 1:
                        dve.wait_ge(cache_out, 32)
                    nc.vector.scalar_tensor_tensor(out=ckvn[:], in0=z[:, Q_RANK:Q_RANK + KV_RANK], scalar=st[s][:, 6:7],
                                                   in1=kvn[:], op0=ALU.mult, op1=ALU.mult).then_inc(ckvn_full, 1)
                dve.wait_ge(zT_full, t + 1)
                nc.vector.tensor_copy(ckvT[s][:], pckv[:, 0:KV_RANK].rearrange("p (k t) -> p k t", k=2)).then_inc(ckvT_full, 1)

            def rotate(x, cos, sin, m1, m2):
                nc.vector.tensor_mul(m1, x, cos)
                x4 = [v.rearrange("p h (a b f) -> p h a b f", a=2, b=2) for v in (x, sin, m2)]
                for b in range(2):
                    last = nc.vector.tensor_mul(x4[2][:, :, :, b], x4[0][:, :, :, 1 - b], x4[1][:, :, :, b])
                return last

            def project(t, s):
                dve.wait_ge(qkv_full, t + 1)
                dve.wait_ge(v_kept, t + 1)
                if not is_ctx(t):
                    nc.vector.tensor_scalar(qs[:].rearrange("p (b h) c -> p b (h c)", b=2), pq[:, :, 0:2 * QK], st[s][:, 5:6], None, ALU.mult)
                nc.vector.tensor_copy(ks[:].rearrange("p (b h) c -> p b h c", b=2),
                                      pkv[:].rearrange("p b (h c) -> p b h c", h=2)[:, :, :, 0:NOPE]).then_inc(qk_kept, 1)
                dve.wait_ge(qk_kept, t + 1)

            def heads(t, s):
                link.at(t * POST_LINKS)
                cos = rope[:, t, 0:1].to_broadcast([P, HEADS, ROPE])
                sin = rope[:, t, 1:2].to_broadcast([P, HEADS, ROPE])
                link(nc.vector.tensor_mul(km[:, 0], keep.z1[:, t, Q_RANK + KV_RANK:Z_ATT], wkh[:, NOPE:QK]))
                link(rotate(km[:, 0:1], rope[:, t, 0:1], rope[:, t, 1:2], km[:, 1:2], km[:, 2:3]))
                link(nc.vector.tensor_add(km[:, 3], km[:, 1], km[:, 2]))
                dve.wait_ge(head_sq, t + 1)
                nc.vector.tensor_scalar(hst[:, 0, 4:8], hst[:, 0, 4:8], st[s][:, 2:3], None, ALU.add).then_inc(head_sum, 1)
                dve.wait_ge(head_rms, t + 1)
                lo = 4 if is_ctx(t) else 0
                nc.vector.reciprocal(hst[:, 2, lo:8], hst[:, 1, lo:8]).then_inc(head_rec, 1)
                dve.wait_ge(head_rec, t + 1)
                if not (isinstance(t, int) and t == 0):
                    dve.wait_ge(f2_full, t)
                for h in range(HEADS):
                    last = nc.vector.scalar_tensor_tensor(out=kn[:, h, :], in0=ks[:, h, :],
                                                          scalar=hst[:, 2, 4 + h:5 + h], in1=wkh[:, 0:NOPE], op0=ALU.mult, op1=ALU.mult)
                for h in range(HEADS):
                    last = nc.vector.tensor_scalar(kr[:, h, :], km[:, 3, :], hst[:, 2, 4 + h:5 + h], None, ALU.mult)
                if is_ctx(t):
                    last.then_inc(qk_ready, 1)
                else:
                    for h in range(HEADS):
                        last = nc.vector.scalar_tensor_tensor(out=qn[:, h, :], in0=qs[:, h, :], scalar=hst[:, 2, h:h + 1],
                                                              in1=wqh[:], op0=ALU.mult, op1=ALU.mult)
                    link(last)
                    link(rotate(qn[:, :, NOPE:QK], cos, sin, qm[:, 0], qm[:, 1]))
                    nc.vector.tensor_add(qr[:], qm[:, 0], qm[:, 1]).then_inc(qk_ready, 1)
                    assert link.n == POST_LINKS, link.n
                dve.wait_ge(qk_ready, t + 1)

            def post(t, s):
                dve.wait_ge(f1_full, t + 1)
                nc.vector.tensor_copy(keep.kTn[:, :, bass.ds(t * P, P)], pf[1][:]).then_inc(f1_read, 1)

            all_tiles(dve, pre, heads, project, post)

        @block.tensor
        def _(pe):
            pe.wait_ge(w_in, 112)

            def pre(t, s):
                if not is_ctx(t):
                    pe.wait_ge(ckvn_full, t + 1)
                if not (isinstance(t, int) and t == 0):
                    pe.wait_ge(cqT_full, t)
                    pe.wait_ge(ckvT_full, t)
                if is_ctx(t):
                    z = keep.z1[:, CTX]
                else:
                    pe.wait_ge(cq_full, t + 1)
                    for k in range(4):
                        nc.tensor.transpose(pcq[:, k, :], cq[:, k * P:(k + 1) * P], keep.ident)
                for k in range(2):
                    src = z[:, Q_RANK + k * P:Q_RANK + (k + 1) * P] if is_ctx(t) else ckvn[:, k * P:(k + 1) * P]
                    last = nc.tensor.transpose(pckv[:, k * P:(k + 1) * P], src, keep.ident)
                last.then_inc(zT_full, 1)

            def project(t, s):
                pe.wait_ge(ckvT_full, t + 1)
                wait_count(pe, qk_kept, t)
                if not is_ctx(t):
                    pe.wait_ge(cqT_full, t + 1)
                    for b in range(2):
                        for k in range(4):
                            nc.tensor.matmul(pq[:, b, 0:2 * QK], cqT[s][:, k, :], w_uq[:, k, b * 2 * QK:(b + 1) * 2 * QK], start=k == 0, stop=k == 3)
                for b in range(2):
                    for k in range(2):
                        last = nc.tensor.matmul(pkv[:, b, :], ckvT[s][:, k, :], w_ukv[:, k, b * 512:(b + 1) * 512], start=k == 0, stop=k == 1)
                last.then_inc(qkv_full, 1)

            def post(t, s):
                pe.wait_ge(qk_ready, t + 1)
                if not (isinstance(t, int) and t == 0):
                    pe.wait_ge(f2_read, t)
                    pe.wait_ge(f1_read, t)
                if not is_ctx(t):
                    for h in range(HEADS):
                        last = nc.tensor.transpose(pf[0][:, h, :], qn[:, h, 0:NOPE], keep.ident)
                    last.then_inc(f0_full, 1)
                for h in range(HEADS):
                    last = nc.tensor.transpose(pf[1][:, h, :], kn[:, h, :], keep.ident)
                last.then_inc(f1_full, 1)
                if not is_ctx(t):
                    pe.wait_ge(f0_read, t + 1)
                    for b in range(2):
                        nc.tensor.transpose(pf[0][:, b, :], qr[:, 2 * b:2 * b + 2, :].rearrange("p h c -> p (h c)"), keep.ident)
                for b in range(2):
                    last = nc.tensor.transpose(pf[0][:, 2 + b, :], kr[:, 2 * b:2 * b + 2, :].rearrange("p h c -> p (h c)"), keep.ident)
                last.then_inc(f2_full, 1)

            all_tiles(pe, pre, nothing, project, post)


def stage_attention(nc, sem, m, keep, a):
    KT = TILES
    qcn = m.sb("qcn", [P, HEADS, P])
    qcr = m.sb("qcr", [P, 2, P])
    probs = [m.sb(f"probs{i}", [P, KT * P]) for i in range(2)]
    pT_sb = m.sb("pT_sb", [P, KT, P])
    sst = [m.sb(f"sst{i}", [P, 4]) for i in range(2)]
    ps_s = m.ps("ps_s", [P, 3 * 512])
    ps_t = m.ps("ps_t", [P, 12, P])
    ps_o = m.ps("ps_o", [P, P])
    SCALE = QK ** -0.5
    q_full, s_full, s_read, max_done, bias_done, p_full, t_full, pt_a, pt_d, o_full, rec_done, o_read = (
        sem(x) for x in ("q_full", "s_full", "s_read", "max_done", "bias_done", "p_full", "pt_full", "pt_act", "pt_dve",
                         "o_full", "rec_done", "o_read"))

    def spans(t):
        if isinstance(t, int) and t == 0:
            return [(0, P)], 1, 0
        return [(0, 512), (512, 1024), (1024, KT * P)], KT, 1

    with nc.Block() as block:

        @block.gpsimd
        def _(pool):
            def copy(t):
                for h in range(HEADS):
                    if not (isinstance(t, int) and t == 0):
                        pool.wait_ge(s_full, (t - 1) * HEADS + h + 1)
                    if h % 2 == 0:
                        if not (isinstance(t, int) and t == 0):
                            pool.wait_ge(s_full, (t - 1) * HEADS + h + 2)
                        nc.gpsimd.tensor_copy(qcr[:, h // 2, :], keep.qTr[:, h // 2, bass.ds(t * P, P)])
                    nc.gpsimd.tensor_copy(qcn[:, h, :], keep.qTn[:, h, bass.ds(t * P, P)]).then_inc(q_full, 1)

            copy(0)
            copy(1)
            with pool.Fori(2, TILES) as t:
                copy(t)

        @block.tensor
        def _(pe):
            def scores(t, h):
                n = t * HEADS + h
                cuts, _, k0 = spans(t)
                pe.wait_ge(q_full, n + 1)
                if not (isinstance(n, int) and n == 0):
                    pe.wait_ge(s_read, n)
                r = slice((h % 2) * ROPE, (h % 2 + 1) * ROPE)
                for lo, hi in cuts:
                    nc.tensor.matmul(ps_s[:, lo:hi], qcn[:, h, :], keep.kTn[:, h, k0 * P + lo:k0 * P + hi], start=True, stop=False)
                    last = nc.tensor.matmul(ps_s[:, lo:hi], qcr[r, h // 2, :], keep.kTr[r, h // 2, k0 * P + lo:k0 * P + hi], start=False, stop=True)
                last.then_inc(s_full, 1)

            def values(t, h):
                n = t * HEADS + h
                _, kts, k0 = spans(t)
                pe.wait_ge(p_full, n + 1)
                if not (isinstance(n, int) and n == 0):
                    pe.wait_ge(pt_a, n)
                    pe.wait_ge(pt_d, n)
                for k in range(kts):
                    last = nc.tensor.transpose(ps_t[:, k, :], probs[h % 2][:, k * P:(k + 1) * P], keep.ident)
                last.then_inc(t_full, 1)
                pe.wait_ge(pt_a, n + 1)
                if not (isinstance(n, int) and n == 0):
                    pe.wait_ge(o_read, n)
                order = [*range(4, kts), *range(min(4, kts))]
                for k in order:
                    if k == 0:
                        pe.wait_ge(pt_d, n + 1)
                    last = nc.tensor.matmul(ps_o[:], pT_sb[:, k, :], keep.v_sb[:, k0 + k, h * P:(h + 1) * P], start=k == order[0], stop=k == order[-1])
                last.then_inc(o_full, 1)

            def tile(t, more=True):
                for h in range(HEADS):
                    if h < HEADS - 1:
                        scores(t, h + 1)
                    elif more:
                        scores(t + 1, 0)
                    values(t, h)

            scores(0, 0)
            tile(0)
            with pe.Fori(1, TILES - 1) as t:
                tile(t)
            tile(TILES - 1, more=False)

        @block.scalar
        def _(act):
            def exps(t, h):
                n = t * HEADS + h
                cuts, kts, _ = spans(t)
                act.wait_ge(bias_done, n + 1)
                nc.scalar.activation(probs[h % 2][:, 0:kts * P], ps_s[:, 0:kts * P], ACT.Exp, scale=SCALE, bias=sst[h % 2][:, 1:2],
                                     accum_out=sst[h % 2][:, 2:3]).then_inc(p_full, 1)
                act.wait_ge(p_full, n + 1)
                act.sem_inc(s_read, 1)

            def evict(t, h):
                n = t * HEADS + h
                _, kts, _ = spans(t)
                act.wait_ge(t_full, n + 1)
                if kts > 4:
                    nc.scalar.activation(pT_sb[:, 4:kts, :], ps_t[:, 4:kts, :], ACT.Copy).then_inc(pt_a, 1)
                else:
                    act.sem_inc(pt_a, 1)

            def tile(t, more=True):
                for h in range(HEADS):
                    evict(t, h)
                    if h < HEADS - 1:
                        exps(t, h + 1)
                    elif more:
                        exps(t + 1, 0)

            exps(0, 0)
            tile(0)
            with act.Fori(1, TILES - 1) as t:
                tile(t)
            tile(TILES - 1, more=False)

        @block.vector
        def _(dve):
            def maxima(t, h):
                n = t * HEADS + h
                _, kts, _ = spans(t)
                dve.wait_ge(s_full, n + 1)
                nc.vector.reduce_max(sst[h % 2][:, 0:1], ps_s[:, 0:kts * P], AX.X).then_inc(max_done, 1)
                dve.wait_ge(max_done, n + 1)
                nc.vector.tensor_scalar(sst[h % 2][:, 1:2], sst[h % 2][:, 0:1], -SCALE, None, ALU.mult).then_inc(bias_done, 1)

            def evict(t, h):
                n = t * HEADS + h
                _, kts, _ = spans(t)
                dve.wait_ge(t_full, n + 1)
                if not (isinstance(n, int) and n == 0):
                    dve.wait_ge(o_full, n)
                nc.vector.tensor_copy(pT_sb[:, 0:min(4, kts), :], ps_t[:, 0:min(4, kts), :]).then_inc(pt_d, 1)
                nc.vector.reciprocal(sst[h % 2][:, 3:4], sst[h % 2][:, 2:3]).then_inc(rec_done, 1)
                dve.wait_ge(rec_done, n + 1)
                dve.wait_ge(o_full, n + 1)
                nc.vector.tensor_scalar(keep.mix[:, t, h * P:(h + 1) * P], ps_o[:], sst[h % 2][:, 3:4], None, ALU.mult).then_inc(o_read, 1)

            def tile(t, more=True):
                for h in range(HEADS):
                    if h < HEADS - 1:
                        maxima(t, h + 1)
                    elif more:
                        maxima(t + 1, 0)
                    evict(t, h)

            maxima(0, 0)
            tile(0)
            with dve.Fori(1, TILES - 1) as t:
                tile(t)
            tile(TILES - 1, more=False)


def wait_count(eng, sem, count):
    if not isinstance(count, int) or count > 0:
        eng.wait_ge(sem, count)


def stage_retention(nc, sem, m, keep, a):
    HV = HEADS * P
    kv = [m.sb(f"kv{i}", [P, 2, HV]) for i in range(2)]
    kb = [m.sb(f"kb{i}", [P, HEADS, P]) for i in range(2)]
    s_b = m.sb("s_b", [P, TILES, HV])
    s_f = m.sb("s_f", [P, HV])
    s_fin = m.sb("s_fin", [P, 2, HV])
    zt = [m.sb(f"zt{i}", [P, 4, HEADS, P]) for i in range(2)]
    qf = m.sb("qf", [P, HEADS, P])
    qb = m.sb("qb", [P, HEADS, P])
    kf = [m.sb(f"kf{i}", [P, HEADS, P]) for i in range(2)]
    qT, kT = m.sb("qT", [P, HEADS, P]), m.sb("kT", [P, HEADS, P])
    qfT = [m.sb(f"qfT{i}", [P, HEADS, P]) for i in range(2)]
    qbT = [m.sb(f"qbT{i}", [P, HEADS, P]) for i in range(2)]
    aT = [m.sb(f"aT{i}", [P, HEADS, P]) for i in range(2)]
    sg = [m.sb(f"sg{i}", [P, HV]) for i in range(2)]
    gn = m.sb("gn", [P, HV])
    chunk = m.sb("chunk", [P, 4, P])
    decays = m.sb("decays", [P, 8, P])
    decay_T = m.sb("decay_T", [P, HEADS, P])
    stats = m.sb("stats", [P, HEADS, 6])
    mv = m.sb("mv", [P, HEADS, 2])
    rs = m.sb("rs", [P, 2, HEADS])
    on = m.sb("on", [P, HEADS, P])
    bank_q, bank_k, bank_qf, bank_qb, bank_a, bank_s = (
        m.ps(f"bank_{x}", [P, HEADS, P]) for x in ("q", "k", "qf", "qb", "a", "s"))
    bank_o = [m.ps(f"bank_o{i}", [P, HEADS, P]) for i in range(2)]

    s_in, g_in, kv_in, z_in = sem("s_in"), sem("g_in"), [sem("kv_in0"), sem("kv_in1")], [sem("z_in0"), sem("z_in1")]
    kb_full, sb_upd, sb_next = sem("kb_full"), sem("sb_upd"), sem("sb_next")
    qf_full, qb_full, kf_full, qT_full, kT_full, qfT_full, qbT_full = (
        sem(x) for x in ("qf_full", "qb_full", "kf_full", "ret_qT", "ret_kT", "ret_qfT", "ret_qbT"))
    t1_full, t2_full, a_full, aT_full, o_full, st_full, sf_next, sig_full, sg_full = (
        sem(x) for x in ("ret_t1", "ret_t2", "ret_a", "ret_aT", "ret_o", "ret_st", "sf_next", "gate_sig", "gate_silu"))
    decays_full, waited = sem("decays_full"), sem("aggr_waited")
    var_full, std_full, mix_done, dve_d, fin_full, st_out = (
        sem(x) for x in ("ret_var", "ret_std", "ret_mix", "ret_dve", "fin_full", "st_out"))
    zd = keep.z_dram
    LINKS = 3

    with nc.Block() as block:

        @block.sync
        def _(sp):
            sp.dma_start(s_b[:, TILES - 1, :], a["state"][:, 1].rearrange("p h v -> p (h v)")).then_inc(s_in, 16)
            sp.dma_start(s_f[:], a["state"][:, 0].rearrange("p h v -> p (h v)")).then_inc(s_in, 16)
            sp.dma_start(gn[:], a["gn"].partition_broadcast(P)).then_inc(g_in, 16)
            sp.dma_start(chunk[:], a["chunk"]).then_inc(s_in, 16)
            for n in range(TILES - 2):
                if n >= 2:
                    sp.wait_ge(sb_upd, n - 1)
                sp.dma_start(kv[n % 2][:].rearrange("p a c -> p (a c)"), zd[TILES - 1 - n][:, HV:3 * HV]).then_inc(kv_in[n % 2], 16)

            def load(t, s):
                if not (isinstance(t, int) and t < 2):
                    sp.wait_ge(st_full, t - 1)
                    sp.wait_ge(sb_upd, TILES - 1)
                    sp.wait_ge(sg_full, t * 2 - 2)
                sp.dma_start(zt[s][:].rearrange("p a h c -> p (a h c)"), zd[t]).then_inc(z_in[s], 16)

            tiles_in_two_stages(sp, load, lambda t, s: None)
            sp.dma_start(keep.w_out[:], a["w_out"].rearrange("(k p) n -> p k n", p=P)).then_inc(keep.w_out_in, 16)
            sp.wait_ge(fin_full, 2)
            for d in range(2):
                sp.dma_start(a["out"][4][0, 0, d].rearrange("h k v -> k h v"), s_fin[:, d].rearrange("p (h v) -> p h v", h=HEADS)).then_inc(st_out, 16)
            sp.wait_ge(st_out, 32)

        @block.gpsimd
        def _(pool):
            def decayed(out, x, n):
                return nc.gpsimd.tensor_mul(out, x, keep.dec[:, n, :].unsqueeze(2).to_broadcast([P, HEADS, P]))

            for n in range(TILES - 2):
                pool.wait_ge(kv_in[n % 2], 16 * (n // 2 + 1))
                wait_count(pool, sb_upd, n - 1)
                decayed(kb[n % 2][:], kv[n % 2][:, 0].rearrange("p (h c) -> p h c", h=HEADS), 3).then_inc(kb_full, 1)

            def pre(t, s):
                pool.wait_ge(z_in[s], use_of(t, s) * 16 + 16)
                wait_count(pool, t2_full, t)
                decayed(qf[:], zt[s][:, 0], 0).then_inc(qf_full, 1)
                decayed(qb[:], zt[s][:, 0], 1).then_inc(qb_full, 1)
                if isinstance(t, int) and t == 0:
                    pool.wait_ge(sb_upd, TILES - 2)
                    decayed(kb[0][:], zt[s][:, 1], 3).then_inc(kb_full, 1)
                pool.wait_ge(sig_full, t + 1)
                nc.gpsimd.tensor_mul(sg[s][:], sg[s][:], zt[s][:, 3].rearrange("p h c -> p (h c)")).then_inc(sg_full, 1)
                pool.wait_ge(sg_full, t * 2 + 1)
                if isinstance(t, int) and t == 0:
                    pool.wait_ge(g_in, 16)
                nc.gpsimd.tensor_mul(sg[s][:], sg[s][:], gn[:]).then_inc(sg_full, 1)

            tiles_in_two_stages(pool, pre, lambda t, s: None)

        @block.tensor
        def _(pe):
            for n in range(TILES - 2):
                pe.wait_ge(kb_full, n + 1)
                wait_count(pe, sb_next, n)
                for h in range(HEADS):
                    last = nc.tensor.matmul(bank_s[:, h, :], kb[n % 2][:, h, :], kv[n % 2][:, 1, h * P:(h + 1) * P], start=True, stop=True)
                last.then_inc(sb_upd, 1)

            def pre(t, s):
                pe.wait_ge(z_in[s], use_of(t, s) * 16 + 16)
                wait_count(pe, qT_full, t)
                wait_count(pe, kT_full, t)
                for h in range(HEADS):
                    nc.tensor.transpose(bank_q[:, h, :], zt[s][:, 0, h, :], keep.ident)
                for h in range(HEADS):
                    last = nc.tensor.transpose(bank_k[:, h, :], zt[s][:, 1, h, :], keep.ident)
                last.then_inc(t1_full, 1)
                pe.wait_ge(qf_full, t + 1)
                pe.wait_ge(qb_full, t + 1)
                wait_count(pe, qfT_full, t)
                wait_count(pe, qbT_full, t)
                for h in range(HEADS):
                    nc.tensor.transpose(bank_qf[:, h, :], qf[:, h, :], keep.ident)
                for h in range(HEADS):
                    last = nc.tensor.transpose(bank_qb[:, h, :], qb[:, h, :], keep.ident)
                last.then_inc(t2_full, 1)
                pe.wait_ge(qT_full, t + 1)
                pe.wait_ge(kT_full, t + 1)
                wait_count(pe, aT_full, t)
                for h in range(HEADS):
                    last = nc.tensor.matmul(bank_a[:, h, :], kT[:, h, :], qT[:, h, :], start=True, stop=True)
                last.then_inc(a_full, 1)

            def post(t, s):
                prompt = isinstance(t, int) and t == 0
                pe.wait_ge(aT_full, t + 1)
                wait_count(pe, mix_done, t)
                if not prompt:
                    pe.wait_ge(qfT_full, t + 1)
                    pe.wait_ge(qbT_full, t + 1)
                    pe.wait_ge(sb_next, TILES - 2)
                    wait_count(pe, sf_next, t)
                    pe.wait_ge(s_in, 48)
                for h in range(HEADS):
                    v = slice(h * P, (h + 1) * P)
                    last = nc.tensor.matmul(bank_o[s][:, h, :], aT[s][:, h, :], zt[s][:, 2, h, :], start=True, stop=prompt)
                    if not prompt:
                        nc.tensor.matmul(bank_o[s][:, h, :], qfT[s][:, h, :], s_f[:, v], start=False, stop=False)
                        last = nc.tensor.matmul(bank_o[s][:, h, :], qbT[s][:, h, :], s_b[:, t, v], start=False, stop=True)
                last.then_inc(o_full, 1)
                pe.wait_ge(kf_full, t + 1)
                if prompt:
                    pe.wait_ge(sb_next, TILES - 2)
                else:
                    wait_count(pe, sf_next, t)
                for h in range(HEADS):
                    last = nc.tensor.matmul(bank_s[:, h, :], kf[s][:, h, :], zt[s][:, 2, h, :], start=True, stop=True)
                last.then_inc(st_full, 1)
                if prompt:
                    pe.wait_ge(fin_full, 1)
                    pe.wait_ge(kb_full, TILES - 1)
                    for h in range(HEADS):
                        last = nc.tensor.matmul(bank_s[:, h, :], kb[0][:, h, :], zt[s][:, 2, h, :], start=True, stop=True)
                    last.then_inc(sb_upd, 1)
                    pe.wait_ge(fin_full, 2)

            tiles_in_two_stages(pe, pre, post)

        @block.scalar
        def _(act):
            act.wait_ge(s_in, 48)
            for n in range(8):
                last = nc.scalar.activation(decays[:, n, :], chunk[:, C_RELF + n // 4, :], ACT.Exp, scale=keep.log_decay[:, n:n + 1])
            last.then_inc(decays_full, 1)

            def pre(t, s):
                act.wait_ge(z_in[s], use_of(t, s) * 16 + 16)
                wait_count(act, mix_done, t)
                nc.scalar.activation(sg[s][:], zt[s][:, 3].rearrange("p h c -> p (h c)"), ACT.Sigmoid).then_inc(sig_full, 1)
                act.wait_ge(t1_full, t + 1)
                wait_count(act, a_full, t)
                nc.scalar.activation(qT[:], bank_q[:], ACT.Copy).then_inc(qT_full, 1)
                act.wait_ge(t2_full, t + 1)
                wait_count(act, o_full, t - 1)
                nc.scalar.activation(qfT[s][:], bank_qf[:], ACT.Copy).then_inc(qfT_full, 1)

            def post(t, s):
                act.wait_ge(var_full, t + 1)
                nc.scalar.activation(rs[:, 0, :], mv[:, :, 1], ACT.Sqrt, bias=keep.cols[:, 4:5]).then_inc(std_full, 1)

            tiles_in_two_stages(act, pre, post)

        @block.vector
        def _(dve):
            link = Links(dve, dve_d)
            dve.sem_inc(mix_done, 1)
            dve.sem_inc(sf_next, 1)
            dve.wait_ge(s_in, 48)
            dve.wait_ge(decays_full, 1)
            heads = decays[:].rearrange("p (d h) c -> p d h c", d=2)
            for d in range(2):
                last = nc.vector.tensor_mul(heads[:, d], heads[:, d], chunk[:, C_MASKF + d:C_MASKF + d + 1].to_broadcast([P, HEADS, P]))
            link(last)
            link(nc.vector.tensor_add(decay_T[:], heads[:, 0], heads[:, 1]))
            for n in range(TILES - 2):
                t = TILES - 1 - n
                dve.wait_ge(sb_upd, n + 1)
                wait_count(dve, sb_next, n)
                for h in range(HEADS):
                    v = slice(h * P, (h + 1) * P)
                    last = nc.vector.scalar_tensor_tensor(out=s_b[:, t - 1, v], in0=s_b[:, t, v], scalar=keep.cdec[:, 4 + h:5 + h],
                                                          in1=bank_s[:, h, :], op0=ALU.mult, op1=ALU.add)
                last.then_inc(sb_next, 1)

            def pre(t, s):
                dve.wait_ge(z_in[s], use_of(t, s) * 16 + 16)
                wait_count(dve, st_full, t - 1)
                nc.vector.tensor_mul(kf[s][:], zt[s][:, 1], keep.dec[:, 2, :].unsqueeze(2).to_broadcast([P, HEADS, P])).then_inc(kf_full, 1)
                dve.wait_ge(t1_full, t + 1)
                wait_count(dve, a_full, t)
                nc.vector.tensor_copy(kT[:], bank_k[:]).then_inc(kT_full, 1)
                dve.wait_ge(t2_full, t + 1)
                wait_count(dve, o_full, t - 1)
                nc.vector.tensor_copy(qbT[s][:], bank_qb[:]).then_inc(qbT_full, 1)
                dve.wait_ge(a_full, t + 1)
                nc.vector.tensor_mul(aT[s][:], bank_a[:], decay_T[:]).then_inc(aT_full, 1)

            def post(t, s):
                link.at(t * LINKS + 2)
                dve.wait_ge(o_full, t + 1)
                for h in range(HEADS):
                    last = nc.vector.bn_stats(stats[:, h, :], bank_o[s][:, h, :])
                link(last)
                dve.sem_inc(waited, 1)
                for h in range(HEADS):
                    last = nc.vector.bn_aggr(mv[:, h, :], stats[:, h, :])
                last.then_inc(var_full, 1)
                dve.wait_ge(st_full, t + 1)
                if isinstance(t, int) and t == 0:
                    nc.vector.tensor_copy(s_fin[:, 0, :].rearrange("p (h v) -> p h v", h=HEADS), bank_s[:]).then_inc(fin_full, 1)
                    dve.wait_ge(sb_upd, TILES - 1)
                    nc.vector.tensor_copy(s_fin[:, 1, :].rearrange("p (h v) -> p h v", h=HEADS), bank_s[:]).then_inc(fin_full, 1)
                else:
                    for h in range(HEADS):
                        v = slice(h * P, (h + 1) * P)
                        last = nc.vector.scalar_tensor_tensor(out=s_f[:, v], in0=s_f[:, v], scalar=keep.cdec[:, h:h + 1],
                                                              in1=bank_s[:, h, :], op0=ALU.mult, op1=ALU.add)
                    last.then_inc(sf_next, 1)
                    dve.wait_ge(sf_next, t + 1)
                dve.wait_ge(std_full, t + 1)
                link(nc.vector.reciprocal(rs[:, 1, :], rs[:, 0, :]))
                for h in range(HEADS):
                    last = nc.vector.tensor_scalar(on[:, h, :], bank_o[s][:, h, :], mv[:, h, 0:1], rs[:, 1, h:h + 1], ALU.subtract, ALU.mult)
                link(last)
                dve.wait_ge(sg_full, t * 2 + 2)
                nc.vector.tensor_mul(keep.mix[:, t, HV:2 * HV], on[:].rearrange("p h c -> p (h c)"), sg[s][:]).then_inc(mix_done, 1)
                dve.wait_ge(mix_done, t + 2)
                assert link.n == LINKS

            tiles_in_two_stages(dve, pre, post)


def stage_scores(nc, sem, m, keep, a):
    G = 2 * PEER_HEADS
    w_out = keep.w_out
    wc = m.sb("wc", [P, KD, G, P])
    mx = m.sb("mx", [P, D])
    mT = m.sb("mT", [P, KD, P])
    x1 = m.sb("x1", [P, D])
    xn = m.sb("xn2", [P, D])
    hs = m.sb("hs", [P, KD, P])
    st = m.sb("st2", [P, 3])
    sc = m.sb("sc", [P, G, P])
    sc2 = m.sb("sc2", [P, G, P])
    top = m.sb("top", [P, G, TOPK])
    idx = m.sb("idx", [P, G, TOPK], U32)
    idxf = m.sb("idxf", [P, G, TOPK], BF16)
    best = m.sb("best", [P, PEER_HEADS, TOPK])
    selab = m.sb("sel_ab", [P, 2, PEER_HEADS, TOPK], U32)
    sel, column = selab[:, 0], selab[:, 1]
    mask = m.sb("column_mask", [P, PEER_HEADS, TOPK], U32)
    step1 = m.sb("step1", [P, PEER_HEADS, TOPK], BF16)
    starts = m.sb("starts", [P, TOPK], BF16)
    selabf = m.sb("sel_abf", [P, 2, PEER_HEADS, TOPK], BF16)
    iota16 = m.sb("iota16", [P, TOPK], BF16)
    pairs = m.sb("pairs", [P, 3, PEER_HEADS, TOPK])
    sums = m.sb("sums", [P, 2, PEER_HEADS])
    pT = m.ps("pT2", [P, KD, P])
    po = m.ps("po", [P, 2, 512])
    psc = m.ps("psc", [P, G, P])
    wp = [sc[:].rearrange("p g k -> p (g k)")[:, 0:D], sc[:].rearrange("p g k -> p (g k)")[:, D:2 * D]]
    skT = sc2[:, 0:2, :]
    WIDE = 4
    SUMS = WIDE * TOPK + (TOPK - WIDE) * WIDE
    cand, cand2 = (x[:].rearrange("p g k -> p (g k)")[:, 0:PEER_HEADS * SUMS].rearrange("p (h c) -> p h c", h=PEER_HEADS)
                   for x in (sc, sc2))
    hot = tuple(sc2[:].rearrange("p g k -> p (g k)").bitcast(BF16)[:, n * 2 * D:(n + 1) * 2 * D].rearrange(
        "p (h k c) -> p h k c", h=PEER_HEADS, k=TOPK) for n in range(2))

    sk_in, wp_in = sem("sk_in"), [sem("wp_in0"), sem("wp_in1")]
    wc_full, wc_read_a, wc_read_d = sem("wc_full"), sem("wc_read_a"), sem("wc_read_d")
    mx_full, mt_full, mT_full, po_full, x_in, x1_full, x1_out, ss, rms, rec, xn_full = (
        sem(x) for x in ("mx_full", "mt_full", "mT_full", "po_full", "xt2_in", "x1_full", "x1_out", "ss2", "rms2", "rec2", "xn2_full"))
    ht_full, hs_full, h2_out, psc_full, sc_full, dve_t, e_in, e_out, pairs_full, pt_full, pairs_read, gated, idxf_full, step_full, hot_full, picked = (
        sem(x) for x in ("ht_full", "hs_full", "h2_out", "psc_full", "sc_full", "topk_dve", "e_in", "e_out",
                         "pairs_full", "pairsT_full", "pairs_read", "gated", "idxf_full", "step_full", "hot_full", "picked"))
    waited = sem("sort_waited")
    LINKS = 17
    xv = a["x"].rearrange("(t p) d -> t p d", p=P)
    wpv = a["w_pqT"].rearrange("(g p) d -> g p d", p=P)

    with nc.Block() as block:

        @block.sync
        def _(sp):
            sp.dma_start(x1[:], xv[0]).then_inc(x_in, 16)
            sp.dma_start(skT, a["keysT"]).then_inc(sk_in, 16)
            for g in range(G):
                wait_count(sp, wc_full, 2 * g - 2)
                sp.dma_start(wp[g % 2], wpv[g]).then_inc(wp_in[g % 2], 16)

            def tile(t):
                if not (isinstance(t, int) and t == 0):
                    sp.wait_ge(x1_out, t * 16)
                    sp.wait_ge(xn_full, t)
                    sp.sem_inc(waited, 1)
                    sp.dma_start(x1[:], xv[t]).then_inc(x_in, 16)
                sp.wait_ge(x1_full, t + 1)
                sp.dma_start(keep.x1_dram[t], x1[:]).then_inc(x1_out, 16)
                sp.wait_ge(hs_full, t + 1)
                sp.dma_start(keep.h2_dram[:, :, bass.ds(t * P, P)], hs[:]).then_inc(h2_out, 16)

            tile(0)
            with sp.Fori(1, TILES) as t:
                tile(t)
            sp.wait_ge(x1_out, 16 * TILES)
            sp.wait_ge(h2_out, 16 * TILES)

        def in_turns(eng, columns, scores, before, sort):
            before()

            def turn(t, projects=True, transposes=True, sorts=True):
                columns(t, projects, transposes)
                scores(t)
                if sorts:
                    sort(t - 1)

            turn(0, sorts=False)
            with eng.Fori(1, TILES - 2) as t:
                turn(t)
            turn(TILES - 2, transposes=False)
            turn(TILES - 1, projects=False, transposes=False)
            sort(TILES - 1)

        @block.gpsimd
        def _(pool):
            pool.sem_inc(picked, 2)
            nc.gpsimd.tensor_copy(iota16[:], keep.grid[:, C_IOTA, 0:TOPK])
            nc.gpsimd.tensor_copy(starts[:], keep.cols[:, 6:6 + TOPK]).then_inc(e_in, 1)

            def mix_rows(t):
                wait_count(pool, mt_full, t)
                nc.gpsimd.tensor_copy(mx[:], keep.mix[:, t, :]).then_inc(mx_full, 1)

            def residual(t):
                pool.wait_ge(x_in, (t + 1) * 16)
                pool.wait_ge(gated, t + 1)
                nc.gpsimd.tensor_add(x1[:], x1[:], xn[:]).then_inc(x1_full, 1)

            def pick(t):
                pool.wait_ge(idxf_full, t + 1)
                pool.wait_ge(picked, t * 2 + 2)
                i4 = idxf[:].rearrange("p (h s) k -> p h s k", s=2)
                nc.gpsimd.tensor_sub(step1[:, :, 1:TOPK], i4[:, :, 0, 1:TOPK], i4[:, :, 0, 0:TOPK - 1])
                nc.gpsimd.tensor_copy(step1[:, :, 0:1], i4[:, :, 0, 0:1]).then_inc(step_full, 1)
                pool.wait_ge(step_full, t + 1)
                for s, index in enumerate((step1[:], i4[:, :, 1, :])):
                    pool.wait_ge(hot_full, t * 2 + s + 1)
                    nc.gpsimd.tensor_mul(hot[s], hot[s], index.unsqueeze(2).to_broadcast([P, PEER_HEADS, TOPK, TOPK])).then_inc(picked, 1)

            def columns(t, projects, transposes):
                if transposes:
                    mix_rows(t + 2)
                if projects:
                    residual(t + 1)

            def before():
                mix_rows(0)
                mix_rows(1)
                residual(0)

            in_turns(pool, columns, lambda t: None, before, pick)

        @block.tensor
        def _(pe):
            pe.sem_inc(pt_full, 1)

            def transpose_mix(t):
                pe.wait_ge(mx_full, t + 1)
                if isinstance(t, int) and t == 1:
                    pe.wait_ge(mT_full, 1)
                else:
                    wait_count(pe, hs_full, t - 1)
                for k in range(KD):
                    last = nc.tensor.transpose(pT[:, k, :], mx[:, k * P:(k + 1) * P], keep.ident)
                last.then_inc(mt_full, 1)

            def project(t):
                pe.wait_ge(mT_full, t + 1)
                wait_count(pe, gated, t)
                for half in range(2):
                    for k in range(KD):
                        last = nc.tensor.matmul(po[:, half, :], mT[:, k, :], w_out[:, k, half * 512:(half + 1) * 512], start=k == 0, stop=k == KD - 1)
                last.then_inc(po_full, 1)

            def transpose_h(t):
                pe.wait_ge(xn_full, t + 1)
                pe.wait_ge(mT_full, min(t + 2, TILES) if isinstance(t, int) else t + 2)
                wait_count(pe, pairs_read, t)
                for k in range(KD):
                    last = nc.tensor.transpose(pT[:, k, :], xn[:, k * P:(k + 1) * P], keep.ident)
                last.then_inc(ht_full, 1)

            def scores(t):
                pe.wait_ge(hs_full, t + 1)
                wait_count(pe, sc_full, t)
                for b in range(4):
                    for k in range(KD):
                        last = nc.tensor.matmul(psc[:, 4 * b:4 * b + 4, :], hs[:, k, :], wc[:, k, 4 * b:4 * b + 4, :], start=k == 0, stop=k == KD - 1)
                last.then_inc(psc_full, 1)

            def pairs_to_columns(t):
                pe.wait_ge(pairs_full, t + 1)
                pe.wait_ge(mT_full, min(t + 4, TILES) if isinstance(t, int) else t + 4)
                pe.wait_ge(pairs_read, t + 1)
                for n in range(3):
                    last = nc.tensor.transpose(pT[:, n, :], pairs[:, n].rearrange("p h k -> p (h k)"), keep.ident)
                last.then_inc(pt_full, 1)

            def before():
                pe.wait_ge(keep.w_out_in, 16)
                transpose_mix(0)
                project(0)
                transpose_mix(1)
                pe.wait_ge(sk_in, 16)
                n = 0
                for g in range(G):
                    pe.wait_ge(wp_in[g % 2], 16 * (g // 2 + 1))
                    for half in range(2):
                        bank = psc[:, 4 * (n % 4):4 * (n % 4) + 4, :]
                        wait_count(pe, wc_read_a if n % 2 == 0 else wc_read_d, n // 2 - 1)
                        for k in range(4):
                            at = (half * 4 + k) * P
                            last = nc.tensor.matmul(bank[:, k, :], wp[g % 2][:, at:at + P], skT[:, g % 2, :], start=True, stop=True)
                        last.then_inc(wc_full, 1)
                        n += 1
                pe.wait_ge(wc_read_a, G)
                pe.wait_ge(wc_read_d, G)

            def columns(t, projects, transposes):
                transpose_h(t)
                if projects:
                    project(t + 1)
                if transposes:
                    transpose_mix(t + 2)

            in_turns(pe, columns, scores, before, pairs_to_columns)

        @block.scalar
        def _(act):
            def mix_columns(t):
                act.wait_ge(mt_full, t + 1)
                wait_count(act, po_full, t)
                nc.scalar.activation(mT[:], pT[:], ACT.Copy).then_inc(mT_full, 1)

            def norm(t):
                act.wait_ge(x1_full, t + 1)
                nc.scalar.activation(xn[:], x1[:], ACT.Square, accum_out=st[:, 0:1]).then_inc(ss, 1)
                act.wait_ge(ss, t + 1)
                nc.scalar.activation(st[:, 1:2], st[:, 0:1], ACT.Sqrt, scale=1.0 / D, bias=keep.cols[:, 4:5]).then_inc(rms, 1)
                act.wait_ge(rec, t + 1)
                nc.scalar.activation(xn[:], x1[:], ACT.Copy, scale=st[:, 2:3]).then_inc(xn_full, 1)

            def modulated(t):
                act.wait_ge(ht_full, t + 1)
                wait_count(act, h2_out, t * 16)
                wait_count(act, psc_full, t)
                c = 0 if isinstance(t, int) and t == 0 else 1
                for k in range(KD):
                    last = nc.scalar.activation(hs[:, k, :], pT[:, k, :], ACT.Identity, scale=keep.mod[:, 2, c, k:k + 1], bias=keep.mod[:, 3, c, k:k + 1])
                last.then_inc(hs_full, 1)

            def keep_scores(t):
                act.wait_ge(psc_full, t + 1)
                wait_count(act, e_in, t + 1)
                nc.scalar.activation(sc[:], psc[:], ACT.Copy).then_inc(sc_full, 1)

            def exps(t):
                act.wait_ge(e_in, t + 2)
                nc.scalar.activation(pairs[:, 2], best[:], ACT.Exp).then_inc(e_out, 1)

            def before():
                mix_columns(0)
                mix_columns(1)
                norm(0)
                for n in range(0, 2 * G, 2):
                    act.wait_ge(wc_full, n + 1)
                    nc.scalar.activation(wc[:, (n % 2) * 4:(n % 2) * 4 + 4, n // 2, :], psc[:, 4 * (n % 4):4 * (n % 4) + 4, :], ACT.Copy).then_inc(wc_read_a, 1)

            def columns(t, projects, transposes):
                modulated(t)
                if transposes:
                    mix_columns(t + 2)
                if projects:
                    norm(t + 1)

            def scores(t):
                if not (isinstance(t, int) and t == 0):
                    exps(t - 1)
                keep_scores(t)

            in_turns(act, columns, scores, before, lambda t: None)
            exps(TILES - 1)

        @block.vector
        def _(dve):
            link = Links(dve, dve_t)
            dve.sem_inc(pairs_read, 1)

            def gated_rows(t):
                c = 0 if isinstance(t, int) and t == 0 else 1
                dve.wait_ge(po_full, t + 1)
                wait_count(dve, ht_full, t)
                nc.vector.tensor_mul(xn[:], po[:].rearrange("p b c -> p (b c)"), keep.gate[:, 0, c, :]).then_inc(gated, 1)

            def reciprocal_norm(t):
                dve.wait_ge(rms, t + 1)
                nc.vector.reciprocal(st[:, 2:3], st[:, 1:2]).then_inc(rec, 1)

            def first_sort(t):
                dve.wait_ge(sc_full, t + 1)
                dve.sem_inc(waited, 1)
                sixteen_best(sc, sc2, top, idx, G)
                dve.wait_ge(picked, t * 2 + 2)
                nc.vector.tensor_copy(idxf[:], idx[:]).then_inc(idxf_full, 1)

            def second_sort(t):
                t4 = top[:].rearrange("p (h s) k -> p h s k", s=2)
                for lo, hi, width, at in ((0, WIDE, TOPK, 0), (WIDE, TOPK, WIDE, WIDE * TOPK)):
                    out = cand[:, :, at:at + (hi - lo) * width].rearrange("p h (a b) -> p h a b", a=hi - lo)
                    shape = [P, PEER_HEADS, hi - lo, width]
                    last = nc.vector.tensor_tensor(out, t4[:, :, 0, lo:hi].unsqueeze(3).to_broadcast(shape),
                                                   t4[:, :, 1, 0:width].unsqueeze(2).to_broadcast(shape), ALU.add)
                link(last)
                dve.sem_inc(waited, 1)
                sixteen_best(cand, cand2, best, sel, PEER_HEADS)

            def weights(t):
                dve.wait_ge(pt_full, t + 1)
                link(nc.vector.tensor_copy(sums[:, 0, :], best[:, :, 0]))
                nc.vector.tensor_tensor(best[:], best[:], sums[:, 0, :].unsqueeze(2).to_broadcast([P, PEER_HEADS, TOPK]), ALU.subtract).then_inc(e_in, 1)
                link(nc.vector.tensor_scalar(mask[:], sel, 6, None, ALU.logical_shift_right))
                link(nc.vector.tensor_scalar(mask[:], mask[:], float(WIDE - TOPK), float(TOPK - 1), ALU.mult, ALU.add))
                link(nc.vector.tensor_tensor(column, sel, mask[:], ALU.bitwise_and))
                link(nc.vector.tensor_copy(selabf[:], selab[:]))
                shape = [P, PEER_HEADS, TOPK, TOPK]
                for s, (row, op) in enumerate(((starts, ALU.is_ge), (iota16, ALU.is_equal))):
                    nc.vector.tensor_tensor(hot[s], selabf[:, s].unsqueeze(3).to_broadcast(shape),
                                            row[:].unsqueeze(1).unsqueeze(1).to_broadcast(shape), op).then_inc(hot_full, 1)
                for s in range(2):
                    dve.wait_ge(picked, t * 2 + s + 3)
                    last = nc.vector.reduce_sum(pairs[:, s], hot[s], AX.X)
                link(last)
                dve.wait_ge(e_out, t + 1)
                link(nc.vector.reduce_sum(sums[:, 0, :], pairs[:, 2], AX.X))
                link(nc.vector.reciprocal(sums[:, 1, :], sums[:, 0, :]))
                nc.vector.tensor_tensor(pairs[:, 2], pairs[:, 2], sums[:, 1, :].unsqueeze(2).to_broadcast([P, PEER_HEADS, TOPK]), ALU.mult).then_inc(pairs_full, 1)
                dve.wait_ge(pt_full, t + 2)
                nc.vector.tensor_copy(keep.pairsT[:, :, bass.ds(t * P, P)], pT[:, 0:3, :]).then_inc(pairs_read, 1)

            def sixteen_best(x, rest, values, where, groups):
                for g in range(groups):
                    last = nc.vector.max(values[:, g, 0:8], x[:, g, :])
                link(last)
                dve.sem_inc(waited, 1)
                for g in range(groups):
                    nc.vector.max_index(where[:, g, 0:8], values[:, g, 0:8], x[:, g, :])
                for g in range(groups):
                    last = nc.vector.match_replace(rest[:, g, :], values[:, g, 0:8], x[:, g, :], NEG)
                link(last)
                dve.sem_inc(waited, 1)
                for g in range(groups):
                    last = nc.vector.max(values[:, g, 8:16], rest[:, g, :])
                link(last)
                dve.sem_inc(waited, 1)
                for g in range(groups):
                    last = nc.vector.max_index(where[:, g, 8:16], values[:, g, 8:16], rest[:, g, :])
                link(last)

            def sort(t, projects=True):
                link.at(t * LINKS)
                first_sort(t)
                if projects:
                    gated_rows(t + 2)
                second_sort(t)
                if projects:
                    reciprocal_norm(t + 2)
                weights(t)
                assert link.n == LINKS, link.n

            gated_rows(0)
            reciprocal_norm(0)
            for n in range(1, 2 * G, 2):
                dve.wait_ge(wc_full, n + 1)
                nc.vector.tensor_copy(wc[:, (n % 2) * 4:(n % 2) * 4 + 4, n // 2, :], psc[:, 4 * (n % 4):4 * (n % 4) + 4, :]).then_inc(wc_read_d, 1)
            gated_rows(1)
            reciprocal_norm(1)
            with dve.Fori(0, TILES - 2) as t:
                sort(t)
            sort(TILES - 2, False)
            sort(TILES - 1, False)


class WeightSteps:
    B = 4
    BLOCK = 32
    STEPS = GROUP * P // B
    PER_BLOCK = BLOCK // B

    def __init__(self, nc, sem, m, keep, banks, name, split):
        B = self.B
        dt = BF16 if split else F32
        parts = 3 if split else 1
        self.nc, self.keep, self.banks = nc, keep, banks
        self.hot_i = [m.sb(f"{name}_hot_i{i}", [P, B, P], dt) for i in range(2)]
        self.hot_j = [[m.sb(f"{name}_hot_j{i}{k}", [P, B, P], dt) for k in range(parts)] for i in range(2)]
        self.iota = m.sb(f"{name}_iota", [P, P], dt)
        if split:
            self.part_bf = m.sb(f"{name}_part_bf", [P, GROUP * P], BF16)
            self.rest = m.sb(f"{name}_w_rest", [P, GROUP * P])
            self.parts = m.sb(f"{name}_w_parts", [P, 3, GROUP * P])
        else:
            self.parts = keep.pairsT[:, 2:3, 0:GROUP * P]
        self.wt = m.sb(f"{name}_wt", [P, 2, N_KEYS, self.BLOCK])
        self.pw = [m.ps(f"{name}_pw{i}", [P, B, N_KEYS]) for i in range(banks)]
        self.iota_full, self.part_done, self.hot_full, self.pw_full, self.pw_read, self.wt_free, self.stored = (
            sem(f"{name}_{x}") for x in ("iota_full", "part_done", "hot_full", "pw_full", "pw_read", "wt_free", "w_stored"))

    def split(self, dve, g, made):
        nc, base = self.nc, made * 6
        w = self.keep.pairsT[:, 2, g * GROUP * P:(g + 1) * GROUP * P]

        def link(ins, n):
            ins.then_inc(self.part_done, 1)
            dve.wait_ge(self.part_done, base + n)

        for k in range(3):
            src = w if k == 0 else self.rest[:]
            link(nc.vector.tensor_copy(self.part_bf[:], src), 2 * k + 1)
            ins = nc.vector.tensor_copy(self.parts[:, k, :], self.part_bf[:])
            if k < 2:
                ins = nc.vector.tensor_sub(self.rest[:], src, self.part_bf[:])
            link(ins, 2 * k + 2)

    def vector(self, dve, g, n, c, s):
        nc = self.nc
        dve.wait_ge(self.pw_full, n + 1)
        for b in range(self.B):
            i, j = (self.keep.pairsT[:, r, bass.ds(c * self.B + (g * GROUP * P + b), 1)] for r in range(2))
            nc.vector.tensor_scalar(self.hot_i[s][:, b, :], self.iota[:], i, None, ALU.is_equal)
            for k in range(len(self.hot_j[s])):
                last = nc.vector.tensor_scalar(self.hot_j[s][k][:, b, :], self.iota[:], j, self.parts[:, k, bass.ds(c * self.B + b, 1)],
                                               ALU.is_equal, ALU.mult)
        last.then_inc(self.hot_full, 1)

    def tensor(self, pe, n, s):
        pe.wait_ge(self.hot_full, n + 1)
        pe.wait_ge(self.pw_read, n + 1)
        for b in range(self.B):
            for k in range(len(self.hot_j[s])):
                last = self.nc.tensor.matmul(self.pw[s % self.banks][:, b, :], self.hot_i[s][:, b, :], self.hot_j[s][k][:, b, :],
                                             start=k == 0, stop=k == len(self.hot_j[s]) - 1)
        last.then_inc(self.pw_full, 1)

    def scalar(self, act, n, s):
        act.wait_ge(self.wt_free, n // self.PER_BLOCK + 1)
        act.wait_ge(self.pw_full, n + 3)
        out = self.wt[:, (n // self.PER_BLOCK) % 2, :, bass.ds((n % self.PER_BLOCK) * self.B, self.B)]
        self.nc.scalar.activation(out.rearrange("p j b -> p b j"), self.pw[s % self.banks][:], ACT.Copy).then_inc(self.pw_read, 1)

    def store(self, eng, block, at):
        wait_count(eng, self.stored, block * 16)
        eng.sem_inc(self.wt_free, 1)
        eng.wait_ge(self.pw_read, block * self.PER_BLOCK + (self.PER_BLOCK + self.banks))
        eng.dma_start(self.keep.w_dram[at], self.wt[:, block % 2]).then_inc(self.stored, 16)


def stage_weights(nc, sem, m, keep, a):
    w = WeightSteps(nc, sem, m, keep, 2, "first", False)
    BLOCKS = w.STEPS // w.PER_BLOCK

    def steps(eng, body):
        body(0, 0)
        body(1, 1)
        with eng.Fori(1, w.STEPS // 2) as k:
            for s in range(2):
                body(k * 2 + s, s)

    with nc.Block() as block:

        @block.vector
        def _(dve):
            nc.vector.tensor_copy(w.iota[:], keep.grid[:, C_IOTA, :]).then_inc(w.iota_full, 1)
            dve.wait_ge(w.iota_full, 1)
            steps(dve, lambda n, s: w.vector(dve, 0, n, n, s))

        @block.tensor
        def _(pe):
            pe.sem_inc(w.pw_full, 2)
            steps(pe, lambda n, s: w.tensor(pe, n, s))

        @block.scalar
        def _(act):
            act.sem_inc(w.wt_free, 1)
            act.sem_inc(w.pw_read, w.banks)
            steps(act, lambda n, s: w.scalar(act, n, s))

        @block.sync
        def _(sp):
            w.store(sp, 0, 0)
            with sp.Fori(1, BLOCKS) as b:
                w.store(sp, b, b)
            sp.wait_ge(w.stored, 16 * BLOCKS)


def stage_experts(nc, sem, m, keep, a):
    GT = GROUP * P
    GROUPS = T // GT
    J = N_KEYS
    h_hi, h_lo = m.sb("h_hi", [P, KD, GT], F32R), m.sb("h_lo", [P, KD, GT], F32R)
    two = lambda name, shape, dt=F32: [m.sb(f"{name}{i}", shape, dt) for i in range(2)]
    u_raw, u_hi, u_lo = two("u_raw", [P, KD, P]), two("u_hi", [P, KD, P], F32R), two("u_lo", [P, KD, P], F32R)
    v_raw, v_hi, v_lo = two("v_raw", [P, D]), two("v_hi", [P, D], F32R), two("v_lo", [P, D], F32R)
    act_g, g_all, g_hi, g_lo = two("act_g", [P, GT]), two("g_all", [P, GT]), two("g_hi", [P, GT], F32R), two("g_lo", [P, GT], F32R)
    x1 = [m.sb(f"x1g{i}", [P, D]) for i in range(GROUP)]
    y = m.sb("y", [P, D])
    w = WeightSteps(nc, sem, m, keep, 1, "next", True)
    JC = 8
    TB = GT // w.BLOCK
    w_ring = m.sb("w_ring", [P, 2, TB, JC, w.BLOCK])
    p_a = m.ps("p_a", [P, 512])
    p_y = [m.ps(f"p_y{i}", [P, 2, 512]) for i in range(GROUP)]

    pair = lambda name: [sem(name + "0"), sem(name + "1")]
    h_in, u_in, v_in, w_in = sem("h_in"), pair("u_in"), pair("v_in"), sem("w_load")
    x1_in, y_out = [sem(f"x1_in{i}") for i in range(GROUP)], [sem(f"y_out{i}") for i in range(GROUP)]
    h_hi_full, h_lo_full, uhi_full, ulo_full, vhi_full, vlo_full, a_full, gelu_full, g_full, ghi_full, glo_full, y_step, y_mul, y_full = (
        sem(x) for x in ("h_hi_full", "h_lo_full", "uhi_full", "ulo_full", "vhi_full", "vlo_full", "a_full", "gelu_full",
                         "g_full", "ghi_full", "glo_full", "y_step", "y_mul", "y_full"))

    def blocks(eng, g, pre, post, between=lambda: None, weights=lambda n, c, s: None, late=None):
        both = lambda n, j, s: (pre(n, j, s), late(n, j, s) if late else None)
        o = g * J
        both(o, 0, 0)
        both(o + 1, 1, 1)
        post(o, 0, 0)
        between()

        def turn(k, c0=None):
            for s in range(2):
                j = k * 2 + s
                pre(j + (o + 2), j + 2, s)
                if c0 is not None and not late:
                    weights(j + c0, j, s)
                post(j + (o + 1), j + 1, 1 - s)
                if c0 is not None and late:
                    weights(j + c0, j, s)
                if late:
                    late(j + (o + 2), j + 2, s)

        done = 0
        if g < GROUPS - 1:
            done = w.STEPS
            with eng.Fori(0, done // 2) as k:
                turn(k, g * w.STEPS)
        with eng.Fori(done // 2, J // 2 - 1) as k:
            turn(k)
        post(o + J - 1, J - 1, 1)

    def used(n, s):
        return n // 2 if isinstance(n, int) else (n - s) // 2

    with nc.Block() as block:

        @block.sync
        def _(sp):
            def load(n, j, s):
                wait_count(sp, ulo_full, n - 1)
                sp.dma_start(u_raw[s][:], a["uT"][j]).then_inc(u_in[s], 16)
                wait_count(sp, vlo_full, n - 1)
                sp.dma_start(v_raw[s][:], a["v"][j]).then_inc(v_in[s], 16)

            def store_y(g):
                for i in range(GROUP):
                    t = g * GROUP + i
                    sp.wait_ge(y_full, t + 1)
                    dst = a["out"][0][0] if t == 0 else a["out"][1][0, (t - 1) * P:t * P, :]
                    sp.dma_start(dst, x1[i][:]).then_inc(y_out[i], 16)

            for g in range(GROUPS):
                def between():
                    if g:
                        store_y(g - 1)
                    for i in range(GROUP):
                        wait_count(sp, y_out[i], 16 * g)
                        sp.dma_start(x1[i][:], keep.x1_dram[g * GROUP + i]).then_inc(x1_in[i], 16)

                blocks(sp, g, load, lambda n, j, s: None, between)
            store_y(GROUPS - 1)
            for i in range(GROUP):
                sp.wait_ge(y_out[i], 16 * GROUPS)

        @block.scalar
        def _(act):
            act.sem_inc(w.wt_free, 1)
            act.sem_inc(w.pw_read, w.banks)

            def split(n, j, s):
                act.wait_ge(u_in[s], used(n, s) * 16 + 16)
                wait_count(act, a_full, n - 1)
                nc.scalar.activation(u_hi[s][:], u_raw[s][:], ACT.Copy).then_inc(uhi_full, 1)

            def split_v(n, j, s):
                act.wait_ge(v_in[s], used(n, s) * 16 + 16)
                wait_count(act, y_step, n)
                nc.scalar.activation(v_hi[s][:], v_raw[s][:], ACT.Copy).then_inc(vhi_full, 1)

            def gelu(n, j, s):
                act.wait_ge(a_full, n + 1)
                wait_count(act, g_full, n)
                nc.scalar.activation(act_g[s][:], p_a[:, 0:GT], ACT.Gelu).then_inc(gelu_full, 1)

            for g in range(GROUPS):
                blocks(act, g, split, gelu, weights=lambda n, c, s: w.scalar(act, n, s), late=split_v)

        @block.gpsimd
        def _(pool):
            CHUNKS = J // JC

            def load_w(g, c):
                n = c + g * CHUNKS
                wait_count(pool, w_in, n * 16)
                wait_count(pool, g_full, (n - 1) * JC + 1)
                pool.dma_start(w_ring[:, n % 2], keep.w_dram[g * TB:(g + 1) * TB, :, bass.ds(c * JC, JC), :].rearrange("b i j t -> i b j t")).then_inc(w_in, 16)

            def split(n, j, s):
                pool.wait_ge(vhi_full, n + 1)
                wait_count(pool, y_step, n)
                nc.gpsimd.tensor_sub(v_lo[s][:], v_raw[s][:], v_hi[s][:].bitcast(F32)).then_inc(vlo_full, 1)

            for g in range(GROUPS):
                if g:
                    pool.wait_ge(a_full, g * J)
                    pool.wait_ge(w.stored, 16 * g * TB)
                pool.dma_start(h_lo[:].bitcast(F32), keep.h2_dram[:, :, g * GT:(g + 1) * GT]).then_inc(h_in, 16)
                load_w(g, 0)
                load_w(g, 1)
                o = g * J
                split(o, 0, 0)
                split(o + 1, 1, 1)

                def eight(k, stores):
                    for s in range(JC):
                        split(k * JC + (o + 2 + s), None, s % 2)
                    if stores:
                        w.store(pool, k + g * TB, k + (g + 1) * TB)
                    load_w(g, k + 2)

                full = TB if g < GROUPS - 1 else 0
                if full:
                    eight(0, True)
                    with pool.Fori(1, TB) as k:
                        eight(k, True)
                with pool.Fori(full, CHUNKS - 2) as k:
                    eight(k, False)
                for j in range(J - 2 * JC + 2, J):
                    split(o + j, None, j % 2)

        @block.vector
        def _(dve):
            dve.sem_inc(g_full, 1)
            nc.vector.tensor_copy(w.iota[:], keep.grid[:, C_IOTA, :]).then_inc(w.iota_full, 1)
            dve.wait_ge(w.iota_full, 1)

            def split(n, j, s):
                dve.wait_ge(uhi_full, n + 1)
                nc.vector.tensor_sub(u_lo[s][:], u_raw[s][:], u_hi[s][:].bitcast(F32)).then_inc(ulo_full, 1)

            def weigh(n, j, s):
                dve.wait_ge(gelu_full, n + 1)
                dve.wait_ge(w_in, (n // JC) * 16 + 16)
                three = lambda x: x[:].rearrange("p (b t) -> p b t", t=w.BLOCK)
                nc.vector.tensor_mul(three(g_all[s]), three(act_g[s]), w_ring[:, (n // JC) % 2, :, n % JC, :]).then_inc(g_full, 1)
                dve.wait_ge(g_full, n + 2)
                wait_count(dve, y_step, n)
                nc.vector.tensor_copy(g_hi[s][:], g_all[s][:]).then_inc(ghi_full, 1)
                dve.wait_ge(ghi_full, n + 1)
                nc.vector.tensor_sub(g_lo[s][:], g_all[s][:], g_hi[s][:].bitcast(F32)).then_inc(glo_full, 1)

            for g in range(GROUPS):
                dve.wait_ge(h_in, 16 * (g + 1))
                nc.vector.tensor_copy(h_hi[:], h_lo[:].bitcast(F32)).then_inc(h_hi_full, 1)
                dve.wait_ge(h_hi_full, g + 1)
                nc.vector.tensor_sub(h_lo[:], h_lo[:].bitcast(F32), h_hi[:].bitcast(F32)).then_inc(h_lo_full, 1)
                if g < GROUPS - 1:
                    dve.wait_ge(w.pw_full, g * w.STEPS + 2)
                    w.split(dve, g + 1, g)
                blocks(dve, g, split, weigh, weights=lambda n, c, s: w.vector(dve, g + 1, n, c, s))
                dve.wait_ge(y_step, (g + 1) * J + 1)
                for i in range(GROUP):
                    t = g * GROUP + i
                    c = 0 if t == 0 else 1
                    wait_count(dve, y_full, t)
                    nc.vector.tensor_mul(y[:], p_y[i][:].rearrange("p b c -> p (b c)"), keep.gate[:, 1, c, :]).then_inc(y_mul, 1)
                    dve.wait_ge(y_mul, t + 1)
                    dve.wait_ge(x1_in[i], 16 * (g + 1))
                    nc.vector.tensor_add(x1[i][:], x1[i][:], y[:]).then_inc(y_full, 1)

        @block.tensor
        def _(pe):
            pe.sem_inc(w.pw_full, 2)
            pe.sem_inc(y_step, 1)
            for g in range(GROUPS):
                def down(n, j, s):
                    pe.wait_ge(uhi_full, n + 1)
                    wait_count(pe, gelu_full, n)
                    for k in range(KD):
                        nc.tensor.matmul(p_a[:, 0:GT], u_hi[s][:, k, :], h_hi[:, k, :], start=k == 0, stop=False)
                        nc.tensor.matmul(p_a[:, 0:GT], u_hi[s][:, k, :], h_lo[:, k, :], start=False, stop=False)
                    pe.wait_ge(ulo_full, n + 1)
                    for k in range(KD):
                        last = nc.tensor.matmul(p_a[:, 0:GT], u_lo[s][:, k, :], h_hi[:, k, :], start=False, stop=k == KD - 1)
                    last.then_inc(a_full, 1)

                def up(n, j, s):
                    pe.wait_ge(ghi_full, n + 1)
                    pe.wait_ge(vlo_full, n + 1)
                    first, end = (isinstance(j, int) and j == x for x in (0, J - 1))
                    if first:
                        wait_count(pe, y_mul, g * GROUP)
                    for hi in (True, False):
                        if not hi:
                            pe.wait_ge(glo_full, n + 1)
                        for i in range(GROUP):
                            part = (g_hi if hi else g_lo)[s][:, i * P:(i + 1) * P]
                            for vv in (v_hi[s], v_lo[s]) if hi else (v_hi[s],):
                                for half in range(2):
                                    last = nc.tensor.matmul(p_y[i][:, half, :], part, vv[:, half * 512:(half + 1) * 512],
                                                            start=first and hi and vv is v_hi[s], stop=end and not hi)
                    last.then_inc(y_step, 1)

                pe.wait_ge(h_lo_full, g + 1)
                blocks(pe, g, down, up, weights=lambda n, c, s: w.tensor(pe, n, s))



class Keep:
    pass


def build(nc, a, debug=None):
    with ExitStack() as stack:
        top = Mem(nc, stack)
        keep = Keep()

        def run(stage):
            taken = []

            def sem(name):
                taken.append(nc.alloc_semaphore(name=name))
                return taken[-1]

            with ExitStack() as inner:
                stage(nc, sem, Mem(nc, inner), keep, a)
            nc.clear_and_free_semaphores(taken)
            nc.all_engine_barrier()

        keep.grid = top.sb("grid", [P, 2, P])
        keep.ident = keep.grid[:, C_IDENT, :]
        keep.cols = top.sb("cols", [P, 6 + TOPK])
        keep.mod = top.sb("mod", [P, 4, 2, KD])
        keep.gate = top.sb("gate", [P, 2, 2, D])
        keep.dec = top.sb("dec", [P, 4, HEADS])
        keep.cdec = top.sb("cdec", [P, 8])
        keep.log_decay = top.sb("log_decay", [P, 8])
        keep.pairsT = top.sb("pairsT", [P, 3, T])
        keep.z_dram = nc.dram_tensor("z_spill", [TILES, P, Z_RET], F32).ap()
        keep.x1_dram = nc.dram_tensor("x1_spill", [TILES, P, D], F32).ap()
        keep.h2_dram = nc.dram_tensor("h2_spill", [P, KD, T], F32).ap()
        keep.w_dram = nc.dram_tensor("weights_spill", [T // WeightSteps.BLOCK, P, N_KEYS, WeightSteps.BLOCK], F32).ap()
        keep.w_in_in = [stack.enter_context(nc.semaphore(f"w_in_in{c}")) for c in range(2)]

        keep.w_out_in = stack.enter_context(nc.semaphore("w_out_in"))

        with ExitStack() as s1:
            m1 = Mem(nc, s1)
            keep.mix = m1.sb("mix", [P, TILES, D])
            keep.z1 = keep.mix[:].rearrange("p t c -> p (t c)")[:, 0:(TILES + 1) * Z_ATT].rearrange("p (t c) -> p t c", c=Z_ATT)
            with ExitStack() as s2:
                m2 = Mem(nc, s2)
                keep.w_hi, keep.w_lo = ([m2.sb(f"w_{x}{i}", [P, KD, CHUNK], F32R) for i in range(2)] for x in ("hi", "lo"))
                keep.w_raw = [m2.sb(f"w_raw{i}", [P, KD // 4, CHUNK]) for i in range(2)]
                run(stage_modulation)
                run(stage_project)
            if debug and debug(nc, stack, keep, "z1"):
                return
            with ExitStack() as s2:
                m2 = Mem(nc, s2)
                keep.qTn = m2.sb("qTn", [P, HEADS, T])
                keep.qTr = m2.sb("qTr", [P, 2, T])
                keep.kTn = m2.sb("kTn", [P, HEADS, T + P])
                keep.kTr = m2.sb("kTr", [P, 2, T + P])
                keep.v_sb = m2.sb("v_sb", [P, TILES + 1, HEADS * P])
                run(stage_qkv)
                if debug and debug(nc, stack, keep, "qkv"):
                    return
                run(stage_attention)
            keep.w_out = m1.sb("w_out", [P, KD, D])
            run(stage_retention)
            if debug and debug(nc, stack, keep, "mix"):
                return
            run(stage_scores)
            if debug and debug(nc, stack, keep, "topk"):
                return
        run(stage_weights)
        if debug and debug(nc, stack, keep, "w"):
            return
        run(stage_experts)


_OUTS = [(1, 128, 1024), (1, 1024, 1024), (1, 1, 128, 256), (1, 1, 128, 64), (1, 1, 2, 4, 128, 128)]


def lay_out(x):
    g = {k: np.asarray(v) for k, v in x.items()}
    blocks = lambda v: np.ascontiguousarray(v.reshape(-1, P).T)
    sel = np.zeros((2, 2, P), np.float32)
    sel[0, 0] = sel[1, 1] = 1.0
    return {
        "x": np.concatenate([g["x_prompt"][0], g["x_sample"][0]]),
        "cT": np.ascontiguousarray(np.stack([g["c_ctx"], g["c"][0]]).reshape(2, KD, P).transpose(2, 1, 0)),
        "cache_ckv": g["cache_ckv"][0, 0], "cache_krope": g["cache_krope"][0, 0],
        "state": np.ascontiguousarray(g["state_ret"][0, 0].transpose(2, 0, 1, 3)),
        "w_ada": g["w_ada"][0], "b_ada": g["b_ada"][0],
        "norm_cols": np.ascontiguousarray(np.stack([blocks(g["norm1_w"][0]), blocks(g["norm2_w"][0])], 1)),
        "w_in": g["w_in"][0], "q_norm_cols": blocks(g["q_norm_w"][0]), "kv_norm": g["kv_norm_w"][0],
        "w_uq": g["w_uq"][0], "w_ukv": g["w_ukv"][0],
        "q_head_norm": g["q_head_norm_w"][0], "k_head_norm": g["k_head_norm_w"][0],
        "decay_logit": g["ret_decay_logit"][0].reshape(-1), "gn": g["ret_gn_w"][0], "w_out": g["w_out"][0],
        "w_pqT": np.ascontiguousarray(g["w_pq"][0].T),
        "keysT": np.ascontiguousarray(np.stack([g["sub_keys1"][0].T, g["sub_keys2"][0].T], 1)),
        "uT": np.ascontiguousarray(g["u_table"][0].reshape(N_KEYS, N_KEYS, KD, P).transpose(1, 3, 2, 0)),
        "v": np.ascontiguousarray(g["v_table"][0].reshape(N_KEYS, N_KEYS, D).transpose(1, 0, 2)),
        "sel": sel, "grid": grid_constants()[0], "chunk": grid_constants()[1], "cols": column_constants(), "rope": rope_constants(),
    }


def kernel(**inputs):
    import concourse.bacc as _bacc
    from concourse.bass_utils import run_bass_kernel_spmd as _run

    nc = _bacc.Bacc("TRN2", target_bir_lowering=False, num_devices=1)
    arrays = lay_out(inputs)
    a = {k: nc.dram_tensor(f"in_{k}", v.shape, F32, kind="ExternalInput").ap() for k, v in arrays.items()}
    a["out"] = [nc.dram_tensor(f"out_{i}", s, F32, kind="ExternalOutput").ap() for i, s in enumerate(_OUTS)]
    build(nc, a)
    r = _run(nc, [{f"in_{k}": v for k, v in arrays.items()}], core_ids=[0])
    return tuple(r.results[0][f"out_{i}"] for i in range(len(_OUTS)))
```
